# Optimizing a Trainium2 kernel written in Bass

```python
import jax, jax.numpy as jnp
from jax import lax
import numpy as np

D_MODEL = 1024
BATCH = 1
SEQ = 512
DEPTH = 2

CHUNK = 64
N_MIXERS = 2
N_RWKV = (DEPTH + 1) // 2
N_MLSTM = DEPTH // 2
EPS = 1e-6
NEG = -1e30

RW_HEAD = 64
RW_HEADS = D_MODEL // RW_HEAD
LORA_W = 64
LORA_A = 64
LORA_G = 160
RW_SEGS = (D_MODEL, LORA_W, D_MODEL, D_MODEL, LORA_A, LORA_G)
RW_IN = sum(RW_SEGS)
GN_EPS = 64e-5

ML_HEADS = 8
ML_QK = D_MODEL // 2 // ML_HEADS
ML_V = D_MODEL // ML_HEADS
ML_QKW = 2 * ML_HEADS * ML_QK
ML_VW = ML_HEADS * ML_V
ML_IN = ML_QKW + 2 * ML_VW + 2 * ML_HEADS
CONV_W = 4
GATE_CAP = 15.0

D_FF = -(-(8 * D_MODEL) // (3 * 256)) * 256


def _rms(x):
    xf = x.astype(jnp.float32)
    return (xf * lax.rsqrt(jnp.mean(xf * xf, -1, keepdims=True) + EPS)).astype(x.dtype)

def _softcap(t):
    return GATE_CAP * jnp.tanh(t / GATE_CAP)

def _token_shift(x):
    return jnp.pad(x[:, :-1], ((0, 0), (1, 0), (0, 0)))

def _rwkv7_step(state, inp):
    r_t, w_t, k_t, v_t, a_t, b_t = inp
    sa = jnp.einsum('bhvk,bhk->bhv', state, a_t)
    state = state * w_t[:, :, None, :] + sa[..., None] * b_t[:, :, None, :] + v_t[..., None] * k_t[:, :, None, :]
    y = jnp.einsum('bhvk,bhk->bhv', state, r_t)
    return state, y

def _rwkv7_mix(x, mix, w_in, w0, w2, a0, a2, g2, k_k, k_a, r_k, gn_w, gn_b, w_out):
    B, S, D = x.shape
    xx = _token_shift(x) - x
    xs = x[None] + xx[None] * mix[:, None, None, :]
    outs = []
    off = 0
    for i, n in enumerate(RW_SEGS):
        outs.append(xs[i] @ w_in[:, off:off + n])
        off += n
    r, wl, k, v, al, gl = outs
    w_log = -jax.nn.softplus(-(w0 + jnp.tanh(wl) @ w2)) - 0.5
    decay = jnp.exp(-jnp.exp(w_log.astype(jnp.float32)))
    a = jax.nn.sigmoid(a0 + al @ a2)
    g = jax.nn.sigmoid(gl) @ g2
    hs = lambda t: t.reshape(B, S, RW_HEADS, RW_HEAD).astype(jnp.float32)
    kk = hs(k * k_k)
    kk = kk / jnp.maximum(jnp.linalg.norm(kk, axis=-1, keepdims=True), 1e-12)
    k = k * (1.0 + (a - 1.0) * k_a)
    rh, kh, vh, ah, wh = hs(r), hs(k), hs(v), hs(a), hs(decay)
    tm = lambda t: jnp.moveaxis(t, 1, 0)
    state0 = jnp.zeros((B, RW_HEADS, RW_HEAD, RW_HEAD), jnp.float32)
    _, y = lax.scan(_rwkv7_step, state0, (tm(rh), tm(wh), tm(kh), tm(vh), tm(-kk), tm(kk * ah)))
    y = jnp.moveaxis(y, 0, 1)
    mu = jnp.mean(y, -1, keepdims=True)
    var = jnp.mean(jnp.square(y - mu), -1, keepdims=True)
    y = ((y - mu) * lax.rsqrt(var + GN_EPS)).reshape(B, S, D) * gn_w + gn_b
    bonus = (jnp.sum(rh * kh * r_k, -1, keepdims=True) * vh).reshape(B, S, D)
    return ((y + bonus).astype(x.dtype) * g) @ w_out

def _causal_dwconv(x, w, b):
    y = lax.conv_general_dilated(x, w[:, None, :], window_strides=(1,), padding=[(CONV_W - 1, 0)],
                                 dimension_numbers=('NWC', 'WIO', 'NWC'), feature_group_count=x.shape[-1])
    return y + b

def _mlstm_chunk_step(carry, inp):
    C, n, m = carry
    g_c, m_l, C_l, n_l = inp
    m_new = jnp.maximum(g_c + m, m_l)
    sa = jnp.exp(g_c + m - m_new)
    sb = jnp.exp(m_l - m_new)
    C_new = sa[..., None, None] * C + sb[..., None, None] * C_l
    n_new = sa[..., None] * n + sb[..., None] * n_l
    return (C_new, n_new, m_new), (C, n, m)

def _mlstm_mix(x, w_in, conv_w, conv_b, b_i, b_f, hn_w, w_out):
    B, S, D = x.shape
    NC = S // CHUNK
    p = x @ w_in
    qk = jax.nn.silu(_causal_dwconv(p[..., :ML_QKW], conv_w, conv_b))
    v = p[..., ML_QKW:ML_QKW + ML_VW]
    o = p[..., ML_QKW + ML_VW:ML_QKW + 2 * ML_VW]
    gi = p[..., ML_QKW + 2 * ML_VW:ML_QKW + 2 * ML_VW + ML_HEADS]
    gf = p[..., ML_QKW + 2 * ML_VW + ML_HEADS:]
    chunks = lambda t, dh: t.reshape(B, NC, CHUNK, ML_HEADS, dh).transpose(0, 3, 1, 2, 4).astype(jnp.float32)
    q = chunks(qk[..., :ML_QKW // 2], ML_QK) * (ML_QK ** -0.5)
    k = chunks(qk[..., ML_QKW // 2:], ML_QK)
    v = chunks(v, ML_V)
    gate_chunks = lambda t: t.reshape(B, NC, CHUNK, ML_HEADS).transpose(0, 3, 1, 2)
    log_i = gate_chunks(_softcap(gi.astype(jnp.float32) + b_i))
    log_f = gate_chunks(jax.nn.log_sigmoid(_softcap(gf.astype(jnp.float32) + b_f)))
    bcum = jnp.cumsum(log_f, -1)
    causal = jnp.tril(jnp.ones((CHUNK, CHUNK), dtype=bool))
    d_log = jnp.where(causal, bcum[..., :, None] - bcum[..., None, :] + log_i[..., None, :], NEG)
    m_intra = jnp.max(d_log, -1)
    g_tot = bcum[..., -1]
    loc = g_tot[..., None] - bcum + log_i
    m_loc = jnp.max(loc, -1)
    wl = jnp.exp(loc - m_loc[..., None])
    C_loc = jnp.einsum('bhcs,bhcsd,bhcse->bhcde', wl, k, v)
    n_loc = jnp.einsum('bhcs,bhcsd->bhcd', wl, k)
    init = (jnp.zeros((B, ML_HEADS, ML_QK, ML_V), jnp.float32),
            jnp.zeros((B, ML_HEADS, ML_QK), jnp.float32),
            jnp.zeros((B, ML_HEADS), jnp.float32))
    cm = lambda t: jnp.moveaxis(t, 2, 0)
    _, (C_prev, n_prev, m_prev) = lax.scan(_mlstm_chunk_step, init, (cm(g_tot), cm(m_loc), cm(C_loc), cm(n_loc)))
    C_prev, n_prev, m_prev = jnp.moveaxis(C_prev, 0, 2), jnp.moveaxis(n_prev, 0, 2), jnp.moveaxis(m_prev, 0, 2)
    inter = bcum + m_prev[..., None]
    m_t = jnp.maximum(inter, m_intra)
    w_inter = jnp.exp(inter - m_t)
    w_intra = jnp.exp(d_log - m_t[..., None]) * jnp.einsum('bhctd,bhcsd->bhcts', q, k)
    num = w_inter[..., None] * jnp.einsum('bhctd,bhcde->bhcte', q, C_prev) + jnp.einsum('bhcts,bhcse->bhcte', w_intra, v)
    den = w_inter * jnp.einsum('bhctd,bhcd->bhct', q, n_prev) + jnp.sum(w_intra, -1)
    den = jnp.maximum(jnp.abs(den), jnp.exp(-m_t))
    h = num / den[..., None]
    h = h * lax.rsqrt(jnp.mean(h * h, -1, keepdims=True) + EPS) * hn_w[:, None, None, :]
    h = h.transpose(0, 2, 3, 1, 4).reshape(B, S, ML_VW).astype(x.dtype)
    return (h * jax.nn.sigmoid(o)) @ w_out

def _swiglu(x, w_gu, w_down):
    gu = x @ w_gu
    return (jax.nn.silu(gu[..., :D_FF]) * gu[..., D_FF:]) @ w_down

def first_inputs(seed: int = 0) -> dict:
    key = jax.random.key(seed)
    ks = jax.random.split(key, 32)
    nrm = lambda i, shape, s: jax.random.normal(ks[i], shape, jnp.float32) * s
    D = D_MODEL
    lin = jnp.arange(D, dtype=jnp.float32) / (D - 1)
    return {
        "x": nrm(0, (BATCH, SEQ, D), 1.0),
        "c": nrm(1, (BATCH, D), 1.0),
        "ada_w": nrm(2, (DEPTH, D, 6 * D), 0.3 * D ** -0.5),
        "ada_b": nrm(3, (DEPTH, 6 * D), 0.02),
        "rw_mix": jax.random.uniform(ks[4], (N_RWKV, 6, D), jnp.float32),
        "rw_w_in": nrm(5, (N_RWKV, D, RW_IN), D ** -0.5),
        "rw_w0": jnp.broadcast_to(-6.0 + 5.0 * lin ** 1.5, (N_RWKV, D)) + nrm(6, (N_RWKV, D), 0.1),
        "rw_w2": nrm(7, (N_RWKV, LORA_W, D), 0.3 * LORA_W ** -0.5),
        "rw_a0": nrm(8, (N_RWKV, D), 0.1),
        "rw_a2": nrm(9, (N_RWKV, LORA_A, D), LORA_A ** -0.5),
        "rw_g2": nrm(10, (N_RWKV, LORA_G, D), LORA_G ** -0.5),
        "rw_k_k": 0.85 + nrm(11, (N_RWKV, D), 0.05),
        "rw_k_a": 1.0 + nrm(12, (N_RWKV, D), 0.05),
        "rw_r_k": nrm(13, (N_RWKV, RW_HEADS, RW_HEAD), 0.1),
        "rw_gn_w": 1.0 + nrm(14, (N_RWKV, D), 0.05),
        "rw_gn_b": nrm(15, (N_RWKV, D), 0.02),
        "rw_w_out": nrm(16, (N_RWKV, D, D), D ** -0.5),
        "ml_w_in": nrm(17, (N_MLSTM, D, ML_IN), D ** -0.5),
        "ml_conv_w": nrm(18, (N_MLSTM, CONV_W, ML_QKW), CONV_W ** -0.5),
        "ml_conv_b": nrm(19, (N_MLSTM, ML_QKW), 0.02),
        "ml_b_i": nrm(20, (N_MLSTM, ML_HEADS), 0.1),
        "ml_b_f": jnp.broadcast_to(jnp.linspace(3.0, 6.0, ML_HEADS, dtype=jnp.float32), (N_MLSTM, ML_HEADS)) + nrm(21, (N_MLSTM, ML_HEADS), 0.1),
        "ml_hn_w": 1.0 + nrm(22, (N_MLSTM, ML_HEADS, ML_V), 0.05),
        "ml_w_out": nrm(23, (N_MLSTM, D, D), D ** -0.5),
        "ffn_w_gu": nrm(24, (DEPTH, D, 2 * D_FF), D ** -0.5),
        "ffn_w_down": nrm(25, (DEPTH, D_FF, D), D_FF ** -0.5),
        "final_w": 1.0 + nrm(26, (D,), 0.05),
    }

def first_block(x, c, ada_w, ada_b, rw_mix, rw_w_in, rw_w0, rw_w2, rw_a0, rw_a2, rw_g2, rw_k_k, rw_k_a,
              rw_r_k, rw_gn_w, rw_gn_b, rw_w_out, ml_w_in, ml_conv_w, ml_conv_b, ml_b_i, ml_b_f, ml_hn_w,
              ml_w_out, ffn_w_gu, ffn_w_down, final_w):
    c_act = jax.nn.silu(c)
    for i in range(DEPTH):
        mod = c_act @ ada_w[i] + ada_b[i]
        sh1, sc1, g1, sh2, sc2, g2 = [t[:, None, :] for t in jnp.split(mod, 6, axis=-1)]
        h = _rms(x) * (1.0 + sc1) + sh1
        j = i // N_MIXERS
        if i % N_MIXERS == 0:
            y = _rwkv7_mix(h, rw_mix[j], rw_w_in[j], rw_w0[j], rw_w2[j], rw_a0[j], rw_a2[j], rw_g2[j],
                           rw_k_k[j], rw_k_a[j], rw_r_k[j], rw_gn_w[j], rw_gn_b[j], rw_w_out[j])
        else:
            y = _mlstm_mix(h, ml_w_in[j], ml_conv_w[j], ml_conv_b[j], ml_b_i[j], ml_b_f[j], ml_hn_w[j], ml_w_out[j])
        x = x + g1 * y
        h = _rms(x) * (1.0 + sc2) + sh2
        x = x + g2 * _swiglu(h, ffn_w_gu[i], ffn_w_down[i])
    return _rms(x) * final_w


N_RET_LAYERS = (DEPTH + 1) // 2
N_MLA_LAYERS = DEPTH // 2

ROPE_BASE = 10000.0
NORM_EPS = 1e-6

RET_HEADS = 4
RET_QK_DIM = D_MODEL // RET_HEADS
RET_V_DIM = 2 * RET_QK_DIM
RET_WIDTH = RET_HEADS * RET_V_DIM
RET_CHUNK = 128

MLA_HEADS = 16
MLA_NOPE = 128
MLA_ROPE = 64
MLA_V = 128
Q_LORA = 3 * D_MODEL // 4
KV_LORA = D_MODEL // 4
MLA_WIDTH = MLA_HEADS * MLA_V
Q_BLOCK = 128

PLE_DIM = 256


def rms_norm(x, g):
    xf = x.astype(jnp.float32)
    y = xf * lax.rsqrt(jnp.mean(xf * xf, axis=-1, keepdims=True) + NORM_EPS)
    return (y * g.astype(jnp.float32)).astype(x.dtype)

def rope(x, pos):
    half = x.shape[-1] // 2
    inv_freq = ROPE_BASE ** (-jnp.arange(half, dtype=jnp.float32) / half)
    ang = pos.astype(jnp.float32)[..., None] * inv_freq
    cos = jnp.cos(ang)[:, :, None, :]
    sin = jnp.sin(ang)[:, :, None, :]
    xf = x.astype(jnp.float32)
    x1, x2 = xf[..., :half], xf[..., half:]
    return jnp.concatenate([x1 * cos - x2 * sin, x2 * cos + x1 * sin], axis=-1).astype(x.dtype)

def retention_branch(h, pos, w_in, gn_g, w_out):
    B, S, _ = h.shape
    n_chunks = S // RET_CHUNK
    z = h @ w_in
    qk_w = RET_HEADS * RET_QK_DIM
    q = z[..., :qk_w].reshape(B, S, RET_HEADS, RET_QK_DIM)
    k = z[..., qk_w:2 * qk_w].reshape(B, S, RET_HEADS, RET_QK_DIM)
    v = z[..., 2 * qk_w:2 * qk_w + RET_WIDTH].reshape(B, S, RET_HEADS, RET_V_DIM)
    gate = z[..., 2 * qk_w + RET_WIDTH:]
    q = rope(q, pos)
    k = rope(k, pos) * (RET_QK_DIM ** -0.5)

    log_g = jnp.log(1.0 - 2.0 ** (-5.0 - jnp.arange(RET_HEADS, dtype=jnp.float32)))
    idx = jnp.arange(RET_CHUNK, dtype=jnp.float32)
    rel = idx[:, None] - idx[None, :]
    dmask = jnp.where(rel[None] >= 0, jnp.exp(jnp.maximum(rel, 0.0)[None] * log_g[:, None, None]), 0.0)
    q_decay = jnp.exp((idx + 1.0)[None, :] * log_g[:, None])
    k_decay = jnp.exp((RET_CHUNK - 1.0 - idx)[None, :] * log_g[:, None])
    c_decay = jnp.exp(RET_CHUNK * log_g)

    def to_chunks(t):
        return t.astype(jnp.float32).reshape(B, n_chunks, RET_CHUNK, RET_HEADS, t.shape[-1]).transpose(1, 0, 3, 2, 4)

    qc, kc, vc = to_chunks(q), to_chunks(k), to_chunks(v)

    def step(state, inp):
        qb, kb, vb = inp
        a = jnp.einsum('bhid,bhjd->bhij', qb, kb) * dmask
        o = jnp.einsum('bhij,bhjv->bhiv', a, vb) + jnp.einsum(
            'bhid,bhdv->bhiv', qb * q_decay[..., None], state)
        state = state * c_decay[:, None, None] + jnp.einsum(
            'bhjd,bhjv->bhdv', kb * k_decay[..., None], vb)
        return state, o

    s0 = jnp.zeros((B, RET_HEADS, RET_QK_DIM, RET_V_DIM), jnp.float32)
    _, o = lax.scan(step, s0, (qc, kc, vc))
    o = o.transpose(1, 0, 3, 2, 4).reshape(B, S, RET_HEADS, RET_V_DIM)
    o = o * lax.rsqrt(jnp.mean(o * o, axis=-1, keepdims=True) + NORM_EPS)
    o = (o.reshape(B, S, RET_WIDTH) * gn_g.astype(jnp.float32)).astype(h.dtype)
    return (jax.nn.silu(gate) * o) @ w_out

def mla_branch(h, pos, w_in, q_norm_g, kv_norm_g, w_uq, w_uk, w_uv, w_out):
    B, S, _ = h.shape
    n_blocks = S // Q_BLOCK
    z = h @ w_in
    o1, o2, o3 = Q_LORA, Q_LORA + KV_LORA, Q_LORA + KV_LORA + MLA_ROPE
    c_q = rms_norm(z[..., :o1], q_norm_g)
    c_kv = rms_norm(z[..., o1:o2], kv_norm_g)
    k_rope = rope(z[..., o2:o3][:, :, None, :], pos)[:, :, 0, :]
    gate = z[..., o3:]

    q = (c_q @ w_uq).reshape(B, S, MLA_HEADS, MLA_NOPE + MLA_ROPE)
    q_nope = q[..., :MLA_NOPE]
    q_rope = rope(q[..., MLA_NOPE:], pos)
    q_abs = jnp.einsum('bshd,chd->bshc', q_nope, w_uk)
    scale = (MLA_NOPE + MLA_ROPE) ** -0.5
    q_cat = jnp.concatenate([q_abs, q_rope], axis=-1) * scale
    k_cat = jnp.concatenate([c_kv, k_rope], axis=-1)
    q_blocks = q_cat.reshape(B, n_blocks, Q_BLOCK, MLA_HEADS, -1).transpose(1, 0, 2, 3, 4)
    key_idx = jnp.arange(S)
    neg = jnp.finfo(jnp.float32).min

    def attend(args):
        qb, bi = args
        s = jnp.einsum('bqhc,bkc->bhqk', qb, k_cat).astype(jnp.float32)
        q_idx = bi * Q_BLOCK + jnp.arange(Q_BLOCK)
        s = jnp.where(key_idx[None, :] <= q_idx[:, None], s, neg)
        pr = jax.nn.softmax(s, axis=-1).astype(c_kv.dtype)
        return jnp.einsum('bhqk,bkc->bqhc', pr, c_kv)

    o_lat = lax.map(attend, (q_blocks, jnp.arange(n_blocks)))
    o_lat = o_lat.transpose(1, 0, 2, 3, 4).reshape(B, S, MLA_HEADS, KV_LORA)
    o = jnp.einsum('bshc,chd->bshd', o_lat, w_uv).reshape(B, S, MLA_WIDTH)
    return (jax.nn.silu(gate) * o) @ w_out

def second_inputs(seed: int = 0) -> dict:
    key = jax.random.key(seed)
    ks = jax.random.split(key, 20)
    f32 = jnp.float32

    def w(k, shape, fan_in):
        return jax.random.normal(k, shape, f32) * (fan_in ** -0.5)

    def gain(k, shape):
        return 1.0 + 0.02 * jax.random.normal(k, shape, f32)

    ret_in_w = 2 * RET_HEADS * RET_QK_DIM + 2 * RET_WIDTH
    mla_in_w = Q_LORA + KV_LORA + MLA_ROPE + MLA_WIDTH
    offset = jax.random.randint(ks[2], (BATCH, 1), 0, 4096, dtype=jnp.int32)
    return {
        "x": jax.random.normal(ks[0], (BATCH, SEQ, D_MODEL), f32),
        "p": jax.random.normal(ks[1], (DEPTH, BATCH, SEQ, PLE_DIM), f32),
        "positions": offset + jnp.arange(SEQ, dtype=jnp.int32)[None, :],
        "pre_norm_g": gain(ks[3], (DEPTH, D_MODEL)),
        "post_norm_g": gain(ks[4], (DEPTH, D_MODEL)),
        "ret_w_in": w(ks[5], (N_RET_LAYERS, D_MODEL, ret_in_w), D_MODEL),
        "ret_gn_g": gain(ks[6], (N_RET_LAYERS, RET_WIDTH)),
        "ret_w_out": w(ks[7], (N_RET_LAYERS, RET_WIDTH, D_MODEL), RET_WIDTH),
        "mla_w_in": w(ks[8], (N_MLA_LAYERS, D_MODEL, mla_in_w), D_MODEL),
        "mla_q_norm_g": gain(ks[9], (N_MLA_LAYERS, Q_LORA)),
        "mla_kv_norm_g": gain(ks[10], (N_MLA_LAYERS, KV_LORA)),
        "mla_w_uq": w(ks[11], (N_MLA_LAYERS, Q_LORA, MLA_HEADS * (MLA_NOPE + MLA_ROPE)), Q_LORA),
        "mla_w_uk": w(ks[12], (N_MLA_LAYERS, KV_LORA, MLA_HEADS, MLA_NOPE), KV_LORA),
        "mla_w_uv": w(ks[13], (N_MLA_LAYERS, KV_LORA, MLA_HEADS, MLA_V), KV_LORA),
        "mla_w_out": w(ks[14], (N_MLA_LAYERS, MLA_WIDTH, D_MODEL), MLA_WIDTH),
        "ple_w_proj": w(ks[15], (DEPTH, PLE_DIM, D_MODEL), PLE_DIM),
        "ple_w_gate": w(ks[16], (DEPTH, D_MODEL, D_MODEL), D_MODEL),
    }

def second_block(x, p, positions, pre_norm_g, post_norm_g, ret_w_in, ret_gn_g, ret_w_out,
              mla_w_in, mla_q_norm_g, mla_kv_norm_g, mla_w_uq, mla_w_uk, mla_w_uv, mla_w_out,
              ple_w_proj, ple_w_gate):
    for i in range(DEPTH):
        h = rms_norm(x, pre_norm_g[i])
        j = i // N_MIXERS
        if i % N_MIXERS == 0:
            y = retention_branch(h, positions, ret_w_in[j], ret_gn_g[j], ret_w_out[j])
        else:
            y = mla_branch(h, positions, mla_w_in[j], mla_q_norm_g[j], mla_kv_norm_g[j],
                           mla_w_uq[j], mla_w_uk[j], mla_w_uv[j], mla_w_out[j])
        x = x + rms_norm(y, post_norm_g[i])
        x = x + (p[i] @ ple_w_proj[i]) * jax.nn.sigmoid(x @ ple_w_gate[i])
    return x


def setup_inputs(seed=0):
    out = dict(first_inputs(seed))
    for name, value in second_inputs(seed + 1).items():
        if name != "x":
            out[name + "_2"] = value
    return out


def reference(
    x, c, ada_w, ada_b, rw_mix, rw_w_in, rw_w0, rw_w2, rw_a0, rw_a2, rw_g2, rw_k_k, rw_k_a,
    rw_r_k, rw_gn_w, rw_gn_b, rw_w_out, ml_w_in, ml_conv_w, ml_conv_b, ml_b_i, ml_b_f, ml_hn_w,
    ml_w_out, ffn_w_gu, ffn_w_down, final_w, p_2, positions_2, pre_norm_g_2, post_norm_g_2,
    ret_w_in_2, ret_gn_g_2, ret_w_out_2, mla_w_in_2, mla_q_norm_g_2, mla_kv_norm_g_2,
    mla_w_uq_2, mla_w_uk_2, mla_w_uv_2, mla_w_out_2, ple_w_proj_2, ple_w_gate_2,
):
    x = first_block(
        x, c, ada_w, ada_b, rw_mix, rw_w_in, rw_w0, rw_w2, rw_a0, rw_a2, rw_g2, rw_k_k, rw_k_a,
        rw_r_k, rw_gn_w, rw_gn_b, rw_w_out, ml_w_in, ml_conv_w, ml_conv_b, ml_b_i, ml_b_f,
        ml_hn_w, ml_w_out, ffn_w_gu, ffn_w_down, final_w,
    )
    return second_block(
        x, p_2, positions_2, pre_norm_g_2, post_norm_g_2, ret_w_in_2, ret_gn_g_2, ret_w_out_2,
        mla_w_in_2, mla_q_norm_g_2, mla_kv_norm_g_2, mla_w_uq_2, mla_w_uk_2, mla_w_uv_2,
        mla_w_out_2, ple_w_proj_2, ple_w_gate_2,
    )


_drawn_inputs = setup_inputs


def setup_inputs(seed=0):
    import zlib

    import numpy as np

    out = dict(_drawn_inputs(seed))
    spreads = {}
    factors = {'rw_w2': 8.0,
     'rw_a0': 7.294,
     'rw_k_k': 6.302,
     'rw_k_a': 4.843,
     'rw_gn_w': 5.672,
     'rw_gn_b': 7.45,
     'ml_conv_b': 8.0,
     'ml_b_i': 23.401,
     'ml_hn_w': 4.421,
     'post_norm_g_2': 2.753,
     'ret_gn_g_2': 3.352,
     'mla_q_norm_g_2': 5.86,
     'mla_kv_norm_g_2': 3.603}
    for name, (base, spread) in spreads.items():
        noise = np.random.default_rng([zlib.crc32(name.encode()), seed]).standard_normal(out[name].shape)
        drawn = base * np.exp(spread * noise) if base else spread * noise
        out[name] = __import__('jax').numpy.asarray(drawn.astype(out[name].dtype))
    for name, factor in factors.items():
        out[name] = (out[name] * factor).astype(out[name].dtype)
    return out
```

```python
from contextlib import ExitStack

import numpy as np

import concourse.bass as bass
from concourse import mybir

F32 = mybir.dt.float32
I32 = mybir.dt.int32
ALU = mybir.AluOpType
ACT = mybir.ActivationFunctionType
AX_X = mybir.AxisListType.X

P = 128
T = 512
D = 1024
KD = D // P
FF = 2816
KF = FF // P
EPS = 1e-6
GN_EPS = 64e-5
SLOT = 2048
SLOTS = 4
LORA, LORA_G = 64, 160
HEAD = 64
ML_HEADS, ML_QK, ML_V, CONV_W, GATE_CAP = 8, 64, 128, 4, 15.0
RET_HEADS, RET_QK, RET_V = 4, 256, 512
MLA_HEADS, NOPE, ROPE, Q_LORA, KV_LORA, PLE = 16, 128, 64, 768, 256, 256


def columns(widths):
    out, at_ = {}, 0
    for name, n in widths:
        out[name] = (at_, at_ + n)
        at_ += n
    return out, at_


VEC, VEC_COLS = columns([
    ("c", KD), ("ada_b", 96), ("mix", 6 * KD), ("w0", KD), ("a0", KD), ("k_k", KD), ("k_a", KD), ("r_k", KD),
    ("gn_w", KD), ("gn_b", KD), ("conv_w", CONV_W * KD), ("conv_b", KD), ("hn_w", KD), ("gate_b", 2),
    ("final_w", KD), ("pre_g", 2 * KD), ("post_g", 2 * KD), ("ret_gn", 16), ("q_g", 6), ("kv_g", 2)])
CONST, CONST_COLS = columns([
    ("block_ones", P), ("head_rows", 16 * KD), ("chunk_keep", T), ("fold", 64),
    ("before", P), ("upto", P), ("levels", 6 * P), ("later", P), ("inv_freq", 2)])


class Tally:

    def __init__(self, sem):
        self.sem, self.n = sem, 0

    def take(self, k):
        base = self.n
        self.n += k
        return base


def at(buf, n):
    return buf[:, n:n + 1, :] if isinstance(n, int) else buf[:, bass.ds(n, 1), :]


def one(ap):
    return ap.rearrange("p (a t) -> p a t", a=1)


def by_four(eng, n, body):
    if n // 4 >= 2:
        with eng.Fori(0, n // 4) as i:
            for s in range(4):
                body(i, s)
    else:
        for r in range(4 * (n // 4)):
            body(r // 4, r % 4)
    for s in range(n % 4):
        body(n // 4, s)


class Chip:

    def __init__(self, nc, ctx, io):
        self.nc, self.ctx, self.io = nc, ctx, io
        self.tallies = {}
        self.top = (nc.sbuf_base + 31) // 32 * 32
        self.floor = self.top
        self.blocks = 0
        self.groups = 2
        self.names = 0
        self.x_offset = self.top
        self.x = self.keep("x_res", [P, KD, T])
        self.ring = self.keep("ring", [P, SLOTS, SLOT])
        self.ones = self.keep("ones", [P, P])
        self.ident = self.keep("ident", [P, P])
        self.mod = self.keep("mod", [P, 96])
        self.vec = self.keep("vec", [P, VEC_COLS])
        self.const = self.keep("const", [P, CONST_COLS])
        self.eps = self.keep("eps", [P, 1])
        self.gn_eps = self.keep("gn_eps", [P, 1])
        self.bank = [ctx.enter_context(nc.psum_tensor(f"bank{n}", [P, 512], F32)) for n in range(8)]
        self.w_full = [self.sem(f"w_full{s}") for s in range(SLOTS)]
        self.pair_free = [self.sem(f"pair_free{s}") for s in range(2)]
        self.gemm_done = self.sem("gemm_done")
        self.floor = self.base_floor = self.top

    def v(self, name):
        a, b = VEC[name]
        return self.vec[:, a:b]

    def k(self, name):
        a, b = CONST[name]
        return self.const[:, a:b]

    def sem(self, name):
        return self.ctx.enter_context(self.nc.semaphore(name))

    def tally(self, name):
        if name not in self.tallies:
            self.tallies[name] = Tally(self.sem(name))
        return self.tallies[name]

    def begin_phase(self):
        self.top = self.floor
        self.steps = self.loads = 0

    def step_tally(self):
        self.steps += 1
        return self.tally(f"step{self.steps}")

    def load_tally(self):
        self.loads += 1
        return self.tally(f"loaded{self.loads}")

    def keep(self, name, shape, dt=F32):
        size = 1
        for n in shape[1:]:
            size *= n
        self.names += 1
        t = self.nc.alloc_sbuf_tensor_at(f"{name}_{self.names}", shape, dt, offset=self.top)
        self.top += (size * 4 + 31) // 32 * 32
        assert self.top <= 229344, (name, self.top)
        return t

    def take_blocks(self, n):
        b, self.blocks = self.blocks, self.blocks + n
        return b

    def take_groups(self, n):
        u, self.groups = self.groups, self.groups + n
        return u

    def slot(self, b, kt):
        return self.ring[:, b % SLOTS, 0:(SLOT // kt) * kt].rearrange("p (k n) -> p k n", k=kt)

    def wait_block(self, pe, b, i=0):
        pe.wait_ge(self.w_full[b % SLOTS], 16 * (b // SLOTS + 1) + 16 * i)

    def wait_pair(self, pe, u, i=0):
        pe.wait_ge(self.pair_free[u % 2], 2 * (u // 2) + 4 * i)

    def pair(self, u):
        return self.bank[2 * (u % 2)], self.bank[2 * (u % 2) + 1]

    def wait_tile(self, eng, b, j, i=0):
        eng.wait_ge(self.gemm_done, 2 * b + j + 1 + 8 * i)

    def pe_features(self, pe, b0, u0, n, kt, rhs, before=None):
        cols = 2 * P

        def body(i, s):
            self.wait_block(pe, b0 + s, i)
            self.wait_pair(pe, u0 + s, i)
            w = self.ring[:, (b0 + s) % SLOTS, 0:kt * cols].rearrange("p (k n) -> p k n", k=kt)
            for j in range(2):
                for k in range(kt):
                    if before and s == 0 and j == 0:
                        before(k)
                    mm = pe.matmul(self.pair(u0 + s)[j][:, :], w[:, k, j * P:(j + 1) * P], rhs(k),
                                   start=(k == 0), stop=(k == kt - 1))
                mm.then_inc(self.gemm_done, 1)

        by_four(pe, n, body)

    def pe_tokens(self, pe, b0, u0, n, kt, lhs, before=None):
        cols = 2 * P

        def body(i, s):
            self.wait_block(pe, b0 + s, i)
            self.wait_pair(pe, u0 + s, i)
            w = self.ring[:, (b0 + s) % SLOTS, 0:kt * cols].rearrange("p (k n) -> p k n", k=kt)
            for j in range(2):
                for half in range(2):
                    for k in range(kt):
                        if before and s == 0 and j == 0 and half == 0:
                            before(k)
                        tok = (2 * j + half) * P
                        mm = pe.matmul(self.pair(u0 + s)[j][:, half * cols:(half + 1) * cols],
                                       lhs(k)[:, tok:tok + P], w[:, k, :],
                                       start=(k == 0), stop=(k == kt - 1))
                mm.then_inc(self.gemm_done, 1)

        by_four(pe, n, body)

    def pe_long(self, pe, b0, u0, tiles, halves, kt, rhs, before=None):
        per = 2 * halves
        step = 8 // per if per == 4 else 2

        def group(i, r):
            for tile in range(2):
                for half in range(halves):
                    s = r * per + tile * halves + half
                    self.wait_block(pe, b0 + s, i * (step * per // 4))
                    if tile == 0 and half == 0:
                        self.wait_pair(pe, u0 + r, i) if step == 4 else self.wait_pair2(pe, u0 + r, i)
                    w = self.ring[:, (b0 + s) % SLOTS, 0:kt * P].rearrange("p (k n) -> p k n", k=kt)
                    for k in range(kt):
                        kk = half * kt + k
                        if before and s == 0:
                            before(kk)
                        mm = pe.matmul(self.pair(u0 + r)[tile][:, :], w[:, k, :], rhs(kk),
                                       start=(kk == 0), stop=(kk == halves * kt - 1))
                    mm.then_inc(self.gemm_done, 2)

        with pe.Fori(0, tiles // 2 // step) as i:
            for r in range(step):
                group(i, r)

    def wait_pair2(self, pe, u, i):
        pe.wait_ge(self.pair_free[u % 2], 2 * (u // 2) + 2 * i)


class Norm:

    def __init__(self, chip, src, dst, tiles, gain, shift=None, bank=4, rstd=None, squares=None):
        self.sq = squares or dst
        self.c, self.src, self.dst, self.tiles = chip, src, dst, tiles
        self.gain, self.shift, self.bank = gain, shift, chip.bank[bank]
        self.rstd = rstd if rstd is not None else chip.keep("rstd", [P, T])
        self.steps = {}
        for name, k in (("squared", tiles), ("mean_square", 1), ("root", 1), ("rstd_ready", 1),
                        ("scaled", tiles if shift else 0), ("normed", tiles)):
            t = chip.tally("norm_" + name)
            self.steps[name] = (t.sem, t.take(k))
        self.squared, self.mean_square, self.root, self.rstd_ready, self.scaled, self.normed = \
            self.steps.values()

    def scalar(self, act, ready=None):
        sem, base = self.squared
        for k in range(self.tiles):
            if ready:
                ready(k)
            act.activation(self.sq(k), self.src(k), ACT.Square).then_inc(sem, 1)
        act.wait_ge(self.mean_square[0], self.mean_square[1] + 1)
        act.activation(self.rstd[:, :], self.bank[:, :], ACT.Sqrt, bias=self.c.eps[:, :],
                       scale=1.0 / (self.tiles * P)).then_inc(self.root[0], 1)
        if self.shift:
            for k in range(self.tiles):
                act.wait_ge(self.scaled[0], self.scaled[1] + k + 1)
                act.activation(self.dst(k), self.dst(k), ACT.Identity, bias=self.shift(k))\
                   .then_inc(self.normed[0], 1)

    def tensor(self, pe):
        for k in range(self.tiles):
            pe.wait_ge(self.squared[0], self.squared[1] + k + 1)
            mm = pe.matmul(self.bank[:, :], self.c.ones[:, :], self.sq(k),
                           start=(k == 0), stop=(k == self.tiles - 1))
        mm.then_inc(self.mean_square[0], 1)

    def vector(self, dve):
        dve.wait_ge(self.root[0], self.root[1] + 1)
        dve.reciprocal(self.rstd[:, :], self.rstd[:, :]).then_inc(self.rstd_ready[0], 1)
        dve.wait_ge(self.rstd_ready[0], self.rstd_ready[1] + 1)
        sem = self.scaled[0] if self.shift else self.normed[0]
        for k in range(self.tiles):
            dve.scalar_tensor_tensor(out=self.dst(k), in0=self.src(k), scalar=self.gain(k),
                                     in1=self.rstd[:, :], op0=ALU.mult, op1=ALU.mult).then_inc(sem, 1)

    def wait(self, eng, k):
        eng.wait_ge(self.normed[0], self.normed[1] + k + 1)


class Step:

    def __init__(self, chip, name, results):
        tally = chip.step_tally()
        self.name, self.sem, self.base = name, tally.sem, tally.take(results)

    def of(self, k):
        return self.base + k + 1


class Load:

    def __init__(self, chip):
        tally = chip.load_tally()
        self.sem = tally.sem
        self.landed = tally.take(16) + 16


def ada(chip):
    blocks = ADA_BLOCKS
    slots = 4
    wa = chip.keep("ada_w", [P, slots, SLOT])
    acc = chip.keep("ada_acc", [P, 2, 2 * P])
    c_act = chip.keep("c_act", [P, KD])
    landed = [chip.sem(f"ada_landed{s}") for s in range(slots)]
    silu = Step(chip, "ada_silu", 1)
    part = Step(chip, "ada_part", blocks * KD)
    summed = Step(chip, "ada_summed", blocks)
    biased = Step(chip, "ada_biased", 1)
    one_plus = Step(chip, "ada_one_plus", 1)

    def tensor(pe):
        for g in range(blocks):
            pe.wait_ge(part.sem, part.of(g * KD + KD - 1))
            for j in range(2):
                mm = pe.matmul(chip.bank[5][:, 2 * g + j:2 * g + j + 1], acc[:, g % 2, j * P:(j + 1) * P],
                               chip.ones[:, 0:1], start=True, stop=True)
            mm.then_inc(summed.sem, 1)

    def scalar(act):
        act.activation(c_act[:, :], chip.v("c"), ACT.Silu).then_inc(silu.sem, 1)
        for g in range(blocks):
            if g >= slots:
                act.wait_ge(part.sem, part.of((g - slots) * KD + KD - 1))
            act.dma_start(wa[:, g % slots, :], chip.io["ada"][g]).then_inc(landed[g % slots], 16)

    def vector(dve):
        dve.wait_ge(silu.sem, silu.of(0))
        for g in range(blocks):
            dve.wait_ge(landed[g % slots], 16 * (g // slots + 1))
            if g >= 2:
                dve.wait_ge(summed.sem, summed.of(g - 2))
            w = wa[:, g % slots, :].rearrange("p (k n) -> p k n", k=KD)
            dve.tensor_scalar(acc[:, g % 2, :], w[:, 0, :], c_act[:, 0:1], None, ALU.mult)\
               .then_inc(part.sem, 1)
            for k in range(1, KD):
                dve.wait_ge(part.sem, part.of(g * KD + k - 1))
                dve.scalar_tensor_tensor(out=acc[:, g % 2, :], in0=w[:, k, :], scalar=c_act[:, k:k + 1],
                                         in1=acc[:, g % 2, :], op0=ALU.mult, op1=ALU.add)\
                   .then_inc(part.sem, 1)
        dve.wait_ge(summed.sem, summed.of(blocks - 1))
        dve.tensor_tensor(chip.mod[:, :], chip.bank[5][:, 0:96], chip.v("ada_b"), ALU.add)\
           .then_inc(biased.sem, 1)
        dve.wait_ge(biased.sem, biased.of(0))
        scales = chip.mod[:, :].rearrange("p (l k) -> p l k", k=24)[:, :, KD:2 * KD]
        dve.tensor_scalar(scales, scales, 1.0, None, ALU.add).then_inc(one_plus.sem, 1)

    return tensor, scalar, vector, None


ADA_BLOCKS = 48
KAPPA = float(np.exp(-0.5))
CHUNK = 64
NC_ = T // CHUNK
SEGS = ("r", "k", "v", "w", "a", "g")
MIX_ROW = {"r": 0, "w": 1, "k": 2, "v": 3, "a": 4, "g": 5}


class Rwkv:

    def __init__(self, chip):
        full = [P, KD, T]
        self.r = chip.keep("rw_r", full)
        self.k = chip.keep("rw_k", full)
        self.v = chip.keep("rw_v", full)
        self.cum = chip.keep("rw_cum", full)
        self.nkk = chip.keep("rw_nkk", full)
        self.kb = chip.keep("rw_kb", full)
        self.bsum = chip.keep("rw_bsum", [16, T])
        self.sgl = chip.keep("rw_sgl", [P, 2, T])
        chip.floor = chip.top


def rwkv_project(chip):
    f = chip.rwkv = Rwkv(chip)
    h = chip.keep("h", [P, KD, T])
    xx = chip.keep("shift_diff", [P, KD, T])
    twl = chip.keep("tanh_wl", [LORA, T])
    al = chip.keep("al", [LORA, T])
    tmp = chip.keep("tmp", [P, 2, T])
    tmp2 = chip.keep("tmp2", [P, 2, T])
    xs = [f.nkk, f.kb]
    a_sig, squares = h, xx
    norm = Norm(chip, lambda k: chip.x[:, k, :], lambda k: h[:, k, :], KD,
                lambda k: chip.mod[:, 8 + k:9 + k], lambda k: chip.mod[:, k:k + 1], rstd=tmp[:, 0, :])
    diff = Step(chip, "rw_diff", KD + 1)
    mixed = Step(chip, "rw_mixed", 6 * KD)
    seg_done = {}
    blk = {s: chip.take_blocks(4) for s in "rkv"}
    grp = {s: chip.take_groups(4) for s in "rkv"}
    b_wa, u_wa = chip.take_blocks(1), chip.take_groups(1)
    b_g, u_g = chip.take_blocks(1), chip.take_groups(1)
    b_l, u_l = chip.take_blocks(1), chip.take_groups(KD)
    low = Step(chip, "rw_low", 2)
    lora = Step(chip, "rw_lora", 2 * KD)
    sigma = Step(chip, "rw_sigma", KD)
    a_ready = Step(chip, "rw_a", KD)
    cum = Step(chip, "rw_cumsum", KD)
    kk = Step(chip, "rw_kk", KD)
    kk_sq = Step(chip, "rw_kk_sq", KD)
    kk_sum = Step(chip, "rw_kk_sum", KD)
    kk_root = Step(chip, "rw_kk_root", KD)
    chain = Step(chip, "rw_key_chain", 6 * KD)
    bonus = Step(chip, "rw_bonus", KD)
    bsum = Step(chip, "rw_bsum", 1)
    bcopy = Step(chip, "rw_bsum_copied", 1)
    order = {"r": 0, "k": 1, "v": 2, "w": 3, "a": 4, "g": 5}

    def tensor(pe):
        norm.tensor(pe)

        def rhs_of(seg):
            buf = xs[order[seg] % 2]
            return lambda k: buf[:, k, :]

        def before_of(seg):
            return lambda k: pe.wait_ge(mixed.sem, mixed.of(order[seg] * KD + k))

        for seg in "rkv":
            for k in range(KD):
                before_of(seg)(k)
            chip.pe_features(pe, blk[seg], grp[seg], 4, KD, rhs_of(seg))
        chip.wait_block(pe, b_wa)
        chip.wait_pair(pe, u_wa)
        w = chip.ring[:, b_wa % SLOTS, :].rearrange("p (k n) -> p k n", k=KD)
        for j, seg in enumerate("wa"):
            for k in range(KD):
                before_of(seg)(k)
                mm = pe.matmul(chip.pair(u_wa)[j][0:LORA, :], w[:, k, j * LORA:(j + 1) * LORA],
                               rhs_of(seg)(k), start=(k == 0), stop=(k == KD - 1))
            mm.then_inc(chip.gemm_done, 1)
        chip.wait_block(pe, b_g)
        chip.wait_pair(pe, u_g)
        w = chip.ring[:, b_g % SLOTS, :].rearrange("p (k n) -> p k n", k=KD)
        for j, m in enumerate((P, LORA_G - P)):
            for k in range(KD):
                before_of("g")(k)
                mm = pe.matmul(chip.pair(u_g)[j][0:m, :], w[:, k, j * P:j * P + m],
                               rhs_of("g")(k), start=(k == 0), stop=(k == KD - 1))
            mm.then_inc(chip.gemm_done, 1)
        chip.wait_block(pe, b_l)
        pe.wait_ge(low.sem, low.of(1))
        w = chip.ring[0:LORA, b_l % SLOTS, :].rearrange("p (j n) -> p j n", j=2)
        for n in range(KD):
            chip.wait_pair(pe, u_l + n)
            for j, src in enumerate((twl, al)):
                pe.matmul(chip.pair(u_l + n)[j][:, :], w[:, j, n * P:(n + 1) * P], src[:, :],
                          start=True, stop=True).then_inc(lora.sem, 1)
        pe.wait_ge(chip.gemm_done, 2 * b_l + 2)
        for n in range(KD):
            pe.wait_ge(kk_sq.sem, kk_sq.of(n))
            if n >= 2:
                pe.wait_ge(kk_root.sem, kk_root.of(n - 2))
            pe.matmul(chip.bank[5 + n % 2][:, :], chip.k("block_ones"), squares[:, n, :],
                      start=True, stop=True).then_inc(kk_sum.sem, 1)
        for n in range(KD):
            pe.wait_ge(bonus.sem, bonus.of(n))
            mm = pe.matmul(chip.bank[7][0:16, :], chip.k("head_rows")[:, 16 * n:16 * n + 16], squares[:, n, :],
                           start=(n == 0), stop=(n == KD - 1))
        mm.then_inc(bsum.sem, 1)

    def scalar(act):
        norm.scalar(act)
        for q, (seg, dst) in enumerate((("r", f.r), ("k", f.k), ("v", f.v))):
            for n in range(KD):
                chip.wait_tile(act, blk[seg] + n // 2, n % 2)
                u = grp[seg] + n // 2
                act.activation(dst[:, n, :], chip.pair(u)[n % 2][:, :], ACT.Copy)\
                   .then_inc(chip.pair_free[u % 2], 1)
        u = u_wa
        chip.wait_tile(act, b_wa, 0)
        act.activation(twl[:, :], chip.pair(u)[0][0:LORA, :], ACT.Tanh).then_inc(low.sem, 1)
        chip.wait_tile(act, b_wa, 1)
        act.activation(al[:, :], chip.pair(u)[1][0:LORA, :], ACT.Copy).then_inc(low.sem, 1)
        act.wait_ge(low.sem, low.of(1))
        act.sem_inc(chip.pair_free[u % 2], 2)
        u = u_g
        chip.wait_tile(act, b_g, 0)
        act.activation(f.sgl[:, 0, :], chip.pair(u)[0][:, :], ACT.Sigmoid).then_inc(chip.pair_free[u % 2], 1)
        chip.wait_tile(act, b_g, 1)
        act.activation(f.sgl[0:LORA_G - P, 1, :], chip.pair(u)[1][0:LORA_G - P, :], ACT.Sigmoid)\
           .then_inc(chip.pair_free[u % 2], 1)
        for n in range(KD):
            u = u_l + n
            act.wait_ge(lora.sem, lora.of(2 * n))
            if n >= 2:
                act.wait_ge(cum.sem, cum.of(n - 2))
            act.activation(tmp[:, n % 2, :], chip.pair(u)[0][:, :], ACT.Sigmoid,
                           bias=chip.v("w0")[:, n:n + 1]).then_inc(sigma.sem, 1)
            act.wait_ge(lora.sem, lora.of(2 * n + 1))
            if n == 0:
                act.wait_ge(mixed.sem, mixed.of(6 * KD - 1))
            act.activation(a_sig[:, n, :], chip.pair(u)[1][:, :], ACT.Sigmoid,
                           bias=chip.v("a0")[:, n:n + 1]).then_inc(a_ready.sem, 1)
            act.wait_ge(a_ready.sem, a_ready.of(n))
            act.sem_inc(chip.pair_free[u % 2], 2)
        act.sem_inc(chip.gemm_done, 2)
        for n in range(KD):
            act.wait_ge(kk.sem, kk.of(n))
            act.activation(squares[:, n, :], f.nkk[:, n, :], ACT.Square).then_inc(kk_sq.sem, 1)
        for n in range(KD):
            act.wait_ge(kk_sum.sem, kk_sum.of(n))
            if n >= 2:
                act.wait_ge(chain.sem, chain.of(6 * (n - 2) + 2))
            act.activation(tmp2[:, n % 2, :], chip.bank[5 + n % 2][:, :], ACT.Sqrt).then_inc(kk_root.sem, 1)
        act.wait_ge(bsum.sem, bsum.of(0))
        act.activation(f.bsum[:, :], chip.bank[7][0:16, :], ACT.Copy).then_inc(bcopy.sem, 1)

    def vector(dve):
        norm.vector(dve)
        for k in range(KD):
            norm.wait(dve, k)
            dve.tensor_tensor(xx[:, k, 1:T], h[:, k, 0:T - 1], h[:, k, 1:T], ALU.subtract)\
               .then_inc(diff.sem, 1)
        dve.tensor_scalar(xx[:, :, 0:1], h[:, :, 0:1], -1.0, None, ALU.mult).then_inc(diff.sem, 1)
        dve.wait_ge(diff.sem, diff.of(KD))
        last_block = {"v": blk["r"] + 3, "w": blk["k"] + 3, "a": blk["v"] + 3}
        for seg in ("r", "k", "v", "w", "a", "g"):
            if seg in last_block:
                dve.wait_ge(chip.gemm_done, 2 * last_block[seg] + 2)
            if seg == "g":
                dve.wait_ge(chip.gemm_done, 2 * b_wa + 1)
            row = MIX_ROW[seg]
            for k in range(KD):
                dve.scalar_tensor_tensor(out=xs[order[seg] % 2][:, k, :], in0=xx[:, k, :],
                                         scalar=chip.v("mix")[:, row * KD + k:row * KD + k + 1],
                                         in1=h[:, k, :], op0=ALU.mult, op1=ALU.add).then_inc(mixed.sem, 1)
        dve.wait_ge(chip.gemm_done, 2 * b_g + 2)
        dve.wait_ge(chip.pair_free[(grp["v"] + 3) % 2], 2 * ((grp["v"] + 3) // 2 + 1))
        for n in range(KD):
            dve.tensor_scalar(f.nkk[:, n, :], f.k[:, n, :], chip.v("k_k")[:, n:n + 1], None, ALU.mult)\
               .then_inc(kk.sem, 1)
        for n in range(KD):
            dve.wait_ge(sigma.sem, sigma.of(n))
            dve.tensor_tensor_scan(f.cum[:, n, :], chip.k("chunk_keep"), tmp[:, n % 2, :], 0.0,
                                   ALU.mult, ALU.add).then_inc(cum.sem, 1)
        for n in range(KD):
            dve.wait_ge(kk_root.sem, kk_root.of(n))
            t = tmp2[:, n % 2, :]
            dve.tensor_scalar(t, t, 1e-12, None, ALU.max).then_inc(chain.sem, 1)
            dve.wait_ge(chain.sem, chain.of(6 * n))
            dve.reciprocal(t, t).then_inc(chain.sem, 1)
            dve.wait_ge(chain.sem, chain.of(6 * n + 1))
            dve.scalar_tensor_tensor(out=f.nkk[:, n, :], in0=f.nkk[:, n, :], scalar=-1.0, in1=t,
                                     op0=ALU.mult, op1=ALU.mult).then_inc(chain.sem, 1)
            dve.wait_ge(chain.sem, chain.of(6 * n + 2))
            dve.wait_ge(a_ready.sem, a_ready.of(n))
            dve.scalar_tensor_tensor(out=f.kb[:, n, :], in0=f.nkk[:, n, :], scalar=-1.0, in1=a_sig[:, n, :],
                                     op0=ALU.mult, op1=ALU.mult).then_inc(chain.sem, 1)
            dve.wait_ge(chain.sem, chain.of(6 * n + 3))
            dve.tensor_scalar(a_sig[:, n, :], a_sig[:, n, :], 1.0, chip.v("k_a")[:, n:n + 1],
                              ALU.subtract, ALU.mult).then_inc(chain.sem, 1)
            dve.wait_ge(chain.sem, chain.of(6 * n + 4))
            dve.scalar_tensor_tensor(out=f.k[:, n, :], in0=a_sig[:, n, :], scalar=1.0, in1=f.k[:, n, :],
                                     op0=ALU.add, op1=ALU.mult).then_inc(chain.sem, 1)
            dve.wait_ge(chain.sem, chain.of(6 * n + 5))
            dve.wait_ge(kk_sum.sem, kk_sum.of(n))
            dve.scalar_tensor_tensor(out=squares[:, n, :], in0=f.r[:, n, :],
                                     scalar=chip.v("r_k")[:, n:n + 1], in1=f.k[:, n, :],
                                     op0=ALU.mult, op1=ALU.mult).then_inc(bonus.sem, 1)

    return tensor, scalar, vector, None


def rwkv_chunks(chip):
    f = chip.rwkv
    nc = chip.nc
    wide = [P, KD, P]
    half_w = [P, KD, CHUNK]
    abd, rbd, kbd, bbd = (chip.keep(n, wide) for n in ("a_bd", "r_bd", "k_bd", "b_bd"))
    L, Arb, Aak, Ark = (chip.keep(n, wide) for n in ("ab_bd", "rb_bd", "ak_bd", "rk_bd"))
    Y, Tm, Lm = (chip.keep(n, wide) for n in ("inv_t", "step_t", "level"))
    e = chip.keep("decay", [P, KD, CHUNK + 1])
    low_top = chip.top
    chip.top = chip.x_offset
    X, ra = chip.keep("inv", wide), chip.keep("ra", wide)
    Vs, R, S = (chip.keep(n, half_w) for n in ("v_tok", "rhs", "state"))
    U = en = R
    assert chip.top <= chip.x_offset + KD * T * 4
    chip.top = low_top
    vbd, kt, bt, ybd = Lm, Tm, Lm, X

    def step(name, per):
        s = Step(chip, "ch_" + name, per * NC_)
        s.per = per
        return s

    decay, stacked, keys = step("decay", 2), step("stacked", 2), step("keys", 4)
    diag, vdiag = step("diag", 4), step("vdiag", 2)
    pair_ab, pair_ak, vtok_mm, vtok = step("ab", 2), step("ak", 2), step("vtok_mm", 2), step("vtok", 2)
    masked = step("masked", 8)
    level = step("level", 6)
    first_mm, first_x, first_y = step("first_mm", 2), step("first_x", 2), step("first_y", 2)
    t_mm, t_ready = step("t_mm", 10), step("t_ready", 10)
    x_mm, x_ready = step("x_mm", 8), step("x_ready", 8)
    y_mm, y_ready = step("y_mm", 10), step("y_ready", 10)
    tr_mm, tr = step("tr_mm", 4), step("tr", 4)
    r_mm, r_ready = step("r_mm", 2), step("r_ready", 2)
    u_mm, u_ready = step("u_mm", 2), step("u_ready", 2)
    o_mm, o_diag, ot_mm, o_out = step("o_mm", 2), step("o_diag", 4), step("ot_mm", 2), step("o_out", 2)
    s_mm, s_sum, state = step("s_mm", 2), step("s_sum", 2), step("state", 2)
    cleared = Step(chip, "ch_cleared", 6)

    def wait(eng, st, c, k):
        eng.wait_ge(st.sem, st.of(k) + c * st.per)

    def wait_last(eng, st, c, k):
        eng.wait_ge(st.sem, st.of(k) + c * st.per - st.per) if not isinstance(c, int) or c else None

    def rows(h):
        return slice(64 * h, 64 * h + 64)

    def quad(buf, h):
        return buf[:, 4 * h:4 * h + 4, :]

    def psum(n, w):
        return chip.bank[n][:, 0:4 * w].rearrange("p (q w) -> p q w", q=4)

    def chunks(eng, body):
        body(0)
        with eng.Fori(1, NC_) as c:
            body(c)

    def cut(buf, c):
        return buf[:, :, bass.ds(c * CHUNK, CHUNK)] if not isinstance(c, int) \
            else buf[:, :, c * CHUNK:(c + 1) * CHUNK]

    def cut_part(buf, c, a, b, q0=0, q1=KD):
        if isinstance(c, int):
            return buf[a:b, q0:q1, c * CHUNK:(c + 1) * CHUNK]
        return buf[a:b, q0:q1, bass.ds(c * CHUNK, CHUNK)]

    def tensor(pe):
        pe.wait_ge(cleared.sem, cleared.of(5))

        def body(c):
            for h in range(2):
                wait(pe, stacked, c, 1)
                wait(pe, keys, c, 3)
                if h == 0:
                    wait_last(pe, state, c, 1)
                    wait_last(pe, o_out, c, 1)
                for q in range(4):
                    mm = pe.matmul(psum(4 * h, P)[:, q, :], bbd[:, 4 * h + q, :], ra[:, 4 * h + q, :],
                                   start=True, stop=True)
                mm.then_inc(pair_ab.sem, 1)
                for q in range(4):
                    mm = pe.matmul(psum(4 * h + 1, P)[:, q, :], kbd[:, 4 * h + q, :], ra[:, 4 * h + q, :],
                                   start=True, stop=True)
                mm.then_inc(pair_ak.sem, 1)
                wait(pe, vdiag, c, 1)
                for q in range(4):
                    mm = pe.matmul(psum(4 * h + 3, CHUNK)[:, q, :], vbd[:, 4 * h + q, :],
                                   chip.k("fold"), start=True, stop=True)
                mm.then_inc(vtok_mm.sem, 1)
            for h in range(2):
                wait(pe, level, c, 0)
                wait(pe, masked, c, 4 * h + 1)
                for q in range(4):
                    mm = pe.matmul(psum(4 * h, P)[:, q, :], Lm[:, 4 * h + q, :], chip.ident[:, :],
                                   start=True, stop=True)
                mm.then_inc(first_mm.sem, 1)
            for lv in range(1, 6):
                for h in range(2):
                    wait(pe, level, c, lv)
                    if lv == 1:
                        wait(pe, first_x, c, h)
                        wait(pe, first_y, c, h)
                    else:
                        wait(pe, x_ready, c, 2 * (lv - 2) + h)
                        wait(pe, y_ready, c, 2 * (lv - 2) + h)
                    for q in range(4):
                        mm = pe.matmul(psum(4 * h, P)[:, q, :], Lm[:, 4 * h + q, :], X[:, 4 * h + q, :],
                                       start=True, stop=True)
                    mm.then_inc(t_mm.sem, 1)
                for h in range(2):
                    wait(pe, t_ready, c, 2 * (lv - 1) + h)
                    if lv < 5:
                        for q in range(4):
                            mm = pe.matmul(psum(4 * h + 1, P)[:, q, :], Y[:, 4 * h + q, :],
                                           Tm[:, 4 * h + q, :], start=True, stop=True)
                        mm.then_inc(x_mm.sem, 1)
                    for q in range(4):
                        mm = pe.matmul(psum(4 * h + 2, P)[:, q, :], Tm[:, 4 * h + q, :],
                                       Y[:, 4 * h + q, :], start=True, stop=True)
                    mm.then_inc(y_mm.sem, 1)
            for h in range(2):
                wait(pe, masked, c, 7)
                for n, src in enumerate((kbd, bbd)):
                    for q in range(4):
                        mm = pe.matmul(psum(4 * h + n, P)[:, q, :], src[:, 4 * h + q, :], chip.ident[:, :],
                                       start=True, stop=True)
                    mm.then_inc(tr_mm.sem, 1)
                wait(pe, vtok, c, h)
                for q in range(4):
                    p = 4 * h + q
                    pe.matmul(psum(4 * h + 3, CHUNK)[:, q, :], abd[:, p, :], S[:, p, :], start=True, stop=False)
                    mm = pe.matmul(psum(4 * h + 3, CHUNK)[:, q, :], Aak[:, p, :], Vs[:, p, :],
                                   start=False, stop=True)
                mm.then_inc(r_mm.sem, 1)
            for h in range(2):
                wait(pe, r_ready, c, h)
                wait(pe, y_ready, c, 8 + h)
                for q in range(4):
                    mm = pe.matmul(psum(4 * h + 2, CHUNK)[:, q, :], Y[:, 4 * h + q, :], R[:, 4 * h + q, :],
                                   start=True, stop=True)
                mm.then_inc(u_mm.sem, 1)
            for h in range(2):
                wait(pe, u_ready, c, h)
                wait(pe, tr, c, 2 * h + 1)
                for q in range(4):
                    p = 4 * h + q
                    pe.matmul(psum(4 * h, CHUNK)[:, q, :], kt[:, p, :], Vs[:, p, :], start=True, stop=False)
                    mm = pe.matmul(psum(4 * h, CHUNK)[:, q, :], bt[:, p, :], U[:, p, :], start=False, stop=True)
                mm.then_inc(s_mm.sem, 1)
                for q in range(4):
                    p = 4 * h + q
                    o = psum(4 * h + 1, CHUNK)[:, q, :]
                    pe.matmul(o, rbd[:, p, :], S[:, p, :], start=True, stop=False)
                    pe.matmul(o, Ark[:, p, :], Vs[:, p, :], start=False, stop=False)
                    mm = pe.matmul(o, Arb[:, p, :], U[:, p, :], start=False, stop=True)
                mm.then_inc(o_mm.sem, 1)
            for h in range(2):
                wait(pe, o_diag, c, 2 * h + 1)
                for q in range(4):
                    mm = pe.matmul(psum(4 * h + 2, CHUNK)[:, q, :], ybd[:, 4 * h + q, :], chip.k("fold"),
                                   start=True, stop=True)
                mm.then_inc(ot_mm.sem, 1)

        chunks(pe, body)

    def scalar(act):
        def body(c):
            wait_last(act, state, c, 1)
            act.activation(e[:, :, 1:CHUNK + 1], cut(f.cum, c), ACT.Exp, scale=-KAPPA).then_inc(decay.sem, 1)
            act.activation(en[:, :, :], cut(f.cum, c), ACT.Exp, scale=KAPPA).then_inc(decay.sem, 1)
            for h in range(2):
                wait(act, vtok_mm, c, h)
                act.activation(quad(Vs, h), psum(4 * h + 3, CHUNK), ACT.Copy).then_inc(vtok.sem, 1)
            for lv in range(1, 6):
                for h in range(2):
                    wait(act, t_mm, c, 2 * (lv - 1) + h)
                    act.activation(quad(Tm, h), psum(4 * h, P), ACT.Copy).then_inc(t_ready.sem, 1)
            for h in range(2):
                wait(act, y_mm, c, 8 + h)
                for n, dst in enumerate((kt, bt)):
                    wait(act, tr_mm, c, 2 * h + n)
                    act.activation(quad(dst, h), psum(4 * h + n, P), ACT.Copy).then_inc(tr.sem, 1)
                wait(act, r_mm, c, h)
                act.activation(quad(R, h), psum(4 * h + 3, CHUNK), ACT.Copy).then_inc(r_ready.sem, 1)
            for h in range(2):
                wait(act, u_mm, c, h)
                act.activation(quad(U, h), psum(4 * h + 2, CHUNK), ACT.Copy).then_inc(u_ready.sem, 1)
            for h in range(2):
                wait(act, ot_mm, c, h)
                act.activation(cut_part(f.r, c, 0, P, 4 * h, 4 * h + 4), psum(4 * h + 2, CHUNK), ACT.Copy)\
                   .then_inc(o_out.sem, 1)

        chunks(act, body)

    def vector(dve):
        dve.memset(S[:, :, :], 0.0).then_inc(cleared.sem, 1)
        dve.memset(e[:, :, 0:1], 1.0).then_inc(cleared.sem, 1)
        dve.wait_ge(cleared.sem, cleared.of(5))

        def body(c):
            wait(dve, decay, c, 1)
            dve.tensor_tensor(ra[:, :, 0:CHUNK], cut(f.nkk, c), e[:, :, 0:CHUNK], ALU.mult)\
               .then_inc(stacked.sem, 1)
            dve.tensor_tensor(ra[:, :, CHUNK:P], cut(f.r, c), e[:, :, 1:CHUNK + 1], ALU.mult)\
               .then_inc(stacked.sem, 1)
            for src, dst in ((f.k, kbd), (f.kb, bbd)):
                for h in range(2):
                    dve.tensor_tensor(dst[rows(h), :, 64 * h:64 * h + 64], cut_part(src, c, 64 * h, 64 * h + 64),
                                      en[rows(h), :, :], ALU.mult).then_inc(keys.sem, 1)
            for h in range(2):
                for bank, st, outs in ((4 * h, pair_ab, ((L, "before"), (Arb, "upto"))),
                                       (4 * h + 1, pair_ak, ((Aak, "before"), (Ark, "upto")))):
                    wait(dve, st, c, h)
                    for n, (dst, mask) in enumerate(outs):
                        part = psum(bank, P)[:, :, 64 * n:64 * n + 64]
                        dve.tensor_tensor(quad(dst, h).rearrange("p q (a t) -> p q a t", a=2),
                                          part.unsqueeze(2).to_broadcast([P, 4, 2, CHUNK]),
                                          chip.k(mask).rearrange("p (a t) -> p a t", a=2).unsqueeze(1)
                                          .to_broadcast([P, 4, 2, CHUNK]),
                                          ALU.mult).then_inc(masked.sem, 1)
            for h in range(2):
                wait(dve, first_mm, c, h)
                eye = chip.ident[:, :].unsqueeze(1).to_broadcast([P, 4, P])
                dve.tensor_tensor(quad(X, h), psum(4 * h, P), eye, ALU.add).then_inc(first_x.sem, 1)
                dve.tensor_tensor(quad(Y, h), quad(Lm, h), eye, ALU.add).then_inc(first_y.sem, 1)
            for lv in range(1, 6):
                for h in range(2):
                    wait(dve, y_mm, c, 2 * (lv - 1) + h)
                    if lv < 5:
                        dve.tensor_tensor(quad(X, h), psum(4 * h + 1, P), quad(X, h), ALU.add)\
                           .then_inc(x_ready.sem, 1)
                    dve.tensor_tensor(quad(Y, h), psum(4 * h + 2, P), quad(Y, h), ALU.add)\
                       .then_inc(y_ready.sem, 1)
            for h in range(2):
                wait(dve, o_mm, c, h)
                for a in range(2):
                    dve.tensor_copy(ybd[rows(a), 4 * h:4 * h + 4, 64 * a:64 * a + 64],
                                    psum(4 * h + 1, CHUNK)[rows(a), :, :]).then_inc(o_diag.sem, 1)
                wait(dve, s_mm, c, h)
                dve.tensor_tensor(quad(S, h), psum(4 * h, CHUNK), quad(S, h), ALU.add).then_inc(s_sum.sem, 1)
                wait(dve, s_sum, c, h)
                dve.tensor_tensor(quad(S, h), quad(S, h),
                                  e[:, 4 * h:4 * h + 4, CHUNK:CHUNK + 1].to_broadcast([P, 4, CHUNK]),
                                  ALU.mult).then_inc(state.sem, 1)

        chunks(dve, body)

    def gpsimd(pool):
        for buf in (abd, rbd, kbd, bbd):
            pool.memset(buf[:, :, :], 0.0).then_inc(cleared.sem, 1)
        pool.wait_ge(cleared.sem, cleared.of(5))

        def body(c):
            wait_last(pool, s_mm, c, 1)
            if c == 0:
                pool.memset(vbd[:, :, :], 0.0).then_inc(vzero.sem, 1)
                pool.wait_ge(vzero.sem, vzero.of(0))
            for h in range(2):
                pool.tensor_copy(vbd[rows(h), :, 64 * h:64 * h + 64], cut_part(f.v, c, 64 * h, 64 * h + 64))\
                    .then_inc(vdiag.sem, 1)
                wait(pool, vdiag, c, h)
            wait(pool, stacked, c, 1)
            wait_last(pool, o_mm, c, 1)
            for n, dst in enumerate((abd, rbd)):
                for h in range(2):
                    pool.tensor_copy(dst[rows(h), :, 64 * h:64 * h + 64], ra[rows(h), :, 64 * n:64 * n + 64])\
                        .then_inc(diag.sem, 1)
                    wait(pool, diag, c, 2 * n + h)
            for lv in range(6):
                if lv == 0:
                    wait(pool, vtok_mm, c, 1)
                    wait(pool, masked, c, 7)
                elif lv == 1:
                    wait(pool, first_y, c, 1)
                else:
                    wait(pool, t_mm, c, 2 * (lv - 2) + 1)
                pool.tensor_tensor(Lm[:, :, :], L[:, :, :],
                                   chip.k("levels")[:, lv * P:(lv + 1) * P].unsqueeze(1).to_broadcast([P, KD, P]),
                                   ALU.mult).then_inc(level.sem, 1)

        for c in range(NC_):
            body(c)

    vzero = Step(chip, "ch_vzero", 1)
    return tensor, scalar, vector, gpsimd


def rwkv_output(chip):
    f = chip.rwkv
    sq = chip.keep("sq", [P, 2, T])
    rstd = chip.keep("gn_rstd", [P, 2, T])
    bv = chip.keep("bonus_v", [P, 2, T])
    head_cols = chip.keep("head_cols", [16, D])
    b_g, u_g = chip.take_blocks(1), chip.take_groups(KD)
    b_o, u_o = chip.take_blocks(4), chip.take_groups(4)
    z = f.k
    x_back, cols_ready = Load(chip), Load(chip)
    mean_mm, centred, sq_done = Step(chip, "rw_mean", KD), Step(chip, "rw_centred", KD), Step(chip, "rw_sq", KD)
    var_mm, root = Step(chip, "rw_var", KD), Step(chip, "rw_root", KD)
    gate_mm, bonus_mm, out = Step(chip, "rw_gate", KD), Step(chip, "rw_bonus_mm", KD), Step(chip, "rw_out", 4 * KD)
    gated = Step(chip, "rw_gated", KD)

    def tensor(pe):
        chip.wait_block(pe, b_g)
        w = chip.ring[:, b_g % SLOTS, :].rearrange("p (j n) -> p j n", j=2)

        def mean(n):
            if n >= 2:
                pe.wait_ge(centred.sem, centred.of(n - 2))
            pe.matmul(chip.bank[4 + n % 2][:, :], chip.k("block_ones"), f.r[:, n, :], start=True, stop=True)\
              .then_inc(mean_mm.sem, 1)

        def rest(n):
            pe.wait_ge(sq_done.sem, sq_done.of(n))
            if n >= 2:
                pe.wait_ge(root.sem, root.of(n - 2))
            pe.matmul(chip.bank[6 + n % 2][:, :], chip.k("block_ones"), sq[:, n % 2, :], start=True, stop=True)\
              .then_inc(var_mm.sem, 1)
            if n == 0:
                pe.wait_ge(cols_ready.sem, cols_ready.landed)
            chip.wait_pair(pe, u_g + n)
            pe.matmul(chip.pair(u_g + n)[0][:, :], w[:, 0, n * P:(n + 1) * P], f.sgl[:, 0, :],
                      start=True, stop=False)
            pe.matmul(chip.pair(u_g + n)[0][:, :], w[0:LORA_G - P, 1, n * P:(n + 1) * P],
                      f.sgl[0:LORA_G - P, 1, :], start=False, stop=True).then_inc(gate_mm.sem, 1)
            pe.matmul(chip.pair(u_g + n)[1][:, :], head_cols[:, n * P:(n + 1) * P], f.bsum[:, :],
                      start=True, stop=True).then_inc(bonus_mm.sem, 1)

        for n in range(KD + 1):
            if n < KD:
                mean(n)
            if n:
                rest(n - 1)
        pe.wait_ge(chip.gemm_done, 2 * b_g + 2)
        chip.pe_features(pe, b_o, u_o, 4, KD, lambda k: z[:, k, :],
                         before=lambda k: pe.wait_ge(gated.sem, gated.of(k)))

    def scalar(act):
        act.dma_start(head_cols[:, :], chip.io["head_cols"]).then_inc(cols_ready.sem, 16)
        act.dma_start(chip.x[:, :, :], chip.io["x"].rearrange("(k p) t -> p k t", p=P)).then_inc(x_back.sem, 16)
        for n in range(KD):
            act.wait_ge(centred.sem, centred.of(n))
            if n >= 2:
                act.wait_ge(var_mm.sem, var_mm.of(n - 2))
            act.activation(sq[:, n % 2, :], f.r[:, n, :], ACT.Square).then_inc(sq_done.sem, 1)
            act.wait_ge(var_mm.sem, var_mm.of(n))
            if n >= 2:
                act.wait_ge(out.sem, out.of(4 * (n - 2) + 1))
            act.activation(rstd[:, n % 2, :], chip.bank[6 + n % 2][:, :], ACT.Sqrt, bias=chip.gn_eps[:, :],
                           scale=1.0 / HEAD).then_inc(root.sem, 1)

    def vector(dve):
        def centre(n):
            dve.wait_ge(mean_mm.sem, mean_mm.of(n))
            dve.scalar_tensor_tensor(out=f.r[:, n, :], in0=chip.bank[4 + n % 2][:, :], scalar=-1.0 / HEAD,
                                     in1=f.r[:, n, :], op0=ALU.mult, op1=ALU.add).then_inc(centred.sem, 1)

        def finish(n):
            y, t = f.r[:, n, :], rstd[:, n % 2, :]
            dve.wait_ge(root.sem, root.of(n))
            dve.reciprocal(t, t).then_inc(out.sem, 1)
            dve.wait_ge(out.sem, out.of(4 * n))
            dve.scalar_tensor_tensor(out=y, in0=y, scalar=chip.v("gn_w")[:, n:n + 1], in1=t,
                                     op0=ALU.mult, op1=ALU.mult).then_inc(out.sem, 1)
            dve.wait_ge(bonus_mm.sem, bonus_mm.of(n))
            dve.tensor_tensor(bv[:, n % 2, :], chip.pair(u_g + n)[1][:, :], f.v[:, n, :], ALU.mult)\
               .then_inc(out.sem, 1)
            dve.wait_ge(out.sem, out.of(4 * n + 2))
            dve.scalar_tensor_tensor(out=y, in0=y, scalar=chip.v("gn_b")[:, n:n + 1], in1=bv[:, n % 2, :],
                                     op0=ALU.add, op1=ALU.add).then_inc(out.sem, 1)
            dve.wait_ge(out.sem, out.of(4 * n + 3))
            dve.tensor_tensor(z[:, n, :], chip.pair(u_g + n)[0][:, :], y, ALU.mult).then_inc(gated.sem, 1)
            dve.wait_ge(gated.sem, gated.of(n))
            dve.sem_inc(chip.pair_free[(u_g + n) % 2], 2)

        for n in range(KD + 1):
            if n < KD:
                centre(n)
            if n:
                finish(n - 1)
        dve.sem_inc(chip.gemm_done, 2)
        dve.wait_ge(x_back.sem, x_back.landed)
        residual(chip, dve, b_o, u_o, lambda n: chip.mod[:, 16 + n:17 + n])

    chip.floor = chip.base_floor
    return tensor, scalar, vector, None


def residual(chip, dve, b0, u0, gain):
    for n in range(KD):
        chip.wait_tile(dve, b0 + n // 2, n % 2)
        u = u0 + n // 2
        dve.scalar_tensor_tensor(out=chip.x[:, n, :], in0=chip.pair(u)[n % 2][:, :], scalar=gain(n),
                                 in1=chip.x[:, n, :], op0=ALU.mult, op1=ALU.add)\
           .then_inc(chip.pair_free[u % 2], 1)


def ffn(chip, layer):
    m = 48 * layer
    h = chip.keep("h", [P, KD, T])
    act_tile = chip.keep("silu_gate", [P, 2, T])
    hid = chip.keep("hidden", [P, KF, T])
    norm = Norm(chip, lambda k: chip.x[:, k, :], lambda k: h[:, k, :], KD,
                lambda k: chip.mod[:, m + 32 + k:m + 33 + k], lambda k: chip.mod[:, m + 24 + k:m + 25 + k])
    b0, u0 = chip.take_blocks(KF), chip.take_groups(KF)
    b1, u1 = chip.take_blocks(2 * KD), chip.take_groups(KD // 2)
    gated = Step(chip, "ffn_gated", KF)

    def tensor(pe):
        norm.tensor(pe)
        for k in range(KD):
            norm.wait(pe, k)
        chip.pe_features(pe, b0, u0, KF, KD, lambda k: h[:, k, :])
        pe.wait_ge(chip.pair_free[(u1 - 1) % 2], 2 * ((u1 - 1) // 2 + 1))
        pe.wait_ge(chip.pair_free[(u1 - 2) % 2], 2 * ((u1 - 2) // 2 + 1))
        chip.pe_long(pe, b1, u1, KD, 2, KF // 2, lambda k: hid[:, k, :])

    def scalar(act):
        norm.scalar(act)

        def gate(i, s):
            chip.wait_tile(act, b0 + s, 0, i)
            act.activation(act_tile[:, (u0 + s) % 2, :], chip.pair(u0 + s)[0][:, :], ACT.Silu)\
               .then_inc(gated.sem, 1)
        by_four(act, KF, gate)

    def vector(dve):
        norm.vector(dve)

        def up(i, s):
            dve.wait_ge(gated.sem, gated.of(s) + 4 * i)
            chip.wait_tile(dve, b0 + s, 1, i)
            dve.tensor_tensor(at(hid, 4 * i + s), one(act_tile[:, (u0 + s) % 2, :]),
                              one(chip.pair(u0 + s)[1][:, :]), ALU.mult)\
               .then_inc(chip.pair_free[(u0 + s) % 2], 2)
        by_four(dve, KF, up)
        for n in range(KD):
            dve.wait_ge(chip.gemm_done, 2 * (b1 + 2 * n + 2))
            dve.scalar_tensor_tensor(out=chip.x[:, n, :], in0=chip.pair(u1 + n // 2)[n % 2][:, :],
                                     scalar=chip.mod[:, m + 40 + n:m + 41 + n], in1=chip.x[:, n, :],
                                     op0=ALU.mult, op1=ALU.add)\
               .then_inc(chip.pair_free[(u1 + n // 2) % 2], 1)

    return tensor, scalar, vector, None




def mlstm(chip):
    m = 48
    H = ML_HEADS
    ST = T // P
    h = chip.keep("h", [P, KD, T])
    qk = chip.keep("qk", [P, KD, T])
    v = chip.keep("v_tok", [P, ST, D])
    og = chip.keep("o_gate", [P, KD, T])
    pad = chip.keep("conv_in", [P, 2, T + CONV_W - 1])
    conv = chip.keep("conv_out", [P, 2, T])
    rows = chip.keep("gate_rows", [H, 5, T])
    li, lf, ee, mm_, en_m = (rows[:, n, :] for n in range(5))
    gb = chip.keep("gate_bias", [H, 2])
    ones_row = chip.keep("ones_row", [H, T])
    ecol = chip.keep("e_col", [P, ST, H])
    m_all = chip.keep("m_all", [P, H, T])
    enm_all = chip.keep("exp_neg_m", [P, H, T])
    dd = chip.keep("weights", [P, ST, T])
    z = h
    norm = Norm(chip, lambda k: chip.x[:, k, :], lambda k: h[:, k, :], KD,
                lambda k: chip.mod[:, m + 8 + k:m + 9 + k], lambda k: chip.mod[:, m + k:m + k + 1])
    b_qk, u_qk = chip.take_blocks(4), chip.take_groups(4)
    b_g, u_g = chip.take_blocks(1), chip.take_groups(1)
    b_v, u_v = chip.take_blocks(4), chip.take_groups(4)
    b_o, u_o = chip.take_blocks(4), chip.take_groups(4)
    b_w, u_w = chip.take_blocks(4), chip.take_groups(4)
    padded, taps, qk_ready = Step(chip, "ml_padded", 2), Step(chip, "ml_taps", 4 * KD), Step(chip, "ml_qk", KD)
    og_ready = None
    gate = Step(chip, "ml_gate", 6)
    gate_v = Step(chip, "ml_gate_v", 4)
    ecol_mm, ecol_ready = Step(chip, "ml_ecol_mm", ST), Step(chip, "ml_ecol", ST)
    bc_mm, bc_ready = Step(chip, "ml_bc_mm", 2 * H), Step(chip, "ml_bc", 2 * H)
    s_mm = Step(chip, "ml_s_mm", H * ST)
    gap, ex, tri, wt = (Step(chip, "ml_" + n, H * ST) for n in ("gap", "exp", "tri", "weight"))
    nd_mm, fin, sq, ms_mm, root = Step(chip, "ml_nd", H), Step(chip, "ml_fin", 4 * H), Step(chip, "ml_sq", H), \
        Step(chip, "ml_ms", H), Step(chip, "ml_root", H)
    z_ready = Step(chip, "ml_z", H)

    def part(hd):
        return slice(64 * (hd % 2), 64 * (hd % 2) + 64)

    def tensor(pe):
        norm.tensor(pe)
        for k in range(KD):
            norm.wait(pe, k)
        chip.pe_features(pe, b_qk, u_qk, 4, KD, lambda k: h[:, k, :])
        chip.wait_block(pe, b_g)
        chip.wait_pair(pe, u_g)
        w = chip.ring[:, b_g % SLOTS, :].rearrange("p (k n) -> p k n", k=KD)
        for j in range(2):
            for k in range(KD):
                mm = pe.matmul(chip.pair(u_g)[j][0:H, :], w[:, k, j * H:(j + 1) * H], h[:, k, :],
                               start=(k == 0), stop=(k == KD - 1))
            mm.then_inc(chip.gemm_done, 1)
        chip.pe_tokens(pe, b_v, u_v, 4, KD, lambda k: h[:, k, :])
        chip.pe_features(pe, b_o, u_o, 4, KD, lambda k: h[:, k, :])
        pe.wait_ge(gate_v.sem, gate_v.of(3))
        for n in range(ST):
            pe.matmul(chip.bank[4][:, n * H:(n + 1) * H], ee[:, n * P:(n + 1) * P], chip.ident[0:H, 0:H],
                      start=True, stop=True).then_inc(ecol_mm.sem, 1)
        pe.wait_ge(gate.sem, gate.of(5))
        for hd in range(H):
            for n, row in enumerate((mm_, en_m)):
                c = 2 * hd + n
                if c >= 2:
                    pe.wait_ge(bc_ready.sem, bc_ready.of(c - 2))
                pe.matmul(chip.bank[5 + n][:, :], chip.ident[0:H, hd:hd + 1].to_broadcast([H, P]), row,
                          start=True, stop=True).then_inc(bc_mm.sem, 1)
        chip.wait_pair(pe, u_w)
        chip.wait_pair(pe, u_w + 1)
        pe.wait_ge(bc_ready.sem, bc_ready.of(2 * H - 1))
        pe.wait_ge(ecol_ready.sem, ecol_ready.of(0))
        pe.wait_ge(qk_ready.sem, qk_ready.of(KD - 1))

        def scores(hd):
            for i in range(ST):
                n = hd * ST + i
                if hd:
                    pe.wait_ge(wt.sem, wt.of(n - ST))
                pe.matmul(chip.bank[i][:, i * P:T], qk[part(hd), 4 + hd // 2, i * P:(i + 1) * P],
                          qk[part(hd), hd // 2, i * P:T], start=True, stop=True).then_inc(s_mm.sem, 1)

        def sums(hd):
            num, den = chip.bank[4 + 2 * (hd % 2)], chip.bank[5 + 2 * (hd % 2)]
            if hd >= 2:
                pe.wait_ge(z_ready.sem, z_ready.of(hd - 2))
            for i in range(ST):
                pe.wait_ge(wt.sem, wt.of(hd * ST + i))
                pe.matmul(num[:, i * P:T], v[:, i, hd * P:(hd + 1) * P], dd[:, i, i * P:T],
                          start=(i == 0), stop=(i == ST - 1))
                mm = pe.matmul(den[:, i * P:T], chip.ones[:, :], dd[:, i, i * P:T],
                               start=(i == 0), stop=(i == ST - 1))
            mm.then_inc(nd_mm.sem, 1)

        def mean_square(hd):
            pe.wait_ge(sq.sem, sq.of(hd))
            pe.matmul(chip.bank[5 + 2 * (hd % 2)][:, :], chip.ones[:, :], conv[:, hd % 2, :],
                      start=True, stop=True).then_inc(ms_mm.sem, 1)

        scores(0)
        for hd in range(H):
            sums(hd)
            if hd + 1 < H:
                scores(hd + 1)
            mean_square(hd)
        chip.pe_features(pe, b_w, u_w, 4, KD, lambda k: z[:, k, :],
                         before=lambda k: pe.wait_ge(z_ready.sem, z_ready.of(k)))

    def scalar(act):
        norm.scalar(act)
        for n in range(KD):
            chip.wait_tile(act, b_qk + n // 2, n % 2)
            if n >= 2:
                act.wait_ge(taps.sem, taps.of(4 * (n - 2) + 3))
            u = u_qk + n // 2
            if n == 0:
                act.wait_ge(padded.sem, padded.of(0))
            act.activation(pad[:, n % 2, CONV_W - 1:], chip.pair(u)[n % 2][:, :], ACT.Copy)\
               .then_inc(chip.pair_free[u % 2], 1)
            act.wait_ge(taps.sem, taps.of(4 * n + 3))
            act.activation(qk[:, n, :], conv[:, n % 2, :], ACT.Silu, bias=chip.v("conv_b")[:, n:n + 1])\
               .then_inc(qk_ready.sem, 1)
        act.activation(gb[:, :], chip.v("gate_b")[0:H, :], ACT.Copy, scale=1.0 / GATE_CAP).then_inc(gate.sem, 1)
        act.wait_ge(gate.sem, gate.of(0))
        for j, row in enumerate((li, lf)):
            chip.wait_tile(act, b_g, j)
            act.activation(row, chip.pair(u_g)[j][0:H, :], ACT.Tanh, bias=gb[:, j:j + 1],
                           scale=1.0 / GATE_CAP).then_inc(gate.sem, 1)
        act.wait_ge(gate.sem, gate.of(2))
        act.sem_inc(chip.pair_free[u_g % 2], 2)
        act.activation(lf, lf, ACT.Exp, scale=-GATE_CAP).then_inc(gate.sem, 1)
        act.wait_ge(gate.sem, gate.of(3))
        act.activation(lf, lf, ACT.Ln, bias=chip.ones[0:H, 0:1]).then_inc(gate.sem, 1)
        for s in range(4):
            for j in range(2):
                chip.wait_tile(act, b_v + s, j)
                act.activation(v[:, 2 * j:2 * j + 2, s * 2 * P:(s + 1) * 2 * P],
                               chip.pair(u_v + s)[j][:, :].rearrange("p (a n) -> p a n", a=2), ACT.Copy)\
                   .then_inc(chip.pair_free[(u_v + s) % 2], 1)
        act.wait_ge(gate_v.sem, gate_v.of(3))
        act.activation(en_m, li, ACT.Exp, scale=-1.0).then_inc(gate.sem, 1)
        for n in range(KD):
            chip.wait_tile(act, b_o + n // 2, n % 2)
            u = u_o + n // 2
            act.activation(og[:, n, :], chip.pair(u)[n % 2][:, :], ACT.Sigmoid).then_inc(chip.pair_free[u % 2], 1)
        for hd in range(H):
            for n, dst in enumerate((m_all, enm_all)):
                act.wait_ge(bc_mm.sem, bc_mm.of(2 * hd + n))
                act.activation(dst[:, hd, :], chip.bank[5 + n][:, :], ACT.Copy).then_inc(bc_ready.sem, 1)

        def finish(hd):
            act.wait_ge(fin.sem, fin.of(4 * hd + 2))
            if hd >= 2:
                act.wait_ge(ms_mm.sem, ms_mm.of(hd - 2))
            act.activation(conv[:, hd % 2, :], z[:, hd, :], ACT.Square).then_inc(sq.sem, 1)
            act.wait_ge(ms_mm.sem, ms_mm.of(hd))
            act.activation(enm_all[:, hd, :], chip.bank[5 + 2 * (hd % 2)][:, :], ACT.Sqrt,
                           bias=chip.eps[:, :], scale=1.0 / ML_V).then_inc(root.sem, 1)

        for hd in range(H):
            for i in range(ST):
                act.wait_ge(gap.sem, gap.of(hd * ST + i))
                act.activation(dd[:, i, i * P:T], dd[:, i, i * P:T], ACT.Exp, scale=-1.0).then_inc(ex.sem, 1)
            if hd:
                finish(hd - 1)
        finish(H - 1)

    def vector(dve):
        norm.vector(dve)
        dve.memset(pad[:, :, 0:CONV_W - 1], 0.0).then_inc(padded.sem, 1)
        dve.memset(ones_row[:, :], 1.0).then_inc(padded.sem, 1)
        for n in range(KD):
            u = u_qk + n // 2
            dve.wait_ge(chip.pair_free[u % 2], 2 * (u // 2) + n % 2 + 1)
            if n >= 2:
                dve.wait_ge(qk_ready.sem, qk_ready.of(n - 2))
            for j in range(CONV_W):
                w = chip.v("conv_w")[:, j * KD + n:j * KD + n + 1]
                src, dst = pad[:, n % 2, j:j + T], conv[:, n % 2, :]
                if j == 0:
                    dve.tensor_scalar(dst, src, w, None, ALU.mult).then_inc(taps.sem, 1)
                else:
                    dve.wait_ge(taps.sem, taps.of(4 * n + j - 1))
                    dve.scalar_tensor_tensor(out=dst, in0=src, scalar=w, in1=dst, op0=ALU.mult, op1=ALU.add)\
                       .then_inc(taps.sem, 1)
        dve.wait_ge(gate.sem, gate.of(4))
        dve.wait_ge(padded.sem, padded.of(1))
        dve.tensor_tensor_scan(mm_, ones_row[:, :], lf, 0.0, ALU.mult, ALU.subtract)\
           .then_inc(gate_v.sem, 1)
        dve.wait_ge(gate_v.sem, gate_v.of(0))
        dve.scalar_tensor_tensor(out=ee, in0=li, scalar=GATE_CAP, in1=mm_, op0=ALU.mult, op1=ALU.subtract)\
           .then_inc(gate_v.sem, 1)
        dve.tensor_copy(lf, mm_).then_inc(gate_v.sem, 1)
        dve.wait_ge(gate_v.sem, gate_v.of(2))
        dve.tensor_tensor_scan(mm_, ee, ee, 0.0, ALU.max, ALU.max).then_inc(gate_w.sem, 1)
        dve.wait_ge(gate_w.sem, gate_w.of(0))
        dve.tensor_tensor(li, lf, mm_, ALU.add).then_inc(gate_v.sem, 1)
        dve.wait_ge(ecol_mm.sem, ecol_mm.of(ST - 1))
        dve.tensor_copy(ecol[:, :, :], chip.bank[4][:, 0:ST * H].rearrange("p (a n) -> p a n", a=ST))\
           .then_inc(ecol_ready.sem, ST)

        def gaps(hd):
            if hd == 0:
                dve.wait_ge(ecol_ready.sem, ecol_ready.of(0))
            dve.wait_ge(bc_ready.sem, bc_ready.of(2 * hd))
            if hd:
                dve.wait_ge(nd_mm.sem, nd_mm.of(hd - 1))
            for i in range(ST):
                dve.tensor_scalar(dd[:, i, i * P:T], m_all[:, hd, i * P:T], ecol[:, i, hd:hd + 1], 0.0,
                                  ALU.subtract, ALU.max).then_inc(gap.sem, 1)

        def weights(hd):
            for i in range(ST):
                n = hd * ST + i
                dve.wait_ge(tri.sem, tri.of(n))
                dve.wait_ge(s_mm.sem, s_mm.of(n))
                dve.scalar_tensor_tensor(out=dd[:, i, i * P:T], in0=chip.bank[i][:, i * P:T],
                                         scalar=float(ML_QK) ** -0.5, in1=dd[:, i, i * P:T],
                                         op0=ALU.mult, op1=ALU.mult).then_inc(wt.sem, 1)

        def divide(hd):
            num, den = chip.bank[4 + 2 * (hd % 2)], chip.bank[5 + 2 * (hd % 2)]
            dve.wait_ge(nd_mm.sem, nd_mm.of(hd))
            dve.wait_ge(bc_ready.sem, bc_ready.of(2 * hd + 1))
            t = enm_all[:, hd, :]
            dve.scalar_tensor_tensor(out=t, in0=den[:, :], scalar=-1.0, in1=t, op0=ALU.mult, op1=ALU.max)\
               .then_inc(floor_.sem, 1)
            dve.wait_ge(floor_.sem, floor_.of(hd))
            dve.tensor_tensor(t, den[:, :], t, ALU.max).then_inc(fin.sem, 1)
            dve.wait_ge(fin.sem, fin.of(4 * hd))
            dve.reciprocal(t, t).then_inc(fin.sem, 1)
            dve.wait_ge(fin.sem, fin.of(4 * hd + 1))
            dve.tensor_tensor(z[:, hd, :], num[:, :], t, ALU.mult).then_inc(fin.sem, 1)

        def finish(hd):
            t = enm_all[:, hd, :]
            dve.wait_ge(root.sem, root.of(hd))
            dve.reciprocal(t, t).then_inc(fin.sem, 1)
            dve.wait_ge(fin.sem, fin.of(4 * hd + 3))
            dve.scalar_tensor_tensor(out=z[:, hd, :], in0=z[:, hd, :], scalar=chip.v("hn_w")[:, hd:hd + 1],
                                     in1=t, op0=ALU.mult, op1=ALU.mult).then_inc(zn.sem, 1)
            dve.wait_ge(zn.sem, zn.of(hd))
            dve.tensor_tensor(z[:, hd, :], z[:, hd, :], og[:, hd, :], ALU.mult).then_inc(z_ready.sem, 1)

        gaps(0)
        for hd in range(H):
            weights(hd)
            divide(hd)
            if hd + 1 < H:
                gaps(hd + 1)
            finish(hd)
        residual(chip, dve, b_w, u_w, lambda n: chip.mod[:, m + 16 + n:m + 17 + n])

    def gpsimd(pool):
        for n in range(H * ST):
            i = n % ST
            pool.wait_ge(ex.sem, ex.of(n))
            part_ = dd[:, i, i * P:(i + 1) * P]
            pool.affine_select(out=part_, in_=part_, compare_op=ALU.is_ge, fill=0.0, base=0,
                               pattern=[[1, P]], channel_multiplier=-1).then_inc(tri.sem, 1)

    floor_ = Step(chip, "ml_floor", H)
    gate_w, zn = Step(chip, "ml_running_max", 1), Step(chip, "ml_zn", H)
    return tensor, scalar, vector, gpsimd


def final_norm(chip):
    sq = chip.keep("sq", [P, KD, T])
    norm = Norm(chip, lambda k: chip.x[:, k, :], lambda k: chip.x[:, k, :], KD,
                lambda k: chip.v("final_w")[:, k:k + 1], squares=lambda k: sq[:, k, :])
    return norm.tensor, norm.scalar, norm.vector, None


TWO_PI_1 = 6.28125
TWO_PI_2 = 0.0019350051879882812
TWO_PI_3 = 2 * np.pi - TWO_PI_1 - TWO_PI_2
ROUND = 12582912.0


class Rope:

    def __init__(self, chip, column):
        self.chip, self.column = chip, column
        self.pos = chip.keep("positions", [P, T], I32)
        self.ang, self.turns = chip.keep("angle", [P, T]), chip.keep("turns", [P, T])
        self.cos, self.sin = chip.keep("cos", [P, T]), chip.keep("sin", [P, T])
        self.pos_ready = Load(chip)
        self.reduced = Step(chip, "rope_reduced", 8)
        self.sines = Step(chip, "rope_sines", 3)
        self.ready = Step(chip, "rope_ready", 1)

    def load(self, act):
        act.dma_start(self.pos[:, :], self.chip.io["pos"].to_broadcast([P, T])).then_inc(self.pos_ready.sem, 16)

    def scalar(self, act):
        r, s = self.reduced, self.sines
        act.wait_ge(r.sem, r.of(7))
        act.activation(self.sin[:, :], self.ang[:, :], ACT.Sin).then_inc(s.sem, 1)
        act.activation(self.turns[:, :], self.ang[:, :], ACT.Sin, scale=0.5).then_inc(s.sem, 1)
        act.wait_ge(s.sem, s.of(1))
        act.activation(self.turns[:, :], self.turns[:, :], ACT.Square).then_inc(s.sem, 1)

    def vector(self, dve):
        r, ang, n = self.reduced, self.ang[:, :], self.turns[:, :]
        freq = self.chip.k("inv_freq")[:, self.column:self.column + 1]
        dve.wait_ge(self.pos_ready.sem, self.pos_ready.landed)
        dve.tensor_copy(n, self.pos[:, :]).then_inc(r.sem, 1)
        dve.wait_ge(r.sem, r.of(0))
        dve.tensor_scalar(ang, n, freq, None, ALU.mult).then_inc(r.sem, 1)
        dve.wait_ge(r.sem, r.of(1))
        dve.tensor_scalar(n, ang, 1.0 / (2 * np.pi), ROUND, ALU.mult, ALU.add).then_inc(r.sem, 1)
        dve.wait_ge(r.sem, r.of(2))
        dve.tensor_scalar(n, n, ROUND, None, ALU.subtract).then_inc(r.sem, 1)
        for q, part in enumerate((TWO_PI_1, TWO_PI_2, TWO_PI_3)):
            dve.wait_ge(r.sem, r.of(3 + q))
            dve.scalar_tensor_tensor(out=ang, in0=n, scalar=-part, in1=ang, op0=ALU.mult, op1=ALU.add)\
               .then_inc(r.sem, 1)
        dve.wait_ge(r.sem, r.of(6))
        dve.tensor_scalar(ang, ang, 3.1415925, -3.1415925, ALU.min, ALU.max).then_inc(r.sem, 1)
        dve.wait_ge(self.sines.sem, self.sines.of(2))
        dve.tensor_scalar(self.cos[:, :], n, -2.0, 1.0, ALU.mult, ALU.add).then_inc(self.ready.sem, 1)

    def wait(self, eng):
        eng.wait_ge(self.ready.sem, self.ready.of(0))


class PostNorm:

    def __init__(self, chip, y, squares, layer, b0, u0):
        self.chip, self.y, self.b0, self.u0 = chip, y, b0, u0
        self.y_ready = Step(chip, "post_y", KD)
        self.added = Step(chip, "post_added", KD)
        self.norm = Norm(chip, lambda k: y[:, k, :], lambda k: y[:, k, :], KD,
                         lambda k: chip.v("post_g")[:, layer * KD + k:layer * KD + k + 1],
                         squares=lambda k: squares[:, k, :])

    def scalar(self, act):
        for n in range(KD):
            u = self.u0 + n // 2
            act.wait_ge(self.chip.gemm_done, 2 * (self.b0 + n + 1))
            act.activation(self.y[:, n, :], self.chip.pair(u)[n % 2][:, :], ACT.Copy)\
               .then_inc(self.y_ready.sem, 1)
            act.wait_ge(self.y_ready.sem, self.y_ready.of(n))
            act.sem_inc(self.chip.pair_free[u % 2], 1)
        self.norm.scalar(act)

    def vector(self, dve):
        self.norm.vector(dve)
        for n in range(KD):
            self.norm.wait(dve, n)
            dve.tensor_tensor(self.chip.x[:, n, :], self.chip.x[:, n, :], self.y[:, n, :], ALU.add)\
               .then_inc(self.added.sem, 1)


def retention(chip):
    ST, RH = T // P, RET_HEADS
    VT = RET_V // P
    h = chip.keep("h", [P, KD, T])
    q, k = chip.keep("q", [P, KD, T]), chip.keep("k", [P, KD, T])
    v = chip.keep("v_tok", [P, ST, RET_HEADS * RET_V])
    sg = chip.keep("silu_gate", [P, 2 * KD, T])
    fall = chip.keep("decay", [P, RH, T])
    rope = Rope(chip, 0)
    turn = chip.keep("turned", [P, 4, T])
    rstd = rope.ang
    dd, sq = h[:, 0:ST, :], h[:, ST:2 * ST, :]
    norm = Norm(chip, lambda n: chip.x[:, n, :], lambda n: h[:, n, :], KD,
                lambda n: chip.v("pre_g")[:, n:n + 1])
    b_qk, u_qk = chip.take_blocks(8), chip.take_groups(8)
    b_v, u_v = chip.take_blocks(8), chip.take_groups(8)
    b_g, u_g = chip.take_blocks(8), chip.take_groups(8)
    b_o, u_o = chip.take_blocks(8), chip.take_groups(4)
    fall_ready = Load(chip)
    turned, roped = Step(chip, "ret_turned", 4 * 8), Step(chip, "ret_roped", 16)
    silu = Step(chip, "ret_silu", 16)
    s_mm, wt = Step(chip, "ret_scores", RH * ST), Step(chip, "ret_weight", RH * ST)
    o_mm, sq_done, ms_mm = Step(chip, "ret_o", RH * VT), Step(chip, "ret_sq", RH * VT), Step(chip, "ret_ms", RH)
    root, recip = Step(chip, "ret_root", RH), Step(chip, "ret_rstd", RH)
    scaled, z_ready = Step(chip, "ret_scaled", RH * VT), Step(chip, "ret_z", RH * VT)
    post = PostNorm(chip, q, k, 0, b_o, u_o)

    def tensor(pe):
        norm.tensor(pe)
        for n in range(KD):
            norm.wait(pe, n)
        chip.pe_features(pe, b_qk, u_qk, 8, KD, lambda n: h[:, n, :])
        chip.pe_tokens(pe, b_v, u_v, 8, KD, lambda n: h[:, n, :])
        chip.pe_features(pe, b_g, u_g, 8, KD, lambda n: h[:, n, :])
        chip.wait_pair(pe, u_o)
        chip.wait_pair(pe, u_o + 1)
        pe.wait_ge(roped.sem, roped.of(15))

        def scores(hd):
            for i in range(ST):
                n = hd * ST + i
                if n >= 2:
                    pe.wait_ge(wt.sem, wt.of(n - 2))
                for a in range(2):
                    mm = pe.matmul(chip.bank[i % 2][:, i * P:T], k[:, 2 * hd + a, i * P:(i + 1) * P],
                                   q[:, 2 * hd + a, i * P:T], start=(a == 0), stop=(a == 1))
                mm.then_inc(s_mm.sem, 1)

        def outs(hd):
            pe.wait_ge(wt.sem, wt.of(hd * ST + ST - 1))
            for j in range(VT):
                if hd:
                    pe.wait_ge(scaled.sem, scaled.of((hd - 1) * VT + j))
                for i in range(ST):
                    col = hd * RET_V + j * P
                    mm = pe.matmul(chip.bank[2 + j][:, i * P:T], v[:, i, col:col + P], dd[:, i, i * P:T],
                                   start=(i == 0), stop=(i == ST - 1))
                mm.then_inc(o_mm.sem, 1)

        def mean_square(hd):
            for j in range(VT):
                pe.wait_ge(sq_done.sem, sq_done.of(hd * VT + j))
                mm = pe.matmul(chip.bank[6][:, :], chip.ones[:, :], sq[:, j, :],
                               start=(j == 0), stop=(j == VT - 1))
            mm.then_inc(ms_mm.sem, 1)

        for hd in range(RH):
            scores(hd)
            outs(hd)
            mean_square(hd)
        pe.wait_ge(z_ready.sem, z_ready.of(RH * VT - 1))
        chip.pe_long(pe, b_o, u_o, KD, 1, 16, lambda n: sg[:, n, :])
        post.norm.tensor(pe)

    def scalar(act):
        rope.load(act)
        act.dma_start(fall[:, :, :], chip.io["ret_decay"].rearrange("p (h t) -> p h t", h=RH))\
           .then_inc(fall_ready.sem, 16)
        norm.scalar(act)
        rope.scalar(act)

        def v_copy(i, s):
            for j in range(2):
                chip.wait_tile(act, b_v + s, j, i)
                act.activation(v[:, 2 * j:2 * j + 2, (4 * i + s) * 2 * P:(4 * i + s + 1) * 2 * P],
                               chip.pair(u_v + s)[j][:, :].rearrange("p (a n) -> p a n", a=2), ACT.Copy)\
                   .then_inc(chip.pair_free[(u_v + s) % 2], 1)
        for n in range(8):
            v_copy(n // 4, n % 4)
        for n in range(16):
            chip.wait_tile(act, b_g + n // 2, n % 2)
            u = u_g + n // 2
            act.activation(sg[:, n, :], chip.pair(u)[n % 2][:, :], ACT.Silu).then_inc(silu.sem, 1)
            act.wait_ge(silu.sem, silu.of(n))
            act.sem_inc(chip.pair_free[u % 2], 1)
        for hd in range(RH):
            for j in range(VT):
                n = hd * VT + j
                act.wait_ge(o_mm.sem, o_mm.of(n))
                if hd:
                    act.wait_ge(ms_mm.sem, ms_mm.of(hd - 1))
                act.activation(sq[:, j, :], chip.bank[2 + j][:, :], ACT.Square).then_inc(sq_done.sem, 1)
            act.wait_ge(ms_mm.sem, ms_mm.of(hd))
            if hd:
                act.wait_ge(scaled.sem, scaled.of(hd * VT - 1))
            act.activation(rstd[:, :], chip.bank[6][:, :], ACT.Sqrt, bias=chip.eps[:, :],
                           scale=1.0 / RET_V).then_inc(root.sem, 1)
        post.scalar(act)

    def vector(dve):
        norm.vector(dve)
        rope.vector(dve)
        rope.wait(dve)
        for n in range(8):
            u = u_qk + n
            x1, x2 = chip.pair(u)[0][:, :], chip.pair(u)[1][:, :]
            dst = (q if n < 4 else k)
            chip.wait_tile(dve, b_qk + n, 1)
            if n:
                dve.wait_ge(roped.sem, roped.of(2 * n - 1))
            for m, (a, b) in enumerate(((x1, rope.cos), (x2, rope.sin), (x2, rope.cos), (x1, rope.sin))):
                dve.tensor_tensor(turn[:, m, :], a, b[:, :], ALU.mult).then_inc(turned.sem, 1)
            dve.wait_ge(turned.sem, turned.of(4 * n + 3))
            dve.sem_inc(chip.pair_free[u % 2], 2)
            dve.tensor_tensor(dst[:, 2 * (n % 4), :], turn[:, 0, :], turn[:, 1, :], ALU.subtract)\
               .then_inc(roped.sem, 1)
            dve.tensor_tensor(dst[:, 2 * (n % 4) + 1, :], turn[:, 2, :], turn[:, 3, :], ALU.add)\
               .then_inc(roped.sem, 1)
        dve.wait_ge(fall_ready.sem, fall_ready.landed)
        dve.wait_ge(silu.sem, silu.of(15))

        def weights(hd):
            for i in range(ST):
                n = hd * ST + i
                dve.wait_ge(s_mm.sem, s_mm.of(n))
                if hd and i == 0:
                    dve.wait_ge(o_mm.sem, o_mm.of(hd * VT - 1))
                dve.scalar_tensor_tensor(out=dd[:, i, i * P:T], in0=chip.bank[i % 2][:, i * P:T],
                                         scalar=float(RET_QK) ** -0.5, in1=fall[:, hd, 0:T - i * P],
                                         op0=ALU.mult, op1=ALU.mult).then_inc(wt.sem, 1)

        def finish(hd):
            dve.wait_ge(root.sem, root.of(hd))
            dve.reciprocal(rstd[:, :], rstd[:, :]).then_inc(recip.sem, 1)
            dve.wait_ge(recip.sem, recip.of(hd))
            for j in range(VT):
                n = hd * VT + j
                dve.scalar_tensor_tensor(out=turn[:, j, :], in0=chip.bank[2 + j][:, :],
                                         scalar=chip.v("ret_gn")[:, n:n + 1], in1=rstd[:, :],
                                         op0=ALU.mult, op1=ALU.mult).then_inc(scaled.sem, 1)
                dve.wait_ge(scaled.sem, scaled.of(n))
                dve.tensor_tensor(sg[:, n, :], sg[:, n, :], turn[:, j, :], ALU.mult).then_inc(z_ready.sem, 1)

        for hd in range(RH):
            weights(hd)
            finish(hd)
        post.vector(dve)

    return tensor, scalar, vector, None


def ple(chip, layer):
    p_in = chip.keep("ple_in", [P, 2, T])
    pp = chip.keep("ple_proj", [P, KD, T])
    sig = chip.keep("ple_gate", [P, 2, T])
    b_p, u_p = chip.take_blocks(1), chip.take_groups(4)
    b_g, u_g = chip.take_blocks(4), chip.take_groups(4)
    loaded = Load(chip)
    proj, copied, gate = Step(chip, "ple_proj_mm", KD - 1), Step(chip, "ple_copied", KD), Step(chip, "ple_gate", KD)
    prod, added = Step(chip, "ple_product", KD), Step(chip, "ple_added", KD)

    def tensor(pe):
        pe.wait_ge(loaded.sem, loaded.landed)
        chip.wait_block(pe, b_p)
        w = chip.ring[:, b_p % SLOTS, :].rearrange("p (k n) -> p k n", k=2)
        for n in range(KD):
            if n % 2 == 0:
                chip.wait_pair(pe, u_p + n // 2)
            for k in range(2):
                mm = pe.matmul(chip.pair(u_p + n // 2)[n % 2][:, :], w[:, k, n * P:(n + 1) * P], p_in[:, k, :],
                               start=(k == 0), stop=(k == 1))
            if n < KD - 1:
                mm.then_inc(proj.sem, 1)
        mm.then_inc(chip.gemm_done, 2)
        chip.pe_features(pe, b_g, u_g, 4, KD, lambda k: chip.x[:, k, :])

    def scalar(act):
        act.dma_start(p_in[:, :, :], chip.io["p"][layer].rearrange("(k p) t -> p k t", p=P))\
           .then_inc(loaded.sem, 16)
        for n in range(KD):
            if n < KD - 1:
                act.wait_ge(proj.sem, proj.of(n))
            else:
                act.wait_ge(chip.gemm_done, 2 * b_p + 2)
            u = u_p + n // 2
            act.activation(pp[:, n, :], chip.pair(u)[n % 2][:, :], ACT.Copy).then_inc(copied.sem, 1)
            act.wait_ge(copied.sem, copied.of(n))
            act.sem_inc(chip.pair_free[u % 2], 1)
        for n in range(KD):
            chip.wait_tile(act, b_g + n // 2, n % 2)
            if n >= 2:
                act.wait_ge(prod.sem, prod.of(n - 2))
            u = u_g + n // 2
            act.activation(sig[:, n % 2, :], chip.pair(u)[n % 2][:, :], ACT.Sigmoid).then_inc(gate.sem, 1)
            act.wait_ge(gate.sem, gate.of(n))
            act.sem_inc(chip.pair_free[u % 2], 1)

    def vector(dve):
        for n in range(KD):
            dve.wait_ge(gate.sem, gate.of(n))
            dve.tensor_tensor(pp[:, n, :], pp[:, n, :], sig[:, n % 2, :], ALU.mult).then_inc(prod.sem, 1)
        dve.wait_ge(prod.sem, prod.of(KD - 1))
        for n in range(KD):
            dve.tensor_tensor(chip.x[:, n, :], chip.x[:, n, :], pp[:, n, :], ALU.add).then_inc(added.sem, 1)

    return tensor, scalar, vector, None


def mla(chip):
    ST, H = T // P, MLA_HEADS
    SCALE = float(NOPE + ROPE) ** -0.5
    QT, CT = Q_LORA // P, KV_LORA // P
    h = chip.keep("h", [P, KD, T])
    cq = chip.keep("c_q", [P, QT, T])
    ckv = chip.keep("c_kv", [P, CT, T])
    kz = chip.keep("k_rope", [P, 2, T])
    qn, qr = chip.keep("q_nope", [P, 4, T]), chip.keep("q_rope", [P, 2, T])
    kn, v = chip.keep("k_nope", [P, 4, T]), chip.keep("v_tok", [P, ST, 4 * P])
    o = chip.keep("o", [P, H, T])
    rope = Rope(chip, 1)
    turn = chip.keep("turned", [P, 4, T])
    pr = chip.keep("probs", [P, ST, T])
    pt = chip.keep("probs_t", [P, ST, T])
    small = chip.keep("softmax_cols", [P, 2, 4 * ST])
    sg = chip.keep("silu_gate", [P, 2, T])
    norm = Norm(chip, lambda n: chip.x[:, n, :], lambda n: h[:, n, :], KD,
                lambda n: chip.v("pre_g")[:, KD + n:KD + n + 1])
    q_norm = Norm(chip, lambda n: cq[:, n, :], lambda n: cq[:, n, :], QT,
                  lambda n: chip.v("q_g")[:, n:n + 1], squares=lambda n: o[:, n, :], rstd=norm.rstd)
    kv_norm = Norm(chip, lambda n: ckv[:, n, :], lambda n: ckv[:, n, :], CT,
                   lambda n: chip.v("kv_g")[:, n:n + 1], squares=lambda n: o[:, QT + n, :], rstd=norm.rstd, bank=5)
    b_c, u_c = chip.take_blocks(4), chip.take_groups(4)
    b_r, u_r = chip.take_blocks(1), chip.take_groups(1)
    quarters = [(chip.take_blocks(4), chip.take_groups(7)) for _ in range(4)]
    b_g, u_g = chip.take_blocks(8), chip.take_groups(8)
    b_o, u_o = chip.take_blocks(8), chip.take_groups(4)
    lat = Step(chip, "mla_latent", QT + CT)
    zeroed, k_rope = Step(chip, "mla_zeroed", 1), Step(chip, "mla_k_rope", 4)
    turned = Step(chip, "mla_turned", 4 * 5)
    q_rope = Step(chip, "mla_q_rope", 8 * 4)
    raised = Step(chip, "mla_raised", 4 * 10)
    up_mm = Step(chip, "mla_up_mm", 4 * 7)
    s_mm = Step(chip, "mla_scores", H * ST)
    masked, top, negated = (Step(chip, "mla_" + n, H * ST) for n in ("masked", "max", "neg_max"))
    ex, inv, soft = (Step(chip, "mla_" + n, H * ST) for n in ("exp", "inverse", "softmax"))
    t_mm, t_copy = Step(chip, "mla_t_mm", H * ST), Step(chip, "mla_t_copy", H * ST)
    o_mm, o_copy = Step(chip, "mla_o_mm", H), Step(chip, "mla_o_copy", H)
    silu, z_ready = Step(chip, "mla_silu", H), Step(chip, "mla_z", H)
    post = PostNorm(chip, h, cq_and_more(chip, pr, pt), 1, b_o, u_o)

    def tensor(pe):
        norm.tensor(pe)
        for n in range(KD):
            norm.wait(pe, n)
        chip.pe_features(pe, b_c, u_c, 4, KD, lambda n: h[:, n, :])
        chip.pe_features(pe, b_r, u_r, 1, KD, lambda n: h[:, n, :])
        q_norm.tensor(pe)
        kv_norm.tensor(pe)
        q_norm.wait(pe, QT - 1)
        kv_norm.wait(pe, CT - 1)
        for qt in range(4):
            b, u = quarters[qt]
            chip.pe_features(pe, b, u, 3, QT, lambda n: cq[:, n, :])
            chip.wait_block(pe, b + 3)
            w = chip.ring[:, (b + 3) % SLOTS, :].rearrange("p (k n) -> p k n", k=CT)
            for n in range(8):
                g = u + 3 + n // 2
                if n % 2 == 0:
                    chip.wait_pair(pe, g)
                out = chip.pair(g)[n % 2]
                for c in range(CT):
                    if n < 4:
                        mm = pe.matmul(out[:, :], w[:, c, n * P:(n + 1) * P], ckv[:, c, :],
                                       start=(c == 0), stop=(c == CT - 1))
                    else:
                        mm = pe.matmul(out[:, :], ckv[:, c, (n - 4) * P:(n - 3) * P], w[:, c, 4 * P:8 * P],
                                       start=(c == 0), stop=(c == CT - 1))
                if n < 7:
                    mm.then_inc(up_mm.sem, 1)
            mm.then_inc(chip.gemm_done, 2)
            pe.wait_ge(raised.sem, raised.of(10 * qt + 9))
            pe.wait_ge(q_rope.sem, q_rope.of(8 * qt + 7))
            pe.wait_ge(k_rope.sem, k_rope.of(3))

            def scores(hd):
                a = hd % 4
                for j in range(ST):
                    n = hd * ST + j
                    if hd:
                        pe.wait_ge(ex.sem, ex.of(n - ST))
                    out = chip.bank[4 + j][:, 0:(j + 1) * P]
                    pe.matmul(out, qn[:, a, j * P:(j + 1) * P], kn[:, a, 0:(j + 1) * P], start=True, stop=False)
                    pe.matmul(out, qr[:, a // 2, j * P:(j + 1) * P], kz[:, a % 2, 0:(j + 1) * P],
                              start=False, stop=True).then_inc(s_mm.sem, 1)

            def values(hd):
                for i in range(ST):
                    n = hd * ST + i
                    if n >= 2:
                        pe.wait_ge(t_copy.sem, t_copy.of(n - 2))
                    for j in range(i, ST):
                        if i == 0:
                            pe.wait_ge(soft.sem, soft.of(hd * ST + j))
                        mm = pe.matmul(chip.bank[i % 2][:, j * P:(j + 1) * P], pr[:, j, i * P:(i + 1) * P],
                                       chip.ident[:, :], start=True, stop=True)
                    mm.then_inc(t_mm.sem, 1)
                if hd >= 2:
                    pe.wait_ge(o_copy.sem, o_copy.of(hd - 2))
                for i in range(ST):
                    pe.wait_ge(t_copy.sem, t_copy.of(hd * ST + i))
                    mm = pe.matmul(chip.bank[2 + hd % 2][:, i * P:T], v[:, i, (hd % 4) * P:(hd % 4 + 1) * P],
                                   pt[:, i, i * P:T], start=(i == 0), stop=(i == ST - 1))
                mm.then_inc(o_mm.sem, 1)

            scores(4 * qt)
            for a in range(4):
                if a < 3:
                    scores(4 * qt + a + 1)
                values(4 * qt + a)
            pe.wait_ge(o_copy.sem, o_copy.of(4 * qt + 3))
        chip.pe_features(pe, b_g, u_g, 8, KD, lambda n: h[:, n, :])
        pe.wait_ge(z_ready.sem, z_ready.of(H - 1))
        chip.pe_long(pe, b_o, u_o, KD, 1, 16, lambda n: o[:, n, :])
        post.norm.tensor(pe)

    def scalar(act):
        rope.load(act)
        norm.scalar(act)
        rope.scalar(act)
        for n in range(QT + CT):
            chip.wait_tile(act, b_c + n // 2, n % 2)
            u = u_c + n // 2
            dst = cq[:, n, :] if n < QT else ckv[:, n - QT, :]
            act.activation(dst, chip.pair(u)[n % 2][:, :], ACT.Copy).then_inc(lat.sem, 1)
            act.wait_ge(lat.sem, lat.of(n))
            act.sem_inc(chip.pair_free[u % 2], 1)
        q_norm.scalar(act)
        q_norm.wait(act, QT - 1)
        kv_norm.scalar(act)
        for qt in range(4):
            b, u = quarters[qt]
            if qt:
                act.wait_ge(o_mm.sem, o_mm.of(4 * qt - 1))
            for n in range(4):
                g = u + n // 2
                chip.wait_tile(act, b + n // 2, n % 2)
                act.activation(qn[:, n, :], chip.pair(g)[n % 2][:, :], ACT.Copy).then_inc(raised.sem, 1)
                act.wait_ge(raised.sem, raised.of(10 * qt + n))
                act.sem_inc(chip.pair_free[g % 2], 1)
            for n in range(8):
                g = u + 3 + n // 2
                if n < 7:
                    act.wait_ge(up_mm.sem, up_mm.of(7 * qt + n))
                else:
                    act.wait_ge(chip.gemm_done, 2 * (b + 3) + 2)
                dst = kn[:, n, :] if n < 4 else v[:, n - 4, :]
                ins = act.activation(dst, chip.pair(g)[n % 2][:, :], ACT.Copy)
                ins.then_inc(raised.sem, 1) if n != 3 and n != 4 else ins.then_inc(mid.sem, 1)
                act.wait_ge(raised.sem, raised.of(10 * qt + 4 + n - (2 if n > 4 else 0))) if n not in (3, 4) \
                    else act.wait_ge(mid.sem, mid.of(2 * qt + n - 3))
                act.sem_inc(chip.pair_free[g % 2], 1)
            for a in range(5):
                if a < 4:
                    hd = 4 * qt + a
                    for j in range(ST):
                        n = hd * ST + j
                        act.wait_ge(negated.sem, negated.of(n))
                        if hd:
                            act.wait_ge(t_mm.sem, t_mm.of(hd * ST - 1))
                        w = (j + 1) * P
                        act.activation(pr[:, j, 0:w], chip.bank[4 + j][:, 0:w], ACT.Exp,
                                       bias=small[:, 0, 4 * (hd % 4) + j:4 * (hd % 4) + j + 1], scale=SCALE,
                                       accum_out=small[:, 1, 4 * (hd % 4) + j:4 * (hd % 4) + j + 1])\
                           .then_inc(ex.sem, 1)
                    for i in range(ST):
                        n = hd * ST + i
                        act.wait_ge(t_mm.sem, t_mm.of(n))
                        if hd:
                            act.wait_ge(o_mm.sem, o_mm.of(hd - 1))
                        act.activation(pt[:, i, i * P:T], chip.bank[i % 2][:, i * P:T], ACT.Copy)\
                           .then_inc(t_copy.sem, 1)
                if a:
                    hd = 4 * qt + a - 1
                    act.wait_ge(o_mm.sem, o_mm.of(hd))
                    act.activation(o[:, hd, :], chip.bank[2 + hd % 2][:, :], ACT.Copy).then_inc(o_copy.sem, 1)
        for n in range(H):
            chip.wait_tile(act, b_g + n // 2, n % 2)
            if n >= 2:
                act.wait_ge(z_ready.sem, z_ready.of(n - 2))
            u = u_g + n // 2
            act.activation(sg[:, n % 2, :], chip.pair(u)[n % 2][:, :], ACT.Silu).then_inc(silu.sem, 1)
            act.wait_ge(silu.sem, silu.of(n))
            act.sem_inc(chip.pair_free[u % 2], 1)
        post.scalar(act)

    def vector(dve):
        norm.vector(dve)
        rope.vector(dve)
        rope.wait(dve)
        dve.memset(kz[:, :, :], 0.0).then_inc(zeroed.sem, 1)

        def turn_pair(n, x1, x2):
            for m, (a, b) in enumerate(((x1, rope.cos), (x2, rope.sin), (x2, rope.cos), (x1, rope.sin))):
                dve.tensor_tensor(turn[:, m, :], a[:, :], b[:, :], ALU.mult).then_inc(turned.sem, 1)
            dve.wait_ge(turned.sem, turned.of(4 * n + 3))

        chip.wait_tile(dve, b_r, 1)
        turn_pair(0, *chip.pair(u_r))
        dve.sem_inc(chip.pair_free[u_r % 2], 2)
        dve.wait_ge(zeroed.sem, zeroed.of(0))
        for g in range(4):
            rows = slice(32 * g, 32 * g + 32)
            a = 2 * (g % 2)
            dve.tensor_tensor(kz[rows, g // 2, :], turn[rows, a, :], turn[rows, a + 1, :],
                              ALU.add if g % 2 else ALU.subtract).then_inc(k_rope.sem, 1)
        q_norm.vector(dve)
        kv_norm.vector(dve)
        for qt in range(4):
            b, u = quarters[qt]
            chip.wait_tile(dve, b + 2, 1)
            dve.wait_ge(k_rope.sem, k_rope.of(3)) if qt == 0 else dve.wait_ge(q_rope.sem, q_rope.of(8 * qt - 1))
            turn_pair(qt + 1, *chip.pair(u + 2))
            dve.sem_inc(chip.pair_free[(u + 2) % 2], 2)
            for g in range(4):
                rows = slice(32 * g, 32 * g + 32)
                for half in range(2):
                    at_ = 64 * (g % 2) + 32 * half
                    dve.tensor_tensor(qr[at_:at_ + 32, g // 2, :], turn[rows, 2 * half, :],
                                      turn[rows, 2 * half + 1, :], ALU.add if half else ALU.subtract)\
                       .then_inc(q_rope.sem, 1)
            def maxima(hd):
                for j in range(ST):
                    n = hd * ST + j
                    col = 4 * (hd % 4) + j
                    w = (j + 1) * P
                    s = chip.bank[4 + j]
                    dve.wait_ge(s_mm.sem, s_mm.of(n))
                    dve.tensor_tensor(s[:, j * P:w], s[:, j * P:w], chip.k("later"), ALU.add)\
                       .then_inc(masked.sem, 1)
                    dve.wait_ge(masked.sem, masked.of(n))
                    dve.reduce_max(small[:, 0, col:col + 1], s[:, 0:w], AX_X).then_inc(top.sem, 1)
                    dve.wait_ge(top.sem, top.of(n))
                    dve.tensor_scalar(small[:, 0, col:col + 1], small[:, 0, col:col + 1], -SCALE, None, ALU.mult)\
                       .then_inc(negated.sem, 1)

            def normalise(hd):
                for j in range(ST):
                    n = hd * ST + j
                    col = 4 * (hd % 4) + j
                    w = (j + 1) * P
                    s1 = small[:, 1, col:col + 1]
                    dve.wait_ge(ex.sem, ex.of(n))
                    dve.reciprocal(s1, s1).then_inc(inv.sem, 1)
                    dve.wait_ge(inv.sem, inv.of(n))
                    dve.tensor_scalar(pr[:, j, 0:w], pr[:, j, 0:w], s1, None, ALU.mult).then_inc(soft.sem, 1)

            for a in range(4):
                maxima(4 * qt + a)
                normalise(4 * qt + a)
        for n in range(H):
            dve.wait_ge(silu.sem, silu.of(n))
            if n == 0:
                dve.wait_ge(o_copy.sem, o_copy.of(H - 1))
            dve.tensor_tensor(o[:, n, :], o[:, n, :], sg[:, n % 2, :], ALU.mult).then_inc(z_ready.sem, 1)
        post.vector(dve)

    mid = Step(chip, "mla_raised_mid", 8)
    return tensor, scalar, vector, None


def cq_and_more(chip, a, b):
    return Joined(a, b)


class Joined:
    def __init__(self, a, b):
        self.a, self.b = a, b

    def __getitem__(self, key):
        p, n, t = key
        return self.a[p, n, t] if n < 4 else self.b[p, n - 4, t]


def block_trunk(nc, io, phases):
    with ExitStack() as ctx:
        chip = Chip(nc, ctx, io)
        const_ready, vec_ready = chip.sem("const_ready"), chip.sem("vec_ready")
        phase_done, out_done = chip.sem("phase_done"), chip.sem("out_done")
        programs = []
        for phase in phases:
            chip.begin_phase()
            programs.append(phase(chip))
        n_blocks = chip.blocks
        assert n_blocks == io["stream"].shape[0], (n_blocks, io["stream"].shape)

        def between(eng, n):
            if n:
                eng.wait_ge(phase_done, 4 * n)
            else:
                eng.wait_ge(const_ready, CONSTS)
                eng.wait_ge(vec_ready, 16 * 3)

        block = ctx.enter_context(nc.Block())

        @block.sync
        def _(sp):
            sp.dma_start(chip.vec[:, :], io["vec"]).then_inc(vec_ready, 16)
            sp.dma_start(chip.const[:, :], io["const"]).then_inc(vec_ready, 16)
            sp.dma_start(chip.x[:, :, :], io["x"].rearrange("(k p) t -> p k t", p=P)).then_inc(vec_ready, 16)

            def load(i, s):
                if isinstance(i, int):
                    if i:
                        sp.wait_ge(chip.gemm_done, 8 * i + 2 * s - 6)
                    src = io["stream"][4 * i + s:4 * i + s + 1, :, :]
                else:
                    sp.wait_ge(chip.gemm_done, 8 * i + 2 * s - 6)
                    src = io["stream"][bass.ds(4 * i + s, 1), :, :]
                sp.dma_start(chip.ring[:, s, :], src.rearrange("a p n -> p (a n)")).then_inc(chip.w_full[s], 16)

            for s in range(min(SLOTS, n_blocks)):
                load(0, s)
            if n_blocks // 4 > 2:
                with sp.Fori(1, n_blocks // 4) as i:
                    for s in range(4):
                        load(i, s)
            elif n_blocks // 4 == 2:
                for s in range(4):
                    load(1, s)
            for s in range(n_blocks % 4 if n_blocks > 4 else 0):
                load(n_blocks // 4, s)
            sp.wait_ge(phase_done, 4 * len(programs))
            sp.dma_start(io["y"].rearrange("(k p) t -> p k t", p=P), chip.x[:, :, :]).then_inc(out_done, 16)
            sp.wait_ge(out_done, 16)

        @block.tensor
        def _(pe):
            for n, (tensor, _, _, _) in enumerate(programs):
                between(pe, n)
                tensor(pe)
                pe.drain().then_inc(phase_done, 1)

        @block.scalar
        def _(act):
            for n, (_, scalar, _, _) in enumerate(programs):
                between(act, n)
                scalar(act)
                act.drain().then_inc(phase_done, 1)

        @block.vector
        def _(dve):
            for pair in chip.pair_free:
                dve.sem_inc(pair, 2)
            dve.memset(chip.ones[:, :], 1.0).then_inc(const_ready, 1)
            dve.memset(chip.eps[:, :], EPS).then_inc(const_ready, 1)
            dve.memset(chip.gn_eps[:, :], GN_EPS).then_inc(const_ready, 1)
            for n, (_, _, vector, _) in enumerate(programs):
                between(dve, n)
                vector(dve)
                dve.drain().then_inc(phase_done, 1)

        @block.gpsimd
        def _(pool):
            pool.memset(chip.ident[:, :], 0.0).then_inc(const_ready, 1)
            pool.wait_ge(const_ready, CONSTS - 1)
            pool.affine_select(out=chip.ident[:, :], in_=chip.ident[:, :], compare_op=ALU.not_equal, fill=1.0,
                               base=0, pattern=[[-1, P]], channel_multiplier=1).then_inc(const_ready, 1)
            for n, (_, _, _, gpsimd) in enumerate(programs):
                between(pool, n)
                if gpsimd:
                    gpsimd(pool)
                pool.drain().then_inc(phase_done, 1)


CONSTS = 5


def tiles(a):
    return np.ascontiguousarray(np.asarray(a).reshape(-1, P).T)


def weight_blocks(w, kt, cols):
    n = w.shape[1] // cols
    b = w.reshape(kt, P, n, cols).transpose(2, 1, 0, 3).reshape(n, P, kt * cols)
    return slotted(b)


def slotted(b):
    return np.pad(b, ((0, 0), (0, 0), (0, SLOT - b.shape[2])))


def stream_rwkv(i):
    w = i["rw_w_in"][0]
    o = {"r": 0, "w": D, "k": D + 64, "v": 2 * D + 64, "a": 3 * D + 64, "g": 3 * D + 128}
    out = [weight_blocks(w[:, o[s]:o[s] + D], KD, 2 * P) for s in "rkv"]
    z = np.zeros((D, 2 * P), w.dtype)
    wa, g = z.copy(), z.copy()
    wa[:, :64], wa[:, 64:128] = w[:, o["w"]:o["w"] + 64], w[:, o["a"]:o["a"] + 64]
    g[:, :LORA_G] = w[:, o["g"]:]
    out += [weight_blocks(wa, KD, 2 * P), weight_blocks(g, KD, 2 * P)]
    low = np.zeros((1, P, SLOT), w.dtype)
    low[0, :64, :D], low[0, :64, D:] = i["rw_w2"][0], i["rw_a2"][0]
    g2 = np.zeros((1, P, SLOT), w.dtype)
    g2[0, :, :D], g2[0, :LORA_G - P, D:] = i["rw_g2"][0][:P], i["rw_g2"][0][P:]
    return out + [low, g2, weight_blocks(i["rw_w_out"][0], KD, 2 * P)]


def stream_ffn(i, layer):
    gu = i["ffn_w_gu"][layer].reshape(D, 2, KF, P).transpose(0, 2, 1, 3).reshape(D, 2 * FF)
    down = i["ffn_w_down"][layer].reshape(2, KF // 2, P, KD, P).transpose(3, 0, 2, 1, 4)
    return [weight_blocks(gu, KD, 2 * P), slotted(down.reshape(2 * KD, P, KF // 2 * P))]


def stream_mlstm(i):
    w = i["ml_w_in"][0]
    gates = np.zeros((D, 2 * P), w.dtype)
    gates[:, :2 * ML_HEADS] = w[:, 3 * D:]
    return [weight_blocks(w[:, :D], KD, 2 * P), weight_blocks(gates, KD, 2 * P),
            weight_blocks(w[:, D:3 * D], KD, 2 * P), weight_blocks(i["ml_w_out"][0], KD, 2 * P)]


def stream_retention(i):
    w = i["ret_w_in_2"][0]
    out = i["ret_w_out_2"][0]
    return [weight_blocks(w, KD, 2 * P), weight_blocks(out, 2 * KD, P)]


def stream_ple(i, layer):
    proj = i["ple_w_proj_2"][layer].reshape(2, P, D).transpose(1, 0, 2).reshape(1, P, SLOT)
    return [proj, weight_blocks(i["ple_w_gate_2"][layer], KD, 2 * P)]


def stream_mla(i):
    w = i["mla_w_in_2"][0]
    c = Q_LORA + KV_LORA
    r1, r2 = w[:, c:c + 32], w[:, c + 32:c + 64]
    rope_w = np.concatenate([r1] * 4 + [r2] * 4, 1)
    out = [weight_blocks(w[:, :c], KD, 2 * P), weight_blocks(rope_w, KD, 2 * P)]
    uq = i["mla_w_uq_2"][0].reshape(Q_LORA, MLA_HEADS, NOPE + ROPE)
    uk, uv = i["mla_w_uk_2"][0], i["mla_w_uv_2"][0]
    for n in range(0, MLA_HEADS, 4):
        out.append(weight_blocks(uq[:, n:n + 4, :NOPE].reshape(Q_LORA, 4 * P), 6, 2 * P))
        halves = [uq[:, n:n + 4, NOPE + 32 * a:NOPE + 32 * a + 32].reshape(Q_LORA, P) for a in range(2)]
        out.append(weight_blocks(np.concatenate(halves, 1), 6, 2 * P))
        kv = [u[:, n:n + 4].reshape(KV_LORA, 4 * P) for u in (uk, uv)]
        out.append(weight_blocks(np.concatenate(kv, 1), 2, 8 * P))
    return out + [weight_blocks(w[:, c + ROPE:], KD, 2 * P), weight_blocks(i["mla_w_out_2"][0], 2 * KD, P)]


def retention_decay():
    log_g = np.log(np.float32(1) - np.float32(2) ** (np.float32(-5) - np.arange(RET_HEADS, dtype=np.float32)))
    rel = np.arange(T, dtype=np.float32)[None, None, :] - np.arange(P, dtype=np.float32)[:, None, None]
    g = np.where(rel >= 0, np.exp(np.maximum(rel, np.float32(0)) * log_g[None, :, None]), np.float32(0))
    return g.astype(np.float32).reshape(P, RET_HEADS * T)


def vectors(i):
    conv = tiles(i["ml_conv_w"][0])
    gate = np.zeros((P, 2), np.float32)
    gate[:ML_HEADS, 0], gate[:ML_HEADS, 1] = i["ml_b_i"][0], i["ml_b_f"][0]
    parts = {
        "c": tiles(i["c"]), "ada_b": tiles(i["ada_b"]), "mix": tiles(i["rw_mix"]), "w0": tiles(i["rw_w0"]),
        "a0": tiles(i["rw_a0"]), "k_k": tiles(i["rw_k_k"]), "k_a": tiles(i["rw_k_a"]), "r_k": tiles(i["rw_r_k"]),
        "gn_w": tiles(i["rw_gn_w"]), "gn_b": tiles(i["rw_gn_b"]), "conv_w": conv, "conv_b": tiles(i["ml_conv_b"]),
        "hn_w": tiles(i["ml_hn_w"]), "gate_b": gate, "final_w": tiles(i["final_w"]),
        "pre_g": tiles(i["pre_norm_g_2"]), "post_g": tiles(i["post_norm_g_2"]), "ret_gn": tiles(i["ret_gn_g_2"]),
        "q_g": tiles(i["mla_q_norm_g_2"]), "kv_g": tiles(i["mla_kv_norm_g_2"])}
    out = np.zeros((P, VEC_COLS), np.float32)
    for name, (a, b) in VEC.items():
        out[:, a:b] = parts[name]
    return out


def constants():
    out = np.zeros((P, CONST_COLS), np.float32)
    p, q = np.arange(P)[:, None], np.arange(P)[None, :]
    s, t, same = p % 64, q % 64, p // 64 == q // 64
    made = {
        "block_ones": same,
        "head_rows": np.concatenate([np.arange(16)[None, :] == 2 * n + p // 64 for n in range(KD)], 1),
        "chunk_keep": np.broadcast_to(np.arange(T) % CHUNK != 0, (P, T)),
        "fold": p % 64 == np.arange(64)[None, :],
        "before": same & (s < t), "upto": same & (s <= t),
        "levels": np.concatenate([same & (s // (2 * m) == t // (2 * m)) & (s // m % 2 == 0) & (t // m % 2 == 1)
                                  for m in (1, 2, 4, 8, 16, 32)], 1),
        "later": np.where(q > p, np.float32(-1e30), np.float32(0)), "inv_freq": INV_FREQ}
    for name, (a, b) in CONST.items():
        out[:, a:b] = made[name]
    return out


def head_columns():
    return (np.arange(D)[None, :] // HEAD == np.arange(16)[:, None]).astype(np.float32)


_E = np.float32(10000.0)
INV_FREQ = np.stack([_E ** (-np.arange(128, dtype=np.float32) / np.float32(128)),
                     np.tile(_E ** (-np.arange(32, dtype=np.float32) / np.float32(32)), 4)], 1).astype(np.float32)


def ada_blocks(i):
    return np.concatenate([weight_blocks(i["ada_w"][n], KD, 2 * P) for n in range(2)])


def stages():
    return [
        (ada, lambda i: []),
        (rwkv_project, stream_rwkv), (rwkv_chunks, lambda i: []), (rwkv_output, lambda i: []),
        (lambda chip: ffn(chip, 0), lambda i: stream_ffn(i, 0)),
        (mlstm, stream_mlstm),
        (lambda chip: ffn(chip, 1), lambda i: stream_ffn(i, 1)),
        (final_norm, lambda i: []),
        (retention, stream_retention),
        (lambda chip: ple(chip, 0), lambda i: stream_ple(i, 0)),
        (mla, stream_mla),
        (lambda chip: ple(chip, 1), lambda i: stream_ple(i, 1)),
    ]


def kernel(**inputs):
    import concourse.bacc as bacc
    from concourse.bass_utils import run_bass_kernel_spmd

    i = {name: np.asarray(a) for name, a in inputs.items()}
    arrays = {
        "x": np.ascontiguousarray(i["x"][0].T),
        "vec": vectors(i),
        "const": constants(),
        "head_cols": head_columns(),
        "ret_decay": retention_decay(),
        "ada": ada_blocks(i),
        "stream": np.concatenate([b for _, weights in stages() for b in weights(i)]),
        "p": np.ascontiguousarray(i["p_2"][:, 0].transpose(0, 2, 1)),
        "pos": np.ascontiguousarray(i["positions_2"]),
    }
    nc = bacc.Bacc("TRN2", target_bir_lowering=False, num_devices=1)
    io = {name: nc.dram_tensor(f"in_{name}", a.shape, mybir.dt.from_np(a.dtype), kind="ExternalInput").ap()
          for name, a in arrays.items()}
    io["y"] = nc.dram_tensor("out_y", (D, T), F32, kind="ExternalOutput").ap()
    block_trunk(nc, io, [phase for phase, _ in stages()])
    r = run_bass_kernel_spmd(nc, [{f"in_{name}": a for name, a in arrays.items()}], core_ids=[0])
    return np.ascontiguousarray(r.results[0]["out_y"].T)[None]
```

```python
from contextlib import ExitStack

import numpy as np

import concourse.bass as bass
from concourse import mybir

F32 = mybir.dt.float32
F32R = mybir.dt.float32r
I32 = mybir.dt.int32
ALU = mybir.AluOpType
ACT = mybir.ActivationFunctionType
AX_X = mybir.AxisListType.X

P = 128
T = 512
D = 1024
KD = D // P
FF = 2816
KF = FF // P
EPS = 1e-6
GN_EPS = 64e-5
SLOT = 2048
SLOTS = 4
LORA, LORA_G = 64, 160
HEAD = 64
ML_HEADS, ML_QK, ML_V, CONV_W, GATE_CAP = 8, 64, 128, 4, 15.0
RET_HEADS, RET_QK, RET_V = 4, 256, 512
MLA_HEADS, NOPE, ROPE, Q_LORA, KV_LORA, PLE = 16, 128, 64, 768, 256, 256


def columns(widths):
    out, at_ = {}, 0
    for name, n in widths:
        out[name] = (at_, at_ + n)
        at_ += n
    return out, at_


VEC, VEC_COLS = columns([
    ("c", KD), ("ada_b", 96), ("mix", 6 * KD), ("w0", KD), ("a0", KD), ("k_k", KD), ("k_a", KD), ("r_k", KD),
    ("gn_w", KD), ("gn_b", KD), ("conv_w", CONV_W * KD), ("conv_b", KD), ("hn_w", KD), ("gate_b", 2),
    ("final_w", KD), ("pre_g", 2 * KD), ("post_g", 2 * KD), ("ret_gn", 16), ("q_g", 6), ("kv_g", 2)])
CONST, CONST_COLS = columns([
    ("block_ones", P), ("head_rows", 16 * KD), ("chunk_keep", T), ("fold", 64),
    ("before", P), ("upto", P), ("levels", 6 * P), ("later", P), ("inv_freq", 2)])


class Tally:

    def __init__(self, sem):
        self.sem, self.n = sem, 0

    def take(self, k):
        base = self.n
        self.n += k
        return base


def at(buf, n):
    return buf[:, n:n + 1, :] if isinstance(n, int) else buf[:, bass.ds(n, 1), :]


def one(ap):
    return ap.rearrange("p (a t) -> p a t", a=1)


def by_four(eng, n, body):
    if n // 4 >= 2:
        with eng.Fori(0, n // 4) as i:
            for s in range(4):
                body(i, s)
    else:
        for r in range(4 * (n // 4)):
            body(r // 4, r % 4)
    for s in range(n % 4):
        body(n // 4, s)


class Chip:

    def __init__(self, nc, ctx, io):
        self.nc, self.ctx, self.io = nc, ctx, io
        self.tallies = {}
        self.top = (nc.sbuf_base + 31) // 32 * 32
        self.floor = self.top
        self.blocks = 0
        self.groups = 2
        self.names = 0
        self.x_offset = self.top
        self.x = self.keep("x_res", [P, KD, T])
        ring_offset = self.top
        self.ring = self.keep("ring", [P, SLOTS, SLOT])
        self.ring_low = self.over("ring_low", [P, SLOTS, SLOT], F32R, ring_offset)
        self.ones = self.keep("ones", [P, P])
        self.ident = self.keep("ident", [P, P])
        self.mod = self.keep("mod", [P, 96])
        self.c_act = self.keep("c_act", [P, KD])
        self.vec = self.keep("vec", [P, VEC_COLS])
        self.const = self.keep("const", [P, CONST_COLS])
        self.eps = self.keep("eps", [P, 1])
        self.gn_eps = self.keep("gn_eps", [P, 1])
        self.bank = [ctx.enter_context(nc.psum_tensor(f"bank{n}", [P, 512], F32)) for n in range(8)]
        self.w_full = [self.sem(f"w_full{s}") for s in range(SLOTS)]
        self.pair_free = [self.sem(f"pair_free{s}") for s in range(2)]
        self.gemm_done = self.sem("gemm_done")
        self.floor = self.base_floor = self.top

    def v(self, name):
        a, b = VEC[name]
        return self.vec[:, a:b]

    def k(self, name):
        a, b = CONST[name]
        return self.const[:, a:b]

    def sem(self, name):
        return self.ctx.enter_context(self.nc.semaphore(name))

    def tally(self, name):
        if name not in self.tallies:
            self.tallies[name] = Tally(self.sem(name))
        return self.tallies[name]

    def begin_phase(self):
        self.top = self.floor
        self.steps = self.loads = 0

    def step_tally(self):
        self.steps += 1
        return self.tally(f"step{self.steps}")

    def load_tally(self):
        self.loads += 1
        return self.tally(f"loaded{self.loads}")

    def keep(self, name, shape, dt=F32):
        size = 1
        for n in shape[1:]:
            size *= n
        self.names += 1
        t = self.nc.alloc_sbuf_tensor_at(f"{name}_{self.names}", shape, dt, offset=self.top)
        self.top += (size * 4 + 31) // 32 * 32
        assert self.top <= 229344, (name, self.top)
        return t

    def over(self, name, shape, dt, offset):
        self.names += 1
        return self.nc.alloc_sbuf_tensor_at(f"{name}_{self.names}", shape, dt, offset=offset)

    def keep_pair(self, name, shape):
        offset = self.top
        raw = self.keep(name, shape)
        return raw, self.keep(name + "_high", shape, F32R), self.over(name + "_low", shape, F32R, offset)

    def take_blocks(self, n):
        b, self.blocks = self.blocks, self.blocks + n
        return b

    def take_groups(self, n):
        u, self.groups = self.groups, self.groups + n
        return u

    def slot(self, b, kt):
        return self.ring[:, b % SLOTS, 0:(SLOT // kt) * kt].rearrange("p (k n) -> p k n", k=kt)

    def wait_block(self, pe, b, i=0):
        pe.wait_ge(self.w_full[b % SLOTS], 16 * (b // SLOTS + 1) + 16 * i)

    def wait_pair(self, pe, u, i=0):
        pe.wait_ge(self.pair_free[u % 2], 2 * (u // 2) + 4 * i)

    def pair(self, u):
        return self.bank[2 * (u % 2)], self.bank[2 * (u % 2) + 1]

    def wait_tile(self, eng, b, j, i=0):
        eng.wait_ge(self.gemm_done, 2 * b + j + 1 + 8 * i)

    def pe_features(self, pe, b0, u0, n, kt, rhs, before=None, split=None):
        cols = 2 * P

        def split_body(i, s):
            split.wait(pe, b0 + s, i)
            self.wait_pair(pe, u0 + s, i)
            parts = split.parts(b0 + s, kt, cols)
            for j in range(2):
                for k in range(kt):
                    if before and s == 0 and j == 0:
                        before(k)
                    mm = three(pe, self.pair(u0 + s)[j][:, :], parts, k, slice(j * P, (j + 1) * P), rhs(k),
                               k == 0, k == kt - 1)
                mm.then_inc(self.gemm_done, 1)

        if split:
            return by_four(pe, n, split_body)

        def body(i, s):
            self.wait_block(pe, b0 + s, i)
            self.wait_pair(pe, u0 + s, i)
            w = self.ring[:, (b0 + s) % SLOTS, 0:kt * cols].rearrange("p (k n) -> p k n", k=kt)
            for j in range(2):
                for k in range(kt):
                    if before and s == 0 and j == 0:
                        before(k)
                    mm = pe.matmul(self.pair(u0 + s)[j][:, :], w[:, k, j * P:(j + 1) * P], rhs(k),
                                   start=(k == 0), stop=(k == kt - 1))
                mm.then_inc(self.gemm_done, 1)

        by_four(pe, n, body)

    def pe_tokens(self, pe, b0, u0, n, kt, lhs, before=None, split=None):
        cols = 2 * P

        def split_body(i, s):
            split.wait(pe, b0 + s, i)
            self.wait_pair(pe, u0 + s, i)
            w_high, w_low = split.parts(b0 + s, kt, cols)
            for j in range(2):
                for half in range(2):
                    tok = slice((2 * j + half) * P, (2 * j + half + 1) * P)
                    out = self.pair(u0 + s)[j][:, half * cols:(half + 1) * cols]
                    for k in range(kt):
                        x_high, x_low = lhs(k)
                        pe.matmul(out, x_high[:, tok], w_high[:, k, :], start=(k == 0), stop=False)
                        pe.matmul(out, x_high[:, tok], w_low[:, k, :], start=False, stop=False)
                        mm = pe.matmul(out, x_low[:, tok], w_high[:, k, :], start=False, stop=(k == kt - 1))
                mm.then_inc(self.gemm_done, 1)

        if split:
            return by_four(pe, n, split_body)

        def body(i, s):
            self.wait_block(pe, b0 + s, i)
            self.wait_pair(pe, u0 + s, i)
            w = self.ring[:, (b0 + s) % SLOTS, 0:kt * cols].rearrange("p (k n) -> p k n", k=kt)
            for j in range(2):
                for half in range(2):
                    for k in range(kt):
                        if before and s == 0 and j == 0 and half == 0:
                            before(k)
                        tok = (2 * j + half) * P
                        mm = pe.matmul(self.pair(u0 + s)[j][:, half * cols:(half + 1) * cols],
                                       lhs(k)[:, tok:tok + P], w[:, k, :],
                                       start=(k == 0), stop=(k == kt - 1))
                mm.then_inc(self.gemm_done, 1)

        by_four(pe, n, body)

    def pe_long(self, pe, b0, u0, tiles, halves, kt, rhs, before=None, split=None):
        per = 2 * halves
        step = 8 // per if per == 4 else 2

        def group(i, r):
            for tile in range(2):
                for half in range(halves):
                    s = r * per + tile * halves + half
                    if split:
                        split.wait(pe, b0 + s, i * (step * per // 4))
                        parts = split.parts(b0 + s, kt, P)
                    else:
                        self.wait_block(pe, b0 + s, i * (step * per // 4))
                    if tile == 0 and half == 0:
                        self.wait_pair(pe, u0 + r, i) if step == 4 else self.wait_pair2(pe, u0 + r, i)
                    w = self.ring[:, (b0 + s) % SLOTS, 0:kt * P].rearrange("p (k n) -> p k n", k=kt)
                    for k in range(kt):
                        kk = half * kt + k
                        if before and s == 0:
                            before(kk)
                        ends = kk == 0, kk == halves * kt - 1
                        if split:
                            mm = three(pe, self.pair(u0 + r)[tile][:, :], parts, k, slice(0, P), rhs(kk), *ends)
                        else:
                            mm = pe.matmul(self.pair(u0 + r)[tile][:, :], w[:, k, :], rhs(kk),
                                           start=ends[0], stop=ends[1])
                    mm.then_inc(self.gemm_done, 2)

        with pe.Fori(0, tiles // 2 // step) as i:
            for r in range(step):
                group(i, r)

    def wait_pair2(self, pe, u, i):
        pe.wait_ge(self.pair_free[u % 2], 2 * (u // 2) + 2 * i)


def three(pe, out, parts, k, cols, moving, start, stop):
    (w_high, w_low), (x_high, x_low) = parts, moving
    pe.matmul(out, w_high[:, k, cols], x_high, start=start, stop=False)
    pe.matmul(out, w_high[:, k, cols], x_low, start=False, stop=False)
    return pe.matmul(out, w_low[:, k, cols], x_high, start=False, stop=stop)


class Split:

    def __init__(self, chip, b0, n, offset=None):
        self.c, self.b0 = chip, b0
        self.high_buf = chip.keep("w_high", [P, 2, SLOT], F32R) if offset is None \
            else chip.over("w_high", [P, 2, SLOT], F32R, offset)
        self.rounded, self.rest = Step(chip, "w_rounded", n), Step(chip, "w_rest", n)

    def high(self, act, b, i=0, cols=SLOT):
        self.c.wait_block(act, b, i)
        if b - self.b0 >= 2 or not isinstance(i, int):
            act.wait_ge(self.c.gemm_done, 2 * (b - 1) + 8 * i)
        act.activation(self.high_buf[:, b % 2, 0:cols], self.c.ring[:, b % SLOTS, 0:cols], ACT.Copy)\
           .then_inc(self.rounded.sem, 1)

    def low(self, pool, b, i=0, cols=SLOT):
        pool.wait_ge(self.rounded.sem, self.rounded.of(b - self.b0) + 4 * i)
        pool.tensor_tensor(self.c.ring_low[:, b % SLOTS, 0:cols], self.c.ring[:, b % SLOTS, 0:cols],
                           self.high_buf[:, b % 2, 0:cols].bitcast(F32), ALU.subtract).then_inc(self.rest.sem, 1)

    def wait(self, pe, b, i=0):
        pe.wait_ge(self.rest.sem, self.rest.of(b - self.b0) + 4 * i)

    def parts(self, b, kt, cols):
        return [a[:, 0:kt * cols].rearrange("p (k n) -> p k n", k=kt)
                for a in (self.high_buf[:, b % 2, :], self.c.ring_low[:, b % SLOTS, :])]


class Norm:

    def __init__(self, chip, src, dst, tiles, gain, shift=None, bank=4, rstd=None, squares=None,
                 high=None, low=None):
        self.high, self.low = high, low
        self.sq = squares or dst
        self.c, self.src, self.dst, self.tiles = chip, src, dst, tiles
        self.gain, self.shift, self.bank = gain, shift, chip.bank[bank]
        self.rstd = rstd if rstd is not None else chip.keep("rstd", [P, T])
        self.steps = {}
        for name, k in (("squared", tiles), ("mean_square", 1), ("root", 1), ("rstd_ready", 1),
                        ("scaled", tiles if shift or high else 0), ("rounded", tiles if high else 0), ("normed", tiles)):
            t = chip.tally("norm_" + name)
            self.steps[name] = (t.sem, t.take(k))
        self.squared, self.mean_square, self.root, self.rstd_ready, self.scaled, self.rounded, \
            self.normed = \
            self.steps.values()

    def scalar(self, act, ready=None):
        self.square(act, ready)
        self.root_and_round(act)

    def square(self, act, ready=None):
        for k in range(self.tiles):
            if ready:
                ready(k)
            act.activation(self.sq(k), self.src(k), ACT.Square).then_inc(self.squared[0], 1)

    def root_and_round(self, act):
        act.wait_ge(self.mean_square[0], self.mean_square[1] + 1)
        act.activation(self.rstd[:, :], self.bank[:, :], ACT.Sqrt, bias=self.c.eps[:, :],
                       scale=1.0 / (self.tiles * P)).then_inc(self.root[0], 1)
        if self.high:
            for k in range(self.tiles):
                act.wait_ge(self.scaled[0], self.scaled[1] + k + 1)
                act.activation(self.high(k), self.dst(k), ACT.Identity if self.shift else ACT.Copy,
                               **({"bias": self.shift(k)} if self.shift else {})).then_inc(self.rounded[0], 1)
        elif self.shift:
            for k in range(self.tiles):
                act.wait_ge(self.scaled[0], self.scaled[1] + k + 1)
                act.activation(self.dst(k), self.dst(k), ACT.Identity, bias=self.shift(k))\
                   .then_inc(self.normed[0], 1)

    def tensor(self, pe):
        for k in range(self.tiles):
            pe.wait_ge(self.squared[0], self.squared[1] + k + 1)
            mm = pe.matmul(self.bank[:, :], self.c.ones[:, :], self.sq(k),
                           start=(k == 0), stop=(k == self.tiles - 1))
        mm.then_inc(self.mean_square[0], 1)

    def vector(self, dve):
        dve.wait_ge(self.root[0], self.root[1] + 1)
        dve.reciprocal(self.rstd[:, :], self.rstd[:, :]).then_inc(self.rstd_ready[0], 1)
        dve.wait_ge(self.rstd_ready[0], self.rstd_ready[1] + 1)
        sem = self.scaled[0] if self.shift or self.high else self.normed[0]

        def rest(k):
            dve.wait_ge(self.rounded[0], self.rounded[1] + k + 1)
            high = self.high(k).bitcast(F32)
            if self.shift:
                dve.scalar_tensor_tensor(out=self.low(k), in0=self.dst(k), scalar=self.shift(k), in1=high,
                                         op0=ALU.add, op1=ALU.subtract).then_inc(self.normed[0], 1)
            else:
                dve.tensor_tensor(self.low(k), self.dst(k), high, ALU.subtract).then_inc(self.normed[0], 1)

        for k in range(self.tiles):
            if self.high and k >= 2:
                rest(k - 2)
            dve.scalar_tensor_tensor(out=self.dst(k), in0=self.src(k), scalar=self.gain(k),
                                     in1=self.rstd[:, :], op0=ALU.mult, op1=ALU.mult).then_inc(sem, 1)
        if self.high:
            rest(self.tiles - 2)
            rest(self.tiles - 1)

    def wait(self, eng, k):
        eng.wait_ge(self.normed[0], self.normed[1] + k + 1)


class Step:

    def __init__(self, chip, name, results):
        tally = chip.step_tally()
        self.name, self.sem, self.base = name, tally.sem, tally.take(results)

    def of(self, k):
        return self.base + k + 1


class Load:

    def __init__(self, chip):
        tally = chip.load_tally()
        self.sem = tally.sem
        self.landed = tally.take(16) + 16


ADA_BLOCKS, ADA_FIRST = 48, 16


def ada_tensor(chip, pe, acc, b, column, i=0):
    for j in range(2):
        pe.matmul(column(j), acc[:, j * P:(j + 1) * P], chip.ones[:, 0:1], start=True, stop=True)\
          .then_inc(chip.gemm_done, 1)


def ada_vector(chip, dve, acc, b, k, part, done):
    w = chip.ring[:, b % SLOTS, :].rearrange("p (k n) -> p k n", k=KD)
    if k == 0:
        dve.tensor_scalar(acc, w[:, 0, :], chip.c_act[:, 0:1], None, ALU.mult).then_inc(part, 1)
    else:
        dve.wait_ge(part, done)
        dve.scalar_tensor_tensor(out=acc, in0=w[:, k, :], scalar=chip.c_act[:, k:k + 1], in1=acc,
                                 op0=ALU.mult, op1=ALU.add).then_inc(part, 1)


def ada_finish(chip, dve, bank, first, last, biased, one_plus):
    dve.tensor_tensor(chip.mod[:, first:last], bank[:, 0:last - first], chip.v("ada_b")[:, first:last], ALU.add)\
       .then_inc(biased.sem, 1)
    dve.wait_ge(biased.sem, biased.of(0))
    for n in range(KD, 96, 24):
        if first <= n < last:
            dve.tensor_scalar(chip.mod[:, n:n + KD], chip.mod[:, n:n + KD], 1.0, None, ALU.add)\
               .then_inc(one_plus.sem, 1)


def ada(chip):
    acc = chip.keep("ada_acc", [P, 2, 2 * P])
    b0 = chip.take_blocks(ADA_FIRST)
    silu = Step(chip, "ada_silu", 1)
    part = Step(chip, "ada_part", ADA_FIRST * KD)
    biased, one_plus = Step(chip, "ada_biased", 1), Step(chip, "ada_one_plus", 1)

    def tensor(pe):
        for g in range(ADA_FIRST):
            pe.wait_ge(part.sem, part.of(g * KD + KD - 1))
            ada_tensor(chip, pe, acc[:, g % 2, :], b0 + g,
                       lambda j: chip.bank[5][:, 2 * g + j:2 * g + j + 1])

    def scalar(act):
        act.activation(chip.c_act[:, :], chip.v("c"), ACT.Silu).then_inc(silu.sem, 1)

    def vector(dve):
        dve.wait_ge(silu.sem, silu.of(0))
        for g in range(ADA_FIRST):
            chip.wait_block(dve, b0 + g)
            if g >= 2:
                dve.wait_ge(chip.gemm_done, 2 * (b0 + g - 1))
            for k in range(KD):
                ada_vector(chip, dve, acc[:, g % 2, :], b0 + g, k, part.sem, part.of(g * KD + k - 1))
        dve.wait_ge(chip.gemm_done, 2 * (b0 + ADA_FIRST))
        ada_finish(chip, dve, chip.bank[5], 0, 2 * ADA_FIRST, biased, one_plus)

    return tensor, scalar, vector, None


KAPPA = float(np.exp(-0.5))
CHUNK = 64
NC_ = T // CHUNK
SEGS = ("r", "k", "v", "w", "a", "g")
MIX_ROW = {"r": 0, "w": 1, "k": 2, "v": 3, "a": 4, "g": 5}


class Rwkv:

    def __init__(self, chip):
        full = [P, KD, T]
        size = 4 * KD * T
        self.k_offset, self.v_offset, self.cum_offset = chip.top + size, chip.top + 2 * size, chip.top + 3 * size
        self.nkk_offset, self.kb_offset = chip.top + 4 * size, chip.top + 5 * size
        self.r = chip.keep("rw_r", full)
        self.k = chip.keep("rw_k", full)
        self.v = chip.keep("rw_v", full)
        self.cum = chip.keep("rw_cum", full)
        self.nkk = chip.keep("rw_nkk", full)
        self.kb = chip.keep("rw_kb", full)
        self.bsum = chip.keep("rw_bsum", [16, T])
        self.sgl = chip.keep("rw_sgl", [P, 2, T])
        chip.floor = chip.top


def rwkv_project(chip):
    f = chip.rwkv = Rwkv(chip)
    h = chip.keep("h", [P, KD, T])
    xx = chip.keep("shift_diff", [P, KD, T])
    twl = chip.keep("tanh_wl", [LORA, T])
    al = chip.keep("al", [LORA, T])
    tmp = chip.keep("tmp", [P, 2, T])
    tmp2 = chip.keep("tmp2", [P, 2, T])
    xs = [f.nkk, f.kb]
    xs_high = [chip.over(f"mix_high{n}", [P, KD, T], F32R, o) for n, o in enumerate((chip.x_offset, f.v_offset))]
    xs_low = [chip.over(f"mix_low{n}", [P, KD, T], F32R, o) for n, o in enumerate((f.nkk_offset, f.kb_offset))]
    a_sig, squares = h, xx
    norm = Norm(chip, lambda k: chip.x[:, k, :], lambda k: h[:, k, :], KD,
                lambda k: chip.mod[:, 8 + k:9 + k], lambda k: chip.mod[:, k:k + 1], rstd=tmp[:, 0, :])
    diff = Step(chip, "rw_diff", KD + 1)
    mixed = Step(chip, "rw_mixed", 6 * KD)
    blk = {s: chip.take_blocks(4) for s in "rkv"}
    grp = {s: chip.take_groups(4) for s in "rkv"}
    split = Split(chip, blk["r"], 12, offset=f.cum_offset)
    x_rounded, x_rest = Step(chip, "rw_mix_rounded", 3 * KD), Step(chip, "rw_mix_rest", 3 * KD)
    b_wa, u_wa = chip.take_blocks(1), chip.take_groups(1)
    b_g, u_g = chip.take_blocks(1), chip.take_groups(1)
    b_l, u_l = chip.take_blocks(1), chip.take_groups(KD)
    low = Step(chip, "rw_low", 2)
    lora = Step(chip, "rw_lora", 2 * KD)
    sigma = Step(chip, "rw_sigma", KD)
    a_ready = Step(chip, "rw_a", KD)
    cum = Step(chip, "rw_cumsum", KD)
    kk = Step(chip, "rw_kk", KD)
    kk_sq = Step(chip, "rw_kk_sq", KD)
    kk_sum = Step(chip, "rw_kk_sum", KD)
    kk_root = Step(chip, "rw_kk_root", KD)
    chain = Step(chip, "rw_key_chain", 6 * KD)
    bonus = Step(chip, "rw_bonus", KD)
    bsum = Step(chip, "rw_bsum", 1)
    bcopy = Step(chip, "rw_bsum_copied", 1)
    order = {"r": 0, "k": 1, "v": 2, "w": 3, "a": 4, "g": 5}

    def tensor(pe):
        norm.tensor(pe)

        def rhs_of(seg):
            buf = xs[order[seg] % 2]
            return lambda k: buf[:, k, :]

        def before_of(seg):
            return lambda k: pe.wait_ge(mixed.sem, mixed.of(order[seg] * KD + k))

        for q, seg in enumerate("rkv"):
            chip.pe_features(pe, blk[seg], grp[seg], 4, KD,
                             lambda k: (xs_high[q % 2][:, k, :], xs_low[q % 2][:, k, :]),
                             before=lambda k: pe.wait_ge(x_rest.sem, x_rest.of(q * KD + k)), split=split)
        chip.wait_block(pe, b_wa)
        chip.wait_pair(pe, u_wa)
        w = chip.ring[:, b_wa % SLOTS, :].rearrange("p (k n) -> p k n", k=KD)
        for j, seg in enumerate("wa"):
            for k in range(KD):
                before_of(seg)(k)
                mm = pe.matmul(chip.pair(u_wa)[j][0:LORA, :], w[:, k, j * LORA:(j + 1) * LORA],
                               rhs_of(seg)(k), start=(k == 0), stop=(k == KD - 1))
            mm.then_inc(chip.gemm_done, 1)
        chip.wait_block(pe, b_g)
        chip.wait_pair(pe, u_g)
        w = chip.ring[:, b_g % SLOTS, :].rearrange("p (k n) -> p k n", k=KD)
        for j, m in enumerate((P, LORA_G - P)):
            for k in range(KD):
                before_of("g")(k)
                mm = pe.matmul(chip.pair(u_g)[j][0:m, :], w[:, k, j * P:j * P + m],
                               rhs_of("g")(k), start=(k == 0), stop=(k == KD - 1))
            mm.then_inc(chip.gemm_done, 1)
        chip.wait_block(pe, b_l)
        pe.wait_ge(low.sem, low.of(1))
        w = chip.ring[0:LORA, b_l % SLOTS, :].rearrange("p (j n) -> p j n", j=2)
        for n in range(KD):
            chip.wait_pair(pe, u_l + n)
            for j, src in enumerate((twl, al)):
                pe.matmul(chip.pair(u_l + n)[j][:, :], w[:, j, n * P:(n + 1) * P], src[:, :],
                          start=True, stop=True).then_inc(lora.sem, 1)
        pe.wait_ge(chip.gemm_done, 2 * b_l + 2)
        for n in range(KD):
            pe.wait_ge(kk_sq.sem, kk_sq.of(n))
            if n >= 2:
                pe.wait_ge(kk_root.sem, kk_root.of(n - 2))
            pe.matmul(chip.bank[5 + n % 2][:, :], chip.k("block_ones"), squares[:, n, :],
                      start=True, stop=True).then_inc(kk_sum.sem, 1)
        for n in range(KD):
            pe.wait_ge(bonus.sem, bonus.of(n))
            mm = pe.matmul(chip.bank[7][0:16, :], chip.k("head_rows")[:, 16 * n:16 * n + 16], squares[:, n, :],
                           start=(n == 0), stop=(n == KD - 1))
        mm.then_inc(bsum.sem, 1)

    def scalar(act):
        split.high(act, blk["r"])
        split.high(act, blk["r"] + 1)
        norm.scalar(act)

        def round_mix(q):
            for k in range(KD):
                act.wait_ge(mixed.sem, mixed.of(q * KD + k))
                act.activation(xs_high[q % 2][:, k, :], xs[q % 2][:, k, :], ACT.Copy).then_inc(x_rounded.sem, 1)

        round_mix(0)
        round_mix(1)
        for q, (seg, dst) in enumerate((("r", f.r), ("k", f.k), ("v", f.v))):
            for n in range(KD):
                chip.wait_tile(act, blk[seg] + n // 2, n % 2)
                u = grp[seg] + n // 2
                act.activation(dst[:, n, :], chip.pair(u)[n % 2][:, :], ACT.Copy)\
                   .then_inc(chip.pair_free[u % 2], 1)
                if n % 2 and (q < 2 or n < 4):
                    split.high(act, blk[seg] + n // 2 + 2)
            if q == 0:
                round_mix(2)
        u = u_wa
        chip.wait_tile(act, b_wa, 0)
        act.activation(twl[:, :], chip.pair(u)[0][0:LORA, :], ACT.Tanh).then_inc(low.sem, 1)
        chip.wait_tile(act, b_wa, 1)
        act.activation(al[:, :], chip.pair(u)[1][0:LORA, :], ACT.Copy).then_inc(low.sem, 1)
        act.wait_ge(low.sem, low.of(1))
        act.sem_inc(chip.pair_free[u % 2], 2)
        u = u_g
        chip.wait_tile(act, b_g, 0)
        act.activation(f.sgl[:, 0, :], chip.pair(u)[0][:, :], ACT.Sigmoid).then_inc(chip.pair_free[u % 2], 1)
        chip.wait_tile(act, b_g, 1)
        act.activation(f.sgl[0:LORA_G - P, 1, :], chip.pair(u)[1][0:LORA_G - P, :], ACT.Sigmoid)\
           .then_inc(chip.pair_free[u % 2], 1)
        for n in range(KD):
            u = u_l + n
            act.wait_ge(lora.sem, lora.of(2 * n))
            if n >= 2:
                act.wait_ge(cum.sem, cum.of(n - 2))
            act.activation(tmp[:, n % 2, :], chip.pair(u)[0][:, :], ACT.Sigmoid,
                           bias=chip.v("w0")[:, n:n + 1]).then_inc(sigma.sem, 1)
            act.wait_ge(lora.sem, lora.of(2 * n + 1))
            if n == 0:
                act.wait_ge(mixed.sem, mixed.of(6 * KD - 1))
            act.activation(a_sig[:, n, :], chip.pair(u)[1][:, :], ACT.Sigmoid,
                           bias=chip.v("a0")[:, n:n + 1]).then_inc(a_ready.sem, 1)
            act.wait_ge(a_ready.sem, a_ready.of(n))
            act.sem_inc(chip.pair_free[u % 2], 2)
        act.sem_inc(chip.gemm_done, 2)
        for n in range(KD):
            act.wait_ge(kk.sem, kk.of(n))
            act.activation(squares[:, n, :], f.nkk[:, n, :], ACT.Square).then_inc(kk_sq.sem, 1)
        for n in range(KD):
            act.wait_ge(kk_sum.sem, kk_sum.of(n))
            if n >= 2:
                act.wait_ge(chain.sem, chain.of(6 * (n - 2) + 2))
            act.activation(tmp2[:, n % 2, :], chip.bank[5 + n % 2][:, :], ACT.Sqrt).then_inc(kk_root.sem, 1)
        act.wait_ge(bsum.sem, bsum.of(0))
        act.activation(f.bsum[:, :], chip.bank[7][0:16, :], ACT.Copy).then_inc(bcopy.sem, 1)

    def vector(dve):
        norm.vector(dve)
        for k in range(KD):
            norm.wait(dve, k)
            dve.tensor_tensor(xx[:, k, 1:T], h[:, k, 0:T - 1], h[:, k, 1:T], ALU.subtract)\
               .then_inc(diff.sem, 1)
        dve.tensor_scalar(xx[:, :, 0:1], h[:, :, 0:1], -1.0, None, ALU.mult).then_inc(diff.sem, 1)
        dve.wait_ge(diff.sem, diff.of(KD))
        last_block = {"v": blk["r"] + 3, "w": blk["k"] + 3, "a": blk["v"] + 3}
        for seg in ("r", "k", "v", "w", "a", "g"):
            if seg in last_block:
                dve.wait_ge(chip.gemm_done, 2 * last_block[seg] + 2)
            if seg == "g":
                dve.wait_ge(chip.gemm_done, 2 * b_wa + 1)
            row, q = MIX_ROW[seg], order[seg]

            def rest(k):
                dve.wait_ge(x_rounded.sem, x_rounded.of(q * KD + k))
                dve.tensor_tensor(xs_low[q % 2][:, k, :], xs[q % 2][:, k, :], xs_high[q % 2][:, k, :].bitcast(F32),
                                  ALU.subtract).then_inc(x_rest.sem, 1)

            for k in range(KD):
                if q < 3 and k >= 2:
                    rest(k - 2)
                dve.scalar_tensor_tensor(out=xs[order[seg] % 2][:, k, :], in0=xx[:, k, :],
                                         scalar=chip.v("mix")[:, row * KD + k:row * KD + k + 1],
                                         in1=h[:, k, :], op0=ALU.mult, op1=ALU.add).then_inc(mixed.sem, 1)
            if q < 3:
                rest(KD - 2)
                rest(KD - 1)
        dve.wait_ge(chip.gemm_done, 2 * b_g + 2)
        dve.wait_ge(chip.pair_free[(grp["v"] + 3) % 2], 2 * ((grp["v"] + 3) // 2 + 1))
        for n in range(KD):
            dve.tensor_scalar(f.nkk[:, n, :], f.k[:, n, :], chip.v("k_k")[:, n:n + 1], None, ALU.mult)\
               .then_inc(kk.sem, 1)
        for n in range(KD):
            dve.wait_ge(sigma.sem, sigma.of(n))
            dve.tensor_tensor_scan(f.cum[:, n, :], chip.k("chunk_keep"), tmp[:, n % 2, :], 0.0,
                                   ALU.mult, ALU.add).then_inc(cum.sem, 1)
        for n in range(KD):
            dve.wait_ge(kk_root.sem, kk_root.of(n))
            t = tmp2[:, n % 2, :]
            dve.tensor_scalar(t, t, 1e-12, None, ALU.max).then_inc(chain.sem, 1)
            dve.wait_ge(chain.sem, chain.of(6 * n))
            dve.reciprocal(t, t).then_inc(chain.sem, 1)
            dve.wait_ge(chain.sem, chain.of(6 * n + 1))
            dve.scalar_tensor_tensor(out=f.nkk[:, n, :], in0=f.nkk[:, n, :], scalar=-1.0, in1=t,
                                     op0=ALU.mult, op1=ALU.mult).then_inc(chain.sem, 1)
            dve.wait_ge(chain.sem, chain.of(6 * n + 2))
            dve.wait_ge(a_ready.sem, a_ready.of(n))
            dve.scalar_tensor_tensor(out=f.kb[:, n, :], in0=f.nkk[:, n, :], scalar=-1.0, in1=a_sig[:, n, :],
                                     op0=ALU.mult, op1=ALU.mult).then_inc(chain.sem, 1)
            dve.wait_ge(chain.sem, chain.of(6 * n + 3))
            dve.tensor_scalar(a_sig[:, n, :], a_sig[:, n, :], 1.0, chip.v("k_a")[:, n:n + 1],
                              ALU.subtract, ALU.mult).then_inc(chain.sem, 1)
            dve.wait_ge(chain.sem, chain.of(6 * n + 4))
            dve.scalar_tensor_tensor(out=f.k[:, n, :], in0=a_sig[:, n, :], scalar=1.0, in1=f.k[:, n, :],
                                     op0=ALU.add, op1=ALU.mult).then_inc(chain.sem, 1)
            dve.wait_ge(chain.sem, chain.of(6 * n + 5))
            dve.wait_ge(kk_sum.sem, kk_sum.of(n))
            dve.scalar_tensor_tensor(out=squares[:, n, :], in0=f.r[:, n, :],
                                     scalar=chip.v("r_k")[:, n:n + 1], in1=f.k[:, n, :],
                                     op0=ALU.mult, op1=ALU.mult).then_inc(bonus.sem, 1)

    def gpsimd(pool):
        for b in range(blk["r"], blk["r"] + 12):
            split.low(pool, b)

    return tensor, scalar, vector, gpsimd


def rwkv_chunks(chip):
    f = chip.rwkv
    wide = [P, KD, P]
    narrow = [P, KD, CHUNK]
    abd, rbd, kbd, bbd = (chip.keep(n, wide) for n in ("a_bd", "r_bd", "k_bd", "b_bd"))
    L, Arb, Aak, Ark = (chip.keep(n, wide) for n in ("ab_bd", "rb_bd", "ak_bd", "rk_bd"))
    Y, Tm, Lm = (chip.keep(n, wide) for n in ("inv_t", "step_t", "level"))
    e = chip.keep("decay", [P, KD, CHUNK + 1])
    edge = chip.keep("chunk_decay", [P, KD, 1])
    acc = chip.k("chunk_keep").rearrange("p (s n) -> p s n", s=2)
    b_ada = chip.take_blocks(ADA_BLOCKS - ADA_FIRST)
    assert ADA_BLOCKS - ADA_FIRST == SLOTS * NC_
    low_top = chip.top
    chip.top = chip.x_offset
    X, ra = chip.keep("inv", wide), chip.keep("ra", wide)
    Vs, R, S, en = (chip.keep(n, narrow) for n in ("v_tok", "rhs", "state", "growth"))
    U = R
    assert chip.top <= chip.x_offset + KD * T * 4
    chip.top = low_top
    vbd, kt, bt, ybd = Lm, Tm, Lm, X

    def step(name, per):
        s = Step(chip, "ch_" + name, per * NC_)
        s.per = per
        return s

    decay, stacked, keys = step("decay", 2), step("stacked", 2), step("keys", 4)
    diag, vdiag = step("diag", 4), step("vdiag", 2)
    pair_ab, pair_ak, vtok_mm, vtok = step("ab", 2), step("ak", 2), step("vtok_mm", 2), step("vtok", 2)
    masked = step("masked", 8)
    level = step("level", 6)
    first_mm, first_x, first_y = step("first_mm", 2), step("first_x", 2), step("first_y", 2)
    t_mm, t_ready = step("t_mm", 10), step("t_ready", 10)
    x_mm, x_ready = step("x_mm", 8), step("x_ready", 8)
    y_mm, y_ready = step("y_mm", 10), step("y_ready", 10)
    tr_mm, tr = step("tr_mm", 4), step("tr", 4)
    r_mm, r_ready = step("r_mm", 2), step("r_ready", 2)
    u_mm, u_ready = step("u_mm", 2), step("u_ready", 2)
    o_mm, o_diag, ot_mm, o_out = step("o_mm", 2), step("o_diag", 4), step("ot_mm", 2), step("o_out", 2)
    s_mm, s_sum, state = step("s_mm", 2), step("s_sum", 2), step("state", 2)
    cleared = Step(chip, "ch_cleared", 6)
    edged = step("edged", 1)
    part = step("ada_part", SLOTS * KD)
    ada_biased, ada_one_plus = Step(chip, "ada_biased", 1), Step(chip, "ada_one_plus", 3)

    def wait(eng, st, c, k):
        eng.wait_ge(st.sem, st.of(k) + c * st.per)

    def wait_last(eng, st, c, k):
        if not isinstance(c, int) or c:
            eng.wait_ge(st.sem, st.of(k) + c * st.per - st.per)

    def rows(h):
        return slice(64 * h, 64 * h + 64)

    def quad(buf, h):
        return buf[:, 4 * h:4 * h + 4, :]

    def psum(n, w):
        return chip.bank[n][:, 0:4 * w].rearrange("p (q w) -> p q w", q=4)

    def chunks(eng, body):
        body(0)
        with eng.Fori(1, NC_) as c:
            body(c)

    def cut(buf, c):
        return buf[:, :, bass.ds(c * CHUNK, CHUNK)] if not isinstance(c, int) \
            else buf[:, :, c * CHUNK:(c + 1) * CHUNK]

    def cut_part(buf, c, a, b, q0=0, q1=KD):
        if isinstance(c, int):
            return buf[a:b, q0:q1, c * CHUNK:(c + 1) * CHUNK]
        return buf[a:b, q0:q1, bass.ds(c * CHUNK, CHUNK)]

    def tensor(pe):
        pe.wait_ge(cleared.sem, cleared.of(5))

        def sum_ada(c, s):
            wait(pe, part, c, s * KD + KD - 1)
            col = lambda j: chip.bank[7][:, 8 * c + 256 + 2 * s + j:8 * c + 257 + 2 * s + j] \
                if isinstance(c, int) else chip.bank[7][:, bass.ds(8 * c + 256 + 2 * s + j, 1)]
            ada_tensor(chip, pe, acc[:, s % 2, :], b_ada + s, col)

        def body(c):
            for h in range(2):
                wait(pe, stacked, c, 1)
                wait(pe, keys, c, 3)
                if h == 0:
                    wait_last(pe, state, c, 1)
                    wait_last(pe, o_out, c, 1)
                for q in range(4):
                    mm = pe.matmul(psum(4 * h, P)[:, q, :], bbd[:, 4 * h + q, :], ra[:, 4 * h + q, :],
                                   start=True, stop=True)
                mm.then_inc(pair_ab.sem, 1)
                for q in range(4):
                    mm = pe.matmul(psum(4 * h + 1, P)[:, q, :], kbd[:, 4 * h + q, :], ra[:, 4 * h + q, :],
                                   start=True, stop=True)
                mm.then_inc(pair_ak.sem, 1)
                wait(pe, vdiag, c, 1)
                for q in range(4):
                    mm = pe.matmul(psum(4 * h + 3, CHUNK)[:, q, :], vbd[:, 4 * h + q, :],
                                   chip.k("fold"), start=True, stop=True)
                mm.then_inc(vtok_mm.sem, 1)
            for h in range(2):
                wait(pe, level, c, 0)
                wait(pe, masked, c, 4 * h + 1)
                for q in range(4):
                    mm = pe.matmul(psum(4 * h, P)[:, q, :], Lm[:, 4 * h + q, :], chip.ident[:, :],
                                   start=True, stop=True)
                mm.then_inc(first_mm.sem, 1)
            for lv in range(1, 6):
                if lv == 3:
                    wait(pe, vtok, c, 1)
                    sum_ada(c, 0)
                if lv == 4:
                    sum_ada(c, 1)
                for h in range(2):
                    wait(pe, level, c, lv)
                    if lv == 1:
                        wait(pe, first_x, c, h)
                        wait(pe, first_y, c, h)
                    else:
                        wait(pe, x_ready, c, 2 * (lv - 2) + h)
                        wait(pe, y_ready, c, 2 * (lv - 2) + h)
                    for q in range(4):
                        mm = pe.matmul(psum(4 * h, P)[:, q, :], Lm[:, 4 * h + q, :], X[:, 4 * h + q, :],
                                       start=True, stop=True)
                    mm.then_inc(t_mm.sem, 1)
                for h in range(2):
                    wait(pe, t_ready, c, 2 * (lv - 1) + h)
                    if lv < 5:
                        for q in range(4):
                            mm = pe.matmul(psum(4 * h + 1, P)[:, q, :], Y[:, 4 * h + q, :],
                                           Tm[:, 4 * h + q, :], start=True, stop=True)
                        mm.then_inc(x_mm.sem, 1)
                    for q in range(4):
                        mm = pe.matmul(psum(4 * h + 2, P)[:, q, :], Tm[:, 4 * h + q, :],
                                       Y[:, 4 * h + q, :], start=True, stop=True)
                    mm.then_inc(y_mm.sem, 1)
            for h in range(2):
                wait(pe, masked, c, 7)
                for n, src in enumerate((kbd, bbd)):
                    for q in range(4):
                        mm = pe.matmul(psum(4 * h + n, P)[:, q, :], src[:, 4 * h + q, :], chip.ident[:, :],
                                       start=True, stop=True)
                    mm.then_inc(tr_mm.sem, 1)
                wait(pe, vtok, c, h)
                for q in range(4):
                    p = 4 * h + q
                    pe.matmul(psum(4 * h + 3, CHUNK)[:, q, :], abd[:, p, :], S[:, p, :], start=True, stop=False)
                    mm = pe.matmul(psum(4 * h + 3, CHUNK)[:, q, :], Aak[:, p, :], Vs[:, p, :],
                                   start=False, stop=True)
                mm.then_inc(r_mm.sem, 1)
            for h in range(2):
                wait(pe, r_ready, c, h)
                wait(pe, y_ready, c, 8 + h)
                for q in range(4):
                    mm = pe.matmul(psum(4 * h + 2, CHUNK)[:, q, :], Y[:, 4 * h + q, :], R[:, 4 * h + q, :],
                                   start=True, stop=True)
                mm.then_inc(u_mm.sem, 1)
            for h in range(2):
                wait(pe, u_ready, c, h)
                wait(pe, tr, c, 2 * h + 1)
                for q in range(4):
                    p = 4 * h + q
                    pe.matmul(psum(4 * h, CHUNK)[:, q, :], kt[:, p, :], Vs[:, p, :], start=True, stop=False)
                    mm = pe.matmul(psum(4 * h, CHUNK)[:, q, :], bt[:, p, :], U[:, p, :], start=False, stop=True)
                mm.then_inc(s_mm.sem, 1)
                for q in range(4):
                    p = 4 * h + q
                    o = psum(4 * h + 1, CHUNK)[:, q, :]
                    pe.matmul(o, rbd[:, p, :], S[:, p, :], start=True, stop=False)
                    pe.matmul(o, Ark[:, p, :], Vs[:, p, :], start=False, stop=False)
                    mm = pe.matmul(o, Arb[:, p, :], U[:, p, :], start=False, stop=True)
                mm.then_inc(o_mm.sem, 1)
            for h in range(2):
                wait(pe, o_diag, c, 2 * h + 1)
                for q in range(4):
                    mm = pe.matmul(psum(4 * h + 2, CHUNK)[:, q, :], ybd[:, 4 * h + q, :], chip.k("fold"),
                                   start=True, stop=True)
                mm.then_inc(ot_mm.sem, 1)
            sum_ada(c, 2)
            sum_ada(c, 3)

        chunks(pe, body)

    def scalar(act):
        def exps(c):
            act.activation(e[:, :, 1:CHUNK + 1], cut(f.cum, c), ACT.Exp, scale=-KAPPA).then_inc(decay.sem, 1)
            act.activation(en[:, :, :], cut(f.cum, c), ACT.Exp, scale=KAPPA).then_inc(decay.sem, 1)

        def body(c, more=True):
            for h in range(2):
                wait(act, vtok_mm, c, h)
                act.activation(quad(Vs, h), psum(4 * h + 3, CHUNK), ACT.Copy).then_inc(vtok.sem, 1)
            for lv in range(1, 6):
                for h in range(2):
                    wait(act, t_mm, c, 2 * (lv - 1) + h)
                    act.activation(quad(Tm, h), psum(4 * h, P), ACT.Copy).then_inc(t_ready.sem, 1)
                if lv == 3 and more:
                    wait(act, keys, c, 3)
                    wait(act, edged, c, 0)
                    exps(c + 1)
            for h in range(2):
                wait(act, y_mm, c, 8 + h)
                for n, dst in enumerate((kt, bt)):
                    wait(act, tr_mm, c, 2 * h + n)
                    act.activation(quad(dst, h), psum(4 * h + n, P), ACT.Copy).then_inc(tr.sem, 1)
                wait(act, r_mm, c, h)
                act.activation(quad(R, h), psum(4 * h + 3, CHUNK), ACT.Copy).then_inc(r_ready.sem, 1)
            for h in range(2):
                wait(act, u_mm, c, h)
                act.activation(quad(U, h), psum(4 * h + 2, CHUNK), ACT.Copy).then_inc(u_ready.sem, 1)
            for h in range(2):
                wait(act, ot_mm, c, h)
                act.activation(cut_part(f.r, c, 0, P, 4 * h, 4 * h + 4), psum(4 * h + 2, CHUNK), ACT.Copy)\
                   .then_inc(o_out.sem, 1)

        exps(0)
        body(0)
        with act.Fori(1, NC_ - 1) as c:
            body(c)
        body(NC_ - 1, more=False)

    def vector(dve):
        dve.memset(S[:, :, :], 0.0).then_inc(cleared.sem, 1)
        dve.memset(e[:, :, 0:1], 1.0).then_inc(cleared.sem, 1)
        dve.wait_ge(cleared.sem, cleared.of(5))

        def prepare(c):
            wait(dve, decay, c, 1)
            dve.tensor_tensor(ra[:, :, 0:CHUNK], cut(f.nkk, c), e[:, :, 0:CHUNK], ALU.mult)\
               .then_inc(stacked.sem, 1)
            dve.tensor_tensor(ra[:, :, CHUNK:P], cut(f.r, c), e[:, :, 1:CHUNK + 1], ALU.mult)\
               .then_inc(stacked.sem, 1)
            wait_last(dve, tr_mm, c, 3)
            for src, dst in ((f.k, kbd), (f.kb, bbd)):
                for h in range(2):
                    dve.tensor_tensor(dst[rows(h), :, 64 * h:64 * h + 64], cut_part(src, c, 64 * h, 64 * h + 64),
                                      en[rows(h), :, :], ALU.mult).then_inc(keys.sem, 1)

        def body(c, more=True):
            ada_ops = [(s, k) for s in range(SLOTS) for k in range(KD)]

            def some_ada(n):
                for s, k in ada_ops[:n]:
                    if k == 0:
                        chip.wait_block(dve, b_ada + s, c)
                        if s >= 2 or not isinstance(c, int) or c:
                            dve.wait_ge(chip.gemm_done, 2 * (b_ada + s - 1) + 8 * c)
                    ada_vector(chip, dve, acc[:, s % 2, :], b_ada + s, k, part.sem,
                               part.of(s * KD + k - 1) + c * part.per)
                del ada_ops[:n]

            wait_last(dve, state, c, 1)
            dve.tensor_copy(edge[:, :, :], e[:, :, CHUNK:CHUNK + 1]).then_inc(edged.sem, 1)
            for h in range(2):
                for bank, st, outs in ((4 * h, pair_ab, ((L, "before"), (Arb, "upto"))),
                                       (4 * h + 1, pair_ak, ((Aak, "before"), (Ark, "upto")))):
                    wait(dve, st, c, h)
                    for n, (dst, mask) in enumerate(outs):
                        scored = psum(bank, P)[:, :, 64 * n:64 * n + 64]
                        dve.tensor_tensor(quad(dst, h).rearrange("p q (a t) -> p q a t", a=2),
                                          scored.unsqueeze(2).to_broadcast([P, 4, 2, CHUNK]),
                                          chip.k(mask).rearrange("p (a t) -> p a t", a=2).unsqueeze(1)
                                          .to_broadcast([P, 4, 2, CHUNK]),
                                          ALU.mult).then_inc(masked.sem, 1)
            for h in range(2):
                wait(dve, first_mm, c, h)
                eye = chip.ident[:, :].unsqueeze(1).to_broadcast([P, 4, P])
                dve.tensor_tensor(quad(X, h), psum(4 * h, P), eye, ALU.add).then_inc(first_x.sem, 1)
                dve.tensor_tensor(quad(Y, h), quad(Lm, h), eye, ALU.add).then_inc(first_y.sem, 1)
            for lv in range(1, 6):
                for h in range(2):
                    wait(dve, y_mm, c, 2 * (lv - 1) + h)
                    if lv < 5:
                        dve.tensor_tensor(quad(X, h), psum(4 * h + 1, P), quad(X, h), ALU.add)\
                           .then_inc(x_ready.sem, 1)
                    dve.tensor_tensor(quad(Y, h), psum(4 * h + 2, P), quad(Y, h), ALU.add)\
                       .then_inc(y_ready.sem, 1)
                    some_ada(4 if lv == 1 else 3)
            if more:
                prepare(c + 1)
            for h in range(2):
                wait(dve, o_mm, c, h)
                for a in range(2):
                    dve.tensor_copy(ybd[rows(a), 4 * h:4 * h + 4, 64 * a:64 * a + 64],
                                    psum(4 * h + 1, CHUNK)[rows(a), :, :]).then_inc(o_diag.sem, 1)
                wait(dve, s_mm, c, h)
                dve.tensor_tensor(quad(S, h), psum(4 * h, CHUNK), quad(S, h), ALU.add).then_inc(s_sum.sem, 1)
                wait(dve, s_sum, c, h)
                dve.tensor_tensor(quad(S, h), quad(S, h),
                                  edge[:, 4 * h:4 * h + 4, :].to_broadcast([P, 4, CHUNK]),
                                  ALU.mult).then_inc(state.sem, 1)

        prepare(0)
        body(0)
        with dve.Fori(1, NC_ - 1) as c:
            body(c)
        body(NC_ - 1, more=False)
        dve.wait_ge(chip.gemm_done, 2 * (b_ada + ADA_BLOCKS - ADA_FIRST))
        ada_finish(chip, dve, chip.bank[7][:, 256:512], 2 * ADA_FIRST, 96, ada_biased, ada_one_plus)

    def gpsimd(pool):
        for buf in (abd, rbd, kbd, bbd):
            pool.memset(buf[:, :, :], 0.0).then_inc(cleared.sem, 1)
        pool.wait_ge(cleared.sem, cleared.of(5))

        def body(c):
            wait_last(pool, s_mm, c, 1)
            if c == 0:
                pool.memset(vbd[:, :, :], 0.0).then_inc(vzero.sem, 1)
                pool.wait_ge(vzero.sem, vzero.of(0))
            for h in range(2):
                pool.tensor_copy(vbd[rows(h), :, 64 * h:64 * h + 64], cut_part(f.v, c, 64 * h, 64 * h + 64))\
                    .then_inc(vdiag.sem, 1)
                wait(pool, vdiag, c, h)
            wait(pool, stacked, c, 1)
            wait_last(pool, o_mm, c, 1)
            for n, dst in enumerate((abd, rbd)):
                for h in range(2):
                    pool.tensor_copy(dst[rows(h), :, 64 * h:64 * h + 64], ra[rows(h), :, 64 * n:64 * n + 64])\
                        .then_inc(diag.sem, 1)
                    wait(pool, diag, c, 2 * n + h)
            for lv in range(6):
                if lv == 0:
                    wait(pool, vtok_mm, c, 1)
                    wait(pool, masked, c, 7)
                elif lv == 1:
                    wait(pool, first_y, c, 1)
                else:
                    wait(pool, t_mm, c, 2 * (lv - 2) + 1)
                pool.tensor_tensor(Lm[:, :, :], L[:, :, :],
                                   chip.k("levels")[:, lv * P:(lv + 1) * P].unsqueeze(1).to_broadcast([P, KD, P]),
                                   ALU.mult).then_inc(level.sem, 1)

        for c in range(NC_):
            body(c)

    vzero = Step(chip, "ch_vzero", 1)
    return tensor, scalar, vector, gpsimd


def rwkv_output(chip):
    f = chip.rwkv
    sq = chip.keep("sq", [P, 2, T])
    rstd = chip.keep("gn_rstd", [P, 2, T])
    bv = chip.keep("bonus_v", [P, 2, T])
    head_cols = chip.keep("head_cols", [16, D])
    b_g, u_g = chip.take_blocks(1), chip.take_groups(KD)
    b_o, u_o = chip.take_blocks(4), chip.take_groups(4)
    z = f.k
    z_high = chip.over("z_high", [P, KD, T], F32R, f.nkk_offset)
    z_low = chip.over("z_low", [P, KD, T], F32R, f.k_offset)
    split = Split(chip, b_o, 4, offset=f.kb_offset)
    z_rounded, z_rest = Step(chip, "rw_z_rounded", KD), Step(chip, "rw_z_rest", KD)
    x_back, cols_ready = Load(chip), Load(chip)
    mean_mm, centred, sq_done = Step(chip, "rw_mean", KD), Step(chip, "rw_centred", KD), Step(chip, "rw_sq", KD)
    var_mm, root = Step(chip, "rw_var", KD), Step(chip, "rw_root", KD)
    gate_mm, bonus_mm, out = Step(chip, "rw_gate", KD), Step(chip, "rw_bonus_mm", KD), Step(chip, "rw_out", 4 * KD)
    gated = Step(chip, "rw_gated", KD)

    def tensor(pe):
        chip.wait_block(pe, b_g)
        w = chip.ring[:, b_g % SLOTS, :].rearrange("p (j n) -> p j n", j=2)

        def mean(n):
            if n >= 2:
                pe.wait_ge(centred.sem, centred.of(n - 2))
            pe.matmul(chip.bank[4 + n % 2][:, :], chip.k("block_ones"), f.r[:, n, :], start=True, stop=True)\
              .then_inc(mean_mm.sem, 1)

        def rest(n):
            pe.wait_ge(sq_done.sem, sq_done.of(n))
            if n >= 2:
                pe.wait_ge(root.sem, root.of(n - 2))
            pe.matmul(chip.bank[6 + n % 2][:, :], chip.k("block_ones"), sq[:, n % 2, :], start=True, stop=True)\
              .then_inc(var_mm.sem, 1)
            if n == 0:
                pe.wait_ge(cols_ready.sem, cols_ready.landed)
            chip.wait_pair(pe, u_g + n)
            pe.matmul(chip.pair(u_g + n)[0][:, :], w[:, 0, n * P:(n + 1) * P], f.sgl[:, 0, :],
                      start=True, stop=False)
            pe.matmul(chip.pair(u_g + n)[0][:, :], w[0:LORA_G - P, 1, n * P:(n + 1) * P],
                      f.sgl[0:LORA_G - P, 1, :], start=False, stop=True).then_inc(gate_mm.sem, 1)
            pe.matmul(chip.pair(u_g + n)[1][:, :], head_cols[:, n * P:(n + 1) * P], f.bsum[:, :],
                      start=True, stop=True).then_inc(bonus_mm.sem, 1)

        for n in range(KD + 1):
            if n < KD:
                mean(n)
            if n:
                rest(n - 1)
        pe.wait_ge(chip.gemm_done, 2 * b_g + 2)
        chip.pe_features(pe, b_o, u_o, 4, KD, lambda k: (z_high[:, k, :], z_low[:, k, :]),
                         before=lambda k: pe.wait_ge(z_rest.sem, z_rest.of(k)), split=split)

    def scalar(act):
        act.dma_start(head_cols[:, :], chip.io["head_cols"]).then_inc(cols_ready.sem, 16)
        act.dma_start(chip.x[:, :, :], chip.io["x"].rearrange("(k p) t -> p k t", p=P)).then_inc(x_back.sem, 16)
        split.high(act, b_o)
        split.high(act, b_o + 1)

        def round_z(n):
            act.wait_ge(gated.sem, gated.of(n))
            act.activation(z_high[:, n, :], z[:, n, :], ACT.Copy).then_inc(z_rounded.sem, 1)

        for n in range(KD):
            act.wait_ge(centred.sem, centred.of(n))
            if n >= 2:
                act.wait_ge(var_mm.sem, var_mm.of(n - 2))
            act.activation(sq[:, n % 2, :], f.r[:, n, :], ACT.Square).then_inc(sq_done.sem, 1)
            act.wait_ge(var_mm.sem, var_mm.of(n))
            if n >= 2:
                act.wait_ge(out.sem, out.of(4 * (n - 2) + 1))
            act.activation(rstd[:, n % 2, :], chip.bank[6 + n % 2][:, :], ACT.Sqrt, bias=chip.gn_eps[:, :],
                           scale=1.0 / HEAD).then_inc(root.sem, 1)
            if n:
                round_z(n - 1)
        round_z(KD - 1)
        split.high(act, b_o + 2)
        split.high(act, b_o + 3)

    def gpsimd(pool):
        split.low(pool, b_o)
        split.low(pool, b_o + 1)
        for n in range(KD):
            pool.wait_ge(z_rounded.sem, z_rounded.of(n))
            pool.tensor_tensor(z_low[:, n, :], z[:, n, :], z_high[:, n, :].bitcast(F32), ALU.subtract)\
                .then_inc(z_rest.sem, 1)
        split.low(pool, b_o + 2)
        split.low(pool, b_o + 3)

    def vector(dve):
        def centre(n):
            dve.wait_ge(mean_mm.sem, mean_mm.of(n))
            dve.scalar_tensor_tensor(out=f.r[:, n, :], in0=chip.bank[4 + n % 2][:, :], scalar=-1.0 / HEAD,
                                     in1=f.r[:, n, :], op0=ALU.mult, op1=ALU.add).then_inc(centred.sem, 1)

        def finish(n):
            y, t = f.r[:, n, :], rstd[:, n % 2, :]
            dve.wait_ge(root.sem, root.of(n))
            dve.reciprocal(t, t).then_inc(out.sem, 1)
            dve.wait_ge(out.sem, out.of(4 * n))
            dve.scalar_tensor_tensor(out=y, in0=y, scalar=chip.v("gn_w")[:, n:n + 1], in1=t,
                                     op0=ALU.mult, op1=ALU.mult).then_inc(out.sem, 1)
            dve.wait_ge(bonus_mm.sem, bonus_mm.of(n))
            dve.tensor_tensor(bv[:, n % 2, :], chip.pair(u_g + n)[1][:, :], f.v[:, n, :], ALU.mult)\
               .then_inc(out.sem, 1)
            dve.wait_ge(out.sem, out.of(4 * n + 2))
            dve.scalar_tensor_tensor(out=y, in0=y, scalar=chip.v("gn_b")[:, n:n + 1], in1=bv[:, n % 2, :],
                                     op0=ALU.add, op1=ALU.add).then_inc(out.sem, 1)
            dve.wait_ge(out.sem, out.of(4 * n + 3))
            dve.tensor_tensor(z[:, n, :], chip.pair(u_g + n)[0][:, :], y, ALU.mult).then_inc(gated.sem, 1)
            dve.wait_ge(gated.sem, gated.of(n))
            dve.sem_inc(chip.pair_free[(u_g + n) % 2], 2)

        for n in range(KD + 1):
            if n < KD:
                centre(n)
            if n:
                finish(n - 1)
        dve.sem_inc(chip.gemm_done, 2)
        dve.wait_ge(x_back.sem, x_back.landed)
        residual(chip, dve, b_o, u_o, lambda n: chip.mod[:, 16 + n:17 + n])

    chip.floor = chip.base_floor
    return tensor, scalar, vector, gpsimd


def residual(chip, dve, b0, u0, gain):
    for n in range(KD):
        chip.wait_tile(dve, b0 + n // 2, n % 2)
        u = u0 + n // 2
        dve.scalar_tensor_tensor(out=chip.x[:, n, :], in0=chip.pair(u)[n % 2][:, :], scalar=gain(n),
                                 in1=chip.x[:, n, :], op0=ALU.mult, op1=ALU.add)\
           .then_inc(chip.pair_free[u % 2], 1)


def ffn(chip, layer):
    m = 48 * layer
    HALF = KF // 2 * P
    h, h_high, h_low = chip.keep_pair("h", [P, KD, T])
    silu = chip.keep("silu_gate", [P, 2, T])
    prod = chip.keep("product", [P, 2, T])
    hid_high, hid_low = (chip.keep("hidden_" + n, [P, KF, T], F32R) for n in ("high", "low"))
    norm = Norm(chip, lambda k: chip.x[:, k, :], lambda k: h[:, k, :], KD,
                lambda k: chip.mod[:, m + 32 + k:m + 33 + k], lambda k: chip.mod[:, m + 24 + k:m + 25 + k],
                high=lambda k: h_high[:, k, :], low=lambda k: h_low[:, k, :], rstd=prod[:, 0, :])
    b0, u0 = chip.take_blocks(KF), chip.take_groups(KF)
    b1, u1 = chip.take_blocks(2 * KD), chip.take_groups(KD // 2)
    split = Split(chip, b0, KF + 2 * KD)
    gated, product = Step(chip, "ffn_gated", KF), Step(chip, "ffn_product", KF)
    rounded, rest = Step(chip, "ffn_rounded", KF), Step(chip, "ffn_rest", KF)

    def tensor(pe):
        norm.tensor(pe)
        chip.pe_features(pe, b0, u0, 1, KD, lambda k: (h_high[:, k, :], h_low[:, k, :]), split=split,
                         before=lambda k: norm.wait(pe, k))
        chip.pe_features(pe, b0 + 1, u0 + 1, KF - 1, KD, lambda k: (h_high[:, k, :], h_low[:, k, :]), split=split)
        pe.wait_ge(rest.sem, rest.of(KF - 1))
        chip.pe_long(pe, b1, u1, KD, 2, KF // 2, lambda k: (hid_high[:, k, :], hid_low[:, k, :]), split=split)

    def scalar(act):
        norm.scalar(act)
        for b in range(2):
            split.high(act, b0 + b)

        def gate(i, s):
            chip.wait_tile(act, b0 + s, 0, i)
            act.activation(silu[:, (u0 + s) % 2, :], chip.pair(u0 + s)[0][:, :], ACT.Silu)\
               .then_inc(gated.sem, 1)
            act.wait_ge(product.sem, product.of(s) + 4 * i)
            act.activation(at(hid_high, 4 * i + s), one(prod[:, s % 2, :]), ACT.Copy).then_inc(rounded.sem, 1)
            split.high(act, b0 + s + 2, i)
        by_four(act, KF, gate)
        for n in range(2, 2 * KD):
            split.high(act, b1 + n, cols=HALF)

    def vector(dve):
        norm.vector(dve)

        def up(i, s):
            dve.wait_ge(gated.sem, gated.of(s) + 4 * i)
            chip.wait_tile(dve, b0 + s, 1, i)
            dve.tensor_tensor(prod[:, s % 2, :], silu[:, (u0 + s) % 2, :], chip.pair(u0 + s)[1][:, :], ALU.mult)\
               .then_inc(product.sem, 1)
            dve.wait_ge(rounded.sem, rounded.of(s) + 4 * i)
            dve.sem_inc(chip.pair_free[(u0 + s) % 2], 2)
            dve.tensor_tensor(at(hid_low, 4 * i + s), one(prod[:, s % 2, :]),
                              at(hid_high, 4 * i + s).bitcast(F32), ALU.subtract).then_inc(rest.sem, 1)
        by_four(dve, KF, up)
        for n in range(KD):
            dve.wait_ge(chip.gemm_done, 2 * (b1 + 2 * n + 2))
            dve.scalar_tensor_tensor(out=chip.x[:, n, :], in0=chip.pair(u1 + n // 2)[n % 2][:, :],
                                     scalar=chip.mod[:, m + 40 + n:m + 41 + n], in1=chip.x[:, n, :],
                                     op0=ALU.mult, op1=ALU.add)\
               .then_inc(chip.pair_free[(u1 + n // 2) % 2], 1)

    def gpsimd(pool):
        for b in range(2):
            split.low(pool, b0 + b)
        by_four(pool, KF, lambda i, s: split.low(pool, b0 + s + 2, i))
        for n in range(2, 2 * KD):
            split.low(pool, b1 + n, cols=HALF)

    return tensor, scalar, vector, gpsimd




def mlstm(chip):
    m = 48
    H = ML_HEADS
    ST = T // P
    h, h_high, h_low = chip.keep_pair("h", [P, KD, T])
    m_all = chip.over("m_all", [P, H, T], F32, chip.top - 4 * KD * T)
    qk = chip.keep("qk", [P, KD, T])
    v = chip.keep("v_tok", [P, ST, D])
    og = chip.keep("o_gate", [P, KD, T])
    pad = chip.keep("conv_in", [P, 2, T + CONV_W - 1])
    conv = chip.keep("conv_out", [P, 2, T])
    rows = chip.keep("gate_rows", [H, 5, T])
    li, lf, ee, mm_, en_m = (rows[:, n, :] for n in range(5))
    gb = chip.keep("gate_bias", [H, 2])
    ones_row = chip.keep("ones_row", [H, T])
    ecol = chip.keep("e_col", [P, ST, H])
    enm_all = chip.keep("exp_neg_m", [P, H, T])
    dd = chip.keep("weights", [P, ST, T])
    z = h
    norm = Norm(chip, lambda k: chip.x[:, k, :], lambda k: h[:, k, :], KD,
                lambda k: chip.mod[:, m + 8 + k:m + 9 + k], lambda k: chip.mod[:, m + k:m + k + 1],
                high=lambda k: h_high[:, k, :], low=lambda k: h_low[:, k, :])
    b_qk, u_qk = chip.take_blocks(4), chip.take_groups(4)
    b_g, u_g = chip.take_blocks(1), chip.take_groups(1)
    b_v, u_v = chip.take_blocks(4), chip.take_groups(4)
    b_o, u_o = chip.take_blocks(4), chip.take_groups(4)
    b_w, u_w = chip.take_blocks(4), chip.take_groups(4)
    split = Split(chip, b_qk, 17)
    z_mul, z_rounded = Step(chip, "ml_z_product", H), Step(chip, "ml_z_rounded", H)
    padded, taps, qk_ready = Step(chip, "ml_padded", 2), Step(chip, "ml_taps", 4 * KD), Step(chip, "ml_qk", KD)
    gate = Step(chip, "ml_gate", 6)
    gate_v = Step(chip, "ml_gate_v", 4)
    ecol_mm, ecol_ready = Step(chip, "ml_ecol_mm", ST), Step(chip, "ml_ecol", ST)
    bc_mm, bc_ready = Step(chip, "ml_bc_mm", 2 * H), Step(chip, "ml_bc", 2 * H)
    s_mm = Step(chip, "ml_s_mm", H * ST)
    gap, ex, tri, wt = (Step(chip, "ml_" + n, H * ST) for n in ("gap", "exp", "tri", "weight"))
    nd_mm, fin, sq, ms_mm, root = Step(chip, "ml_nd", H), Step(chip, "ml_fin", 4 * H), Step(chip, "ml_sq", H), \
        Step(chip, "ml_ms", H), Step(chip, "ml_root", H)
    z_ready = Step(chip, "ml_z", H)

    def part(hd):
        return slice(64 * (hd % 2), 64 * (hd % 2) + 64)

    def tensor(pe):
        norm.tensor(pe)

        def parts(k):
            return h_high[:, k, :], h_low[:, k, :]

        chip.pe_features(pe, b_qk, u_qk, 1, KD, parts, split=split, before=lambda k: norm.wait(pe, k))
        chip.pe_features(pe, b_qk + 1, u_qk + 1, 3, KD, parts, split=split)
        split.wait(pe, b_g)
        chip.wait_pair(pe, u_g)
        for j in range(2):
            for k in range(KD):
                mm = three(pe, chip.pair(u_g)[j][0:2 * H, :], split.parts(b_g, KD, 2 * P), k,
                           slice(j * H, (j + 2) * H), parts(k), k == 0, k == KD - 1)
            mm.then_inc(chip.gemm_done, 1)
        chip.pe_tokens(pe, b_v, u_v, 4, KD, parts, split=split)
        chip.pe_features(pe, b_o, u_o, 4, KD, parts, split=split)
        pe.wait_ge(gate_v.sem, gate_v.of(3))
        for n in range(ST):
            pe.matmul(chip.bank[4][:, n * H:(n + 1) * H], ee[:, n * P:(n + 1) * P], chip.ident[0:H, 0:H],
                      start=True, stop=True).then_inc(ecol_mm.sem, 1)
        pe.wait_ge(gate.sem, gate.of(5))
        for hd in range(H):
            for n, row in enumerate((mm_, en_m)):
                c = 2 * hd + n
                if c >= 2:
                    pe.wait_ge(bc_ready.sem, bc_ready.of(c - 2))
                pe.matmul(chip.bank[5 + n][:, :], chip.ident[0:H, hd:hd + 1].to_broadcast([H, P]), row,
                          start=True, stop=True).then_inc(bc_mm.sem, 1)
        chip.wait_pair(pe, u_w)
        chip.wait_pair(pe, u_w + 1)
        pe.wait_ge(bc_ready.sem, bc_ready.of(2 * H - 1))
        pe.wait_ge(ecol_ready.sem, ecol_ready.of(0))
        pe.wait_ge(qk_ready.sem, qk_ready.of(KD - 1))

        def scores(hd):
            for i in range(ST):
                n = hd * ST + i
                if hd:
                    pe.wait_ge(wt.sem, wt.of(n - ST))
                pe.matmul(chip.bank[i][:, i * P:T], qk[part(hd), 4 + hd // 2, i * P:(i + 1) * P],
                          qk[part(hd), hd // 2, i * P:T], start=True, stop=True).then_inc(s_mm.sem, 1)

        def sums(hd):
            num, den = chip.bank[4 + 2 * (hd % 2)], chip.bank[5 + 2 * (hd % 2)]
            if hd >= 2:
                pe.wait_ge(z_mul.sem, z_mul.of(hd - 2))
            for i in range(ST):
                pe.wait_ge(wt.sem, wt.of(hd * ST + i))
                pe.matmul(num[:, i * P:T], v[:, i, hd * P:(hd + 1) * P], dd[:, i, i * P:T],
                          start=(i == 0), stop=(i == ST - 1))
                mm = pe.matmul(den[:, i * P:T], chip.ones[:, :], dd[:, i, i * P:T],
                               start=(i == 0), stop=(i == ST - 1))
            mm.then_inc(nd_mm.sem, 1)

        def mean_square(hd):
            pe.wait_ge(sq.sem, sq.of(hd))
            pe.matmul(chip.bank[5 + 2 * (hd % 2)][:, :], chip.ones[:, :], conv[:, hd % 2, :],
                      start=True, stop=True).then_inc(ms_mm.sem, 1)

        scores(0)
        for hd in range(H):
            sums(hd)
            if hd + 1 < H:
                scores(hd + 1)
            mean_square(hd)
        chip.pe_features(pe, b_w, u_w, 4, KD, parts, split=split,
                         before=lambda k: pe.wait_ge(z_ready.sem, z_ready.of(k)))

    def scalar(act):
        norm.scalar(act)
        split.high(act, b_qk)
        split.high(act, b_qk + 1)
        for n in range(KD):
            chip.wait_tile(act, b_qk + n // 2, n % 2)
            if n >= 2:
                act.wait_ge(taps.sem, taps.of(4 * (n - 2) + 3))
            u = u_qk + n // 2
            if n == 0:
                act.wait_ge(padded.sem, padded.of(0))
            act.activation(pad[:, n % 2, CONV_W - 1:], chip.pair(u)[n % 2][:, :], ACT.Copy)\
               .then_inc(chip.pair_free[u % 2], 1)
            act.wait_ge(taps.sem, taps.of(4 * n + 3))
            act.activation(qk[:, n, :], conv[:, n % 2, :], ACT.Silu, bias=chip.v("conv_b")[:, n:n + 1])\
               .then_inc(qk_ready.sem, 1)
            if n % 2:
                split.high(act, b_qk + n // 2 + 2)
        act.activation(gb[:, :], chip.v("gate_b")[0:H, :], ACT.Copy, scale=1.0 / GATE_CAP).then_inc(gate.sem, 1)
        act.wait_ge(gate.sem, gate.of(0))
        for j, row in enumerate((li, lf)):
            chip.wait_tile(act, b_g, j)
            act.activation(row, chip.pair(u_g)[j][0:H, :], ACT.Tanh, bias=gb[:, j:j + 1],
                           scale=1.0 / GATE_CAP).then_inc(gate.sem, 1)
        act.wait_ge(gate.sem, gate.of(2))
        act.sem_inc(chip.pair_free[u_g % 2], 2)
        split.high(act, b_g + 2)
        act.activation(lf, lf, ACT.Exp, scale=-GATE_CAP).then_inc(gate.sem, 1)
        act.wait_ge(gate.sem, gate.of(3))
        act.activation(lf, lf, ACT.Ln, bias=chip.ones[0:H, 0:1]).then_inc(gate.sem, 1)
        for s in range(4):
            for j in range(2):
                chip.wait_tile(act, b_v + s, j)
                act.activation(v[:, 2 * j:2 * j + 2, s * 2 * P:(s + 1) * 2 * P],
                               chip.pair(u_v + s)[j][:, :].rearrange("p (a n) -> p a n", a=2), ACT.Copy)\
                   .then_inc(chip.pair_free[(u_v + s) % 2], 1)
            split.high(act, b_v + s + 2)
        act.wait_ge(gate_v.sem, gate_v.of(3))
        act.activation(en_m, li, ACT.Exp, scale=-1.0).then_inc(gate.sem, 1)
        for n in range(KD):
            chip.wait_tile(act, b_o + n // 2, n % 2)
            u = u_o + n // 2
            act.activation(og[:, n, :], chip.pair(u)[n % 2][:, :], ACT.Sigmoid).then_inc(chip.pair_free[u % 2], 1)
            if n % 2:
                split.high(act, b_o + n // 2 + 2)
        for hd in range(H):
            for n, dst in enumerate((m_all, enm_all)):
                act.wait_ge(bc_mm.sem, bc_mm.of(2 * hd + n))
                act.activation(dst[:, hd, :], chip.bank[5 + n][:, :], ACT.Copy).then_inc(bc_ready.sem, 1)

        def finish(hd):
            act.wait_ge(fin.sem, fin.of(4 * hd + 2))
            if hd >= 2:
                act.wait_ge(ms_mm.sem, ms_mm.of(hd - 2))
            act.activation(conv[:, hd % 2, :], z[:, hd, :], ACT.Square).then_inc(sq.sem, 1)
            act.wait_ge(ms_mm.sem, ms_mm.of(hd))
            act.activation(enm_all[:, hd, :], chip.bank[5 + 2 * (hd % 2)][:, :], ACT.Sqrt,
                           bias=chip.eps[:, :], scale=1.0 / ML_V).then_inc(root.sem, 1)

        def round_z(hd):
            act.wait_ge(z_mul.sem, z_mul.of(hd))
            act.activation(h_high[:, hd, :], z[:, hd, :], ACT.Copy).then_inc(z_rounded.sem, 1)

        for hd in range(H):
            for i in range(ST):
                act.wait_ge(gap.sem, gap.of(hd * ST + i))
                act.activation(dd[:, i, i * P:T], dd[:, i, i * P:T], ACT.Exp, scale=-1.0).then_inc(ex.sem, 1)
            if hd:
                finish(hd - 1)
            if hd >= 2:
                round_z(hd - 2)
        finish(H - 1)
        round_z(H - 2)
        round_z(H - 1)
        for n in range(2, 4):
            split.high(act, b_w + n)

    def vector(dve):
        norm.vector(dve)
        dve.memset(pad[:, :, 0:CONV_W - 1], 0.0).then_inc(padded.sem, 1)
        dve.memset(ones_row[:, :], 1.0).then_inc(padded.sem, 1)
        for n in range(KD):
            u = u_qk + n // 2
            dve.wait_ge(chip.pair_free[u % 2], 2 * (u // 2) + n % 2 + 1)
            if n >= 2:
                dve.wait_ge(qk_ready.sem, qk_ready.of(n - 2))
            for j in range(CONV_W):
                w = chip.v("conv_w")[:, j * KD + n:j * KD + n + 1]
                src, dst = pad[:, n % 2, j:j + T], conv[:, n % 2, :]
                if j == 0:
                    dve.tensor_scalar(dst, src, w, None, ALU.mult).then_inc(taps.sem, 1)
                else:
                    dve.wait_ge(taps.sem, taps.of(4 * n + j - 1))
                    dve.scalar_tensor_tensor(out=dst, in0=src, scalar=w, in1=dst, op0=ALU.mult, op1=ALU.add)\
                       .then_inc(taps.sem, 1)
        dve.wait_ge(gate.sem, gate.of(4))
        dve.wait_ge(padded.sem, padded.of(1))
        dve.tensor_tensor_scan(mm_, ones_row[:, :], lf, 0.0, ALU.mult, ALU.subtract)\
           .then_inc(gate_v.sem, 1)
        dve.wait_ge(gate_v.sem, gate_v.of(0))
        dve.scalar_tensor_tensor(out=ee, in0=li, scalar=GATE_CAP, in1=mm_, op0=ALU.mult, op1=ALU.subtract)\
           .then_inc(gate_v.sem, 1)
        dve.tensor_copy(lf, mm_).then_inc(gate_v.sem, 1)
        dve.wait_ge(gate_v.sem, gate_v.of(2))
        dve.tensor_tensor_scan(mm_, ee, ee, 0.0, ALU.max, ALU.max).then_inc(gate_w.sem, 1)
        dve.wait_ge(gate_w.sem, gate_w.of(0))
        dve.tensor_tensor(li, lf, mm_, ALU.add).then_inc(gate_v.sem, 1)
        dve.wait_ge(ecol_mm.sem, ecol_mm.of(ST - 1))
        dve.tensor_copy(ecol[:, :, :], chip.bank[4][:, 0:ST * H].rearrange("p (a n) -> p a n", a=ST))\
           .then_inc(ecol_ready.sem, ST)

        def gaps(hd):
            if hd == 0:
                dve.wait_ge(ecol_ready.sem, ecol_ready.of(0))
            dve.wait_ge(bc_ready.sem, bc_ready.of(2 * hd))
            if hd:
                dve.wait_ge(nd_mm.sem, nd_mm.of(hd - 1))
            for i in range(ST):
                dve.tensor_scalar(dd[:, i, i * P:T], m_all[:, hd, i * P:T], ecol[:, i, hd:hd + 1], 0.0,
                                  ALU.subtract, ALU.max).then_inc(gap.sem, 1)

        def weights(hd):
            for i in range(ST):
                n = hd * ST + i
                dve.wait_ge(tri.sem, tri.of(n))
                dve.wait_ge(s_mm.sem, s_mm.of(n))
                dve.scalar_tensor_tensor(out=dd[:, i, i * P:T], in0=chip.bank[i][:, i * P:T],
                                         scalar=float(ML_QK) ** -0.5, in1=dd[:, i, i * P:T],
                                         op0=ALU.mult, op1=ALU.mult).then_inc(wt.sem, 1)

        def divide(hd):
            num, den = chip.bank[4 + 2 * (hd % 2)], chip.bank[5 + 2 * (hd % 2)]
            dve.wait_ge(nd_mm.sem, nd_mm.of(hd))
            dve.wait_ge(bc_ready.sem, bc_ready.of(2 * hd + 1))
            t = enm_all[:, hd, :]
            dve.scalar_tensor_tensor(out=t, in0=den[:, :], scalar=-1.0, in1=t, op0=ALU.mult, op1=ALU.max)\
               .then_inc(floor_.sem, 1)
            dve.wait_ge(floor_.sem, floor_.of(hd))
            dve.tensor_tensor(t, den[:, :], t, ALU.max).then_inc(fin.sem, 1)
            dve.wait_ge(fin.sem, fin.of(4 * hd))
            dve.reciprocal(t, t).then_inc(fin.sem, 1)
            dve.wait_ge(fin.sem, fin.of(4 * hd + 1))
            dve.tensor_tensor(z[:, hd, :], num[:, :], t, ALU.mult).then_inc(fin.sem, 1)

        def finish(hd):
            t = enm_all[:, hd, :]
            dve.wait_ge(root.sem, root.of(hd))
            dve.reciprocal(t, t).then_inc(fin.sem, 1)
            dve.wait_ge(fin.sem, fin.of(4 * hd + 3))
            dve.scalar_tensor_tensor(out=z[:, hd, :], in0=z[:, hd, :], scalar=chip.v("hn_w")[:, hd:hd + 1],
                                     in1=t, op0=ALU.mult, op1=ALU.mult).then_inc(zn.sem, 1)
            dve.wait_ge(zn.sem, zn.of(hd))
            dve.tensor_tensor(z[:, hd, :], z[:, hd, :], og[:, hd, :], ALU.mult).then_inc(z_mul.sem, 1)

        def rest_z(hd):
            dve.wait_ge(z_rounded.sem, z_rounded.of(hd))
            dve.tensor_tensor(h_low[:, hd, :], z[:, hd, :], h_high[:, hd, :].bitcast(F32), ALU.subtract)\
               .then_inc(z_ready.sem, 1)

        gaps(0)
        weights(0)
        for hd in range(H):
            if hd + 1 < H:
                gaps(hd + 1)
            divide(hd)
            if hd + 1 < H:
                weights(hd + 1)
            finish(hd)
            if hd:
                rest_z(hd - 1)
        rest_z(H - 1)
        residual(chip, dve, b_w, u_w, lambda n: chip.mod[:, m + 16 + n:m + 17 + n])

    def gpsimd(pool):
        for n in range(15):
            split.low(pool, b_qk + n)
        for n in range(H * ST):
            i = n % ST
            pool.wait_ge(ex.sem, ex.of(n))
            part_ = dd[:, i, i * P:(i + 1) * P]
            pool.affine_select(out=part_, in_=part_, compare_op=ALU.is_ge, fill=0.0, base=0,
                               pattern=[[1, P]], channel_multiplier=-1).then_inc(tri.sem, 1)
        for n in range(2, 4):
            split.low(pool, b_w + n)

    floor_ = Step(chip, "ml_floor", H)
    gate_w, zn = Step(chip, "ml_running_max", 1), Step(chip, "ml_zn", H)
    return tensor, scalar, vector, gpsimd


def final_norm(chip):
    sq = chip.keep("sq", [P, KD, T])
    norm = Norm(chip, lambda k: chip.x[:, k, :], lambda k: chip.x[:, k, :], KD,
                lambda k: chip.v("final_w")[:, k:k + 1], squares=lambda k: sq[:, k, :])
    return norm.tensor, norm.scalar, norm.vector, None


TWO_PI_1 = 6.28125
TWO_PI_2 = 0.0019350051879882812
TWO_PI_3 = 2 * np.pi - TWO_PI_1 - TWO_PI_2
ROUND = 12582912.0


class Rope:

    def __init__(self, chip, column):
        self.chip, self.column = chip, column
        self.ang, self.turns = chip.keep("angle", [P, T]), chip.keep("turns", [P, T])
        self.pos = chip.over("positions", [P, T], I32, chip.top)
        self.cos, self.sin = chip.keep("cos", [P, T]), chip.keep("sin", [P, T])
        self.pos_ready = Load(chip)
        self.reduced = Step(chip, "rope_reduced", 8)
        self.sines = Step(chip, "rope_sines", 3)
        self.ready = Step(chip, "rope_ready", 1)

    def load(self, act):
        act.dma_start(self.pos[:, :], self.chip.io["pos"].to_broadcast([P, T])).then_inc(self.pos_ready.sem, 16)

    def scalar(self, act):
        r, s = self.reduced, self.sines
        act.wait_ge(r.sem, r.of(7))
        act.activation(self.sin[:, :], self.ang[:, :], ACT.Sin).then_inc(s.sem, 1)
        act.activation(self.turns[:, :], self.ang[:, :], ACT.Sin, scale=0.5).then_inc(s.sem, 1)
        act.wait_ge(s.sem, s.of(1))
        act.activation(self.turns[:, :], self.turns[:, :], ACT.Square).then_inc(s.sem, 1)

    def vector(self, dve):
        r, ang, n = self.reduced, self.ang[:, :], self.turns[:, :]
        freq = self.chip.k("inv_freq")[:, self.column:self.column + 1]
        dve.wait_ge(self.pos_ready.sem, self.pos_ready.landed)
        dve.tensor_copy(n, self.pos[:, :]).then_inc(r.sem, 1)
        dve.wait_ge(r.sem, r.of(0))
        dve.tensor_scalar(ang, n, freq, None, ALU.mult).then_inc(r.sem, 1)
        dve.wait_ge(r.sem, r.of(1))
        dve.tensor_scalar(n, ang, 1.0 / (2 * np.pi), ROUND, ALU.mult, ALU.add).then_inc(r.sem, 1)
        dve.wait_ge(r.sem, r.of(2))
        dve.tensor_scalar(n, n, ROUND, None, ALU.subtract).then_inc(r.sem, 1)
        for q, part in enumerate((TWO_PI_1, TWO_PI_2, TWO_PI_3)):
            dve.wait_ge(r.sem, r.of(3 + q))
            dve.scalar_tensor_tensor(out=ang, in0=n, scalar=-part, in1=ang, op0=ALU.mult, op1=ALU.add)\
               .then_inc(r.sem, 1)
        dve.wait_ge(r.sem, r.of(6))
        dve.tensor_scalar(ang, ang, 3.1415925, -3.1415925, ALU.min, ALU.max).then_inc(r.sem, 1)
        dve.wait_ge(self.sines.sem, self.sines.of(2))
        dve.tensor_scalar(self.cos[:, :], n, -2.0, 1.0, ALU.mult, ALU.add).then_inc(self.ready.sem, 1)

    def wait(self, eng):
        eng.wait_ge(self.ready.sem, self.ready.of(0))


class PostNorm:

    def __init__(self, chip, y, squares, layer, b0, u0, rstd=None):
        self.chip, self.y, self.b0, self.u0 = chip, y, b0, u0
        self.y_ready = Step(chip, "post_y", KD)
        self.added = Step(chip, "post_added", KD)
        self.norm = Norm(chip, lambda k: y[:, k, :], lambda k: y[:, k, :], KD,
                         lambda k: chip.v("post_g")[:, layer * KD + k:layer * KD + k + 1],
                         squares=lambda k: squares[:, k, :], rstd=rstd)

    def scalar(self, act, split=None):
        for n in range(KD):
            u = self.u0 + n // 2
            act.wait_ge(self.chip.gemm_done, 2 * (self.b0 + n + 1))
            act.activation(self.y[:, n, :], self.chip.pair(u)[n % 2][:, :], ACT.Copy)\
               .then_inc(self.y_ready.sem, 1)
            act.wait_ge(self.y_ready.sem, self.y_ready.of(n))
            act.sem_inc(self.chip.pair_free[u % 2], 1)
            if split and n < KD - 2:
                split.high(act, self.b0 + n + 2)
        self.norm.scalar(act)

    def vector(self, dve):
        self.norm.vector(dve)
        for n in range(KD):
            self.norm.wait(dve, n)
            dve.tensor_tensor(self.chip.x[:, n, :], self.chip.x[:, n, :], self.y[:, n, :], ALU.add)\
               .then_inc(self.added.sem, 1)


def retention(chip):
    ST, RH = T // P, RET_HEADS
    VT = RET_V // P
    h_offset = chip.top
    h, h_high = chip.keep("h", [P, KD, T]), chip.keep("h_high", [P, KD, T], F32R)
    h_low = chip.over("h_low", [P, KD, T], F32R, h_offset)
    z_high = chip.over("z_high", [P, 2 * KD, T], F32R, h_offset)
    z_offset = chip.top
    z = chip.keep("z", [P, 2 * KD, T])
    z_low = chip.over("z_low", [P, 2 * KD, T], F32R, z_offset)
    qk_offset = chip.top
    q, k = chip.keep("q", [P, 4, T]), chip.keep("k", [P, 4, T])
    y = chip.over("y", [P, KD, T], F32, qk_offset)
    v_offset = chip.top
    v = chip.keep("v_tok", [P, ST, 2 * RET_V])
    y_sq = chip.over("y_squared", [P, KD, T], F32, v_offset)
    fall = chip.keep("decay", [P, RH, T])
    weight = chip.keep("weights", [P, ST, T])
    rope = Rope(chip, 0)
    turn_offset = chip.top
    turn = chip.keep("turned", [P, 4, T])
    sq = chip.over("o_squared", [P, VT, T], F32, turn_offset)
    rstd = rope.ang
    norm = Norm(chip, lambda n: chip.x[:, n, :], lambda n: h[:, n, :], KD,
                lambda n: chip.v("pre_g")[:, n:n + 1], rstd=rstd, high=lambda n: h_high[:, n, :],
                low=lambda n: h_low[:, n, :])
    b_g, u_g = chip.take_blocks(8), chip.take_groups(8)
    pairs = [(chip.take_blocks(8), chip.take_groups(8)) for _ in range(2)]
    b_o, u_o = chip.take_blocks(8), chip.take_groups(4)
    split = Split(chip, b_g, b_o + 8 - b_g)
    fall_ready = Load(chip)
    turned, roped = Step(chip, "ret_turned", 4 * 8), Step(chip, "ret_roped", 16)
    silu, v_ready = Step(chip, "ret_silu", 16), Step(chip, "ret_v", 16)
    s_mm, wt = Step(chip, "ret_scores", RH * ST), Step(chip, "ret_weight", RH * ST)
    o_mm, sq_done, ms_mm = Step(chip, "ret_o", RH * VT), Step(chip, "ret_sq", RH * VT), Step(chip, "ret_ms", RH)
    root, recip = Step(chip, "ret_root", RH), Step(chip, "ret_rstd", RH)
    scaled, z_ready = Step(chip, "ret_scaled", RH * VT), Step(chip, "ret_z", RH * VT)
    z_rounded, z_rest = Step(chip, "ret_z_rounded", RH * VT), Step(chip, "ret_z_rest", RH * VT)
    post = PostNorm(chip, y, y_sq, 0, b_o, u_o, rstd=rstd)

    def tensor(pe):
        def h_parts(n):
            return h_high[:, n, :], h_low[:, n, :]

        def scores(hd):
            for i in range(ST):
                n = hd * ST + i
                if n >= 2:
                    pe.wait_ge(wt.sem, wt.of(n - 2))
                for a in range(2):
                    mm = pe.matmul(chip.bank[i % 2][:, i * P:T], k[:, 2 * (hd % 2) + a, i * P:(i + 1) * P],
                                   q[:, 2 * (hd % 2) + a, i * P:T], start=(a == 0), stop=(a == 1))
                mm.then_inc(s_mm.sem, 1)

        def outs(hd):
            pe.wait_ge(wt.sem, wt.of(hd * ST + ST - 1))
            for j in range(VT):
                if hd:
                    pe.wait_ge(scaled.sem, scaled.of((hd - 1) * VT + j))
                for i in range(ST):
                    col = (hd % 2) * RET_V + j * P
                    mm = pe.matmul(chip.bank[4 + j][:, i * P:T], v[:, i, col:col + P], weight[:, i, i * P:T],
                                   start=(i == 0), stop=(i == ST - 1))
                mm.then_inc(o_mm.sem, 1)

        def mean_square(hd):
            for j in range(VT):
                pe.wait_ge(sq_done.sem, sq_done.of(hd * VT + j))
                mm = pe.matmul(chip.bank[2][:, :], chip.ones[:, :], sq[:, j, :],
                               start=(j == 0), stop=(j == VT - 1))
            mm.then_inc(ms_mm.sem, 1)

        norm.tensor(pe)
        chip.pe_features(pe, b_g, u_g, 8, KD, h_parts, before=lambda n: norm.wait(pe, n), split=split)
        for pair, (b, u) in enumerate(pairs):
            if pair:
                pe.wait_ge(root.sem, root.of(1))
            chip.pe_features(pe, b, u, 4, KD, h_parts, split=split)
            chip.pe_tokens(pe, b + 4, u + 4, 4, KD, h_parts, split=split)
            chip.wait_pair(pe, u + 8)
            chip.wait_pair(pe, u + 9)
            pe.wait_ge(roped.sem, roped.of(8 * pair + 7))
            pe.wait_ge(v_ready.sem, v_ready.of(8 * pair + 7))
            scores(2 * pair)
            outs(2 * pair)
            scores(2 * pair + 1)
            mean_square(2 * pair)
            outs(2 * pair + 1)
            mean_square(2 * pair + 1)
        pe.wait_ge(root.sem, root.of(RH - 1))
        for r in range(4):
            chip.wait_pair(pe, u_o + r)
            for tile in range(2):
                b = b_o + 2 * r + tile
                split.wait(pe, b)
                parts = split.parts(b, 2 * KD, P)
                for n in range(2 * KD):
                    if b == b_o:
                        pe.wait_ge(z_rest.sem, z_rest.of(n))
                    mm = three(pe, chip.pair(u_o + r)[tile][:, :], parts, n, slice(0, P),
                               (z_high[:, n, :], z_low[:, n, :]), n == 0, n == 2 * KD - 1)
                mm.then_inc(chip.gemm_done, 2)
        post.norm.tensor(pe)

    def scalar(act):
        rope.load(act)
        act.dma_start(fall[:, :, :], chip.io["ret_decay"].rearrange("p (h t) -> p h t", h=RH))\
           .then_inc(fall_ready.sem, 16)
        split.high(act, b_g)
        split.high(act, b_g + 1)
        norm.scalar(act)
        rope.scalar(act)
        for n in range(16):
            chip.wait_tile(act, b_g + n // 2, n % 2)
            u = u_g + n // 2
            act.activation(z[:, n, :], chip.pair(u)[n % 2][:, :], ACT.Silu).then_inc(silu.sem, 1)
            act.wait_ge(silu.sem, silu.of(n))
            act.sem_inc(chip.pair_free[u % 2], 1)
            if n % 2:
                split.high(act, b_g + n // 2 + 2)

        def round_z(hd):
            for n in range(hd * VT, (hd + 1) * VT):
                act.wait_ge(z_ready.sem, z_ready.of(n))
                act.activation(z_high[:, n, :], z[:, n, :], ACT.Copy).then_inc(z_rounded.sem, 1)

        for pair, (b, u) in enumerate(pairs):
            for n in range(2, 6):
                split.high(act, b + n)
            for n in range(4):
                for j in range(2):
                    m = 8 * pair + 2 * n + j
                    chip.wait_tile(act, b + 4 + n, j)
                    act.activation(v[:, 2 * j:2 * j + 2, n * 2 * P:(n + 1) * 2 * P],
                                   chip.pair(u + 4 + n)[j][:, :].rearrange("p (a n) -> p a n", a=2), ACT.Copy)\
                       .then_inc(v_ready.sem, 1)
                    act.wait_ge(v_ready.sem, v_ready.of(m))
                    act.sem_inc(chip.pair_free[(u + 4 + n) % 2], 1)
                split.high(act, b + 6 + n)
            if pair:
                round_z(0)
                round_z(1)
            for hd in (2 * pair, 2 * pair + 1):
                for j in range(VT):
                    n = hd * VT + j
                    act.wait_ge(o_mm.sem, o_mm.of(n))
                    if hd:
                        act.wait_ge(z_ready.sem, z_ready.of(n - VT))
                    act.activation(sq[:, j, :], chip.bank[4 + j][:, :], ACT.Square).then_inc(sq_done.sem, 1)
                act.wait_ge(ms_mm.sem, ms_mm.of(hd))
                if hd:
                    act.wait_ge(scaled.sem, scaled.of(hd * VT - 1))
                act.activation(rstd[:, :], chip.bank[2][:, :], ACT.Sqrt, bias=chip.eps[:, :],
                               scale=1.0 / RET_V).then_inc(root.sem, 1)
        round_z(2)
        round_z(3)
        post.scalar(act, split=split)

    def gpsimd(pool):
        for b in range(b_g, b_o + 2):
            split.low(pool, b)
        for n in range(RH * VT):
            pool.wait_ge(z_rounded.sem, z_rounded.of(n))
            pool.tensor_tensor(z_low[:, n, :], z[:, n, :], z_high[:, n, :].bitcast(F32), ALU.subtract)\
                .then_inc(z_rest.sem, 1)
        for b in range(b_o + 2, b_o + 8):
            split.low(pool, b)

    def vector(dve):
        norm.vector(dve)
        rope.vector(dve)
        rope.wait(dve)

        def rope_pair(pair):
            b, u = pairs[pair]
            for m in range(4):
                n = 4 * pair + m
                x1, x2 = chip.pair(u + m)[0][:, :], chip.pair(u + m)[1][:, :]
                dst = q if m < 2 else k
                chip.wait_tile(dve, b + m, 1)
                if n:
                    dve.wait_ge(roped.sem, roped.of(2 * n - 1))
                for r, (a, f) in enumerate(((x1, rope.cos), (x2, rope.sin), (x2, rope.cos), (x1, rope.sin))):
                    dve.tensor_tensor(turn[:, r, :], a, f[:, :], ALU.mult).then_inc(turned.sem, 1)
                dve.wait_ge(turned.sem, turned.of(4 * n + 3))
                dve.sem_inc(chip.pair_free[(u + m) % 2], 2)
                for a, op in enumerate((ALU.subtract, ALU.add)):
                    dve.tensor_tensor(dst[:, 2 * (m % 2) + a, :], turn[:, 2 * a, :], turn[:, 2 * a + 1, :], op)\
                       .then_inc(roped.sem, 1)

        def weights(hd):
            for i in range(ST):
                n = hd * ST + i
                dve.wait_ge(s_mm.sem, s_mm.of(n))
                if hd and i == 0:
                    dve.wait_ge(o_mm.sem, o_mm.of(hd * VT - 1))
                dve.scalar_tensor_tensor(out=weight[:, i, i * P:T], in0=chip.bank[i % 2][:, i * P:T],
                                         scalar=float(RET_QK) ** -0.5, in1=fall[:, hd, 0:T - i * P],
                                         op0=ALU.mult, op1=ALU.mult).then_inc(wt.sem, 1)

        def finish(hd):
            dve.wait_ge(root.sem, root.of(hd))
            dve.reciprocal(rstd[:, :], rstd[:, :]).then_inc(recip.sem, 1)
            dve.wait_ge(recip.sem, recip.of(hd))
            for j in range(VT):
                n = hd * VT + j
                dve.scalar_tensor_tensor(out=turn[:, j, :], in0=chip.bank[4 + j][:, :],
                                         scalar=chip.v("ret_gn")[:, n:n + 1], in1=rstd[:, :],
                                         op0=ALU.mult, op1=ALU.mult).then_inc(scaled.sem, 1)
                dve.wait_ge(scaled.sem, scaled.of(n))
                dve.tensor_tensor(z[:, n, :], z[:, n, :], turn[:, j, :], ALU.mult).then_inc(z_ready.sem, 1)

        for pair in range(2):
            if pair:
                dve.wait_ge(z_ready.sem, z_ready.of(2 * VT - 1))
            rope_pair(pair)
            if pair == 0:
                dve.wait_ge(fall_ready.sem, fall_ready.landed)
            weights(2 * pair)
            weights(2 * pair + 1)
            finish(2 * pair)
            finish(2 * pair + 1)
        post.vector(dve)

    return tensor, scalar, vector, gpsimd


def ple(chip, layer):
    p_in = chip.keep("ple_in", [P, 2, T])
    pp = chip.keep("ple_proj", [P, KD, T])
    sig = chip.keep("ple_gate", [P, 2, T])
    b_p, u_p = chip.take_blocks(1), chip.take_groups(4)
    b_g, u_g = chip.take_blocks(4), chip.take_groups(4)
    x_high, x_low = (chip.keep("x_" + n, [P, KD, T], F32R) for n in ("high", "low"))
    split = Split(chip, b_g, 4)
    x_rounded, x_rest = Step(chip, "ple_x_rounded", KD), Step(chip, "ple_x_rest", KD)
    loaded = Load(chip)
    proj, copied, gate = Step(chip, "ple_proj_mm", KD - 1), Step(chip, "ple_copied", KD), Step(chip, "ple_gate", KD)
    prod, added = Step(chip, "ple_product", KD), Step(chip, "ple_added", KD)

    def tensor(pe):
        pe.wait_ge(loaded.sem, loaded.landed)
        chip.wait_block(pe, b_p)
        w = chip.ring[:, b_p % SLOTS, :].rearrange("p (k n) -> p k n", k=2)
        for n in range(KD):
            if n % 2 == 0:
                chip.wait_pair(pe, u_p + n // 2)
            for k in range(2):
                mm = pe.matmul(chip.pair(u_p + n // 2)[n % 2][:, :], w[:, k, n * P:(n + 1) * P], p_in[:, k, :],
                               start=(k == 0), stop=(k == 1))
            if n < KD - 1:
                mm.then_inc(proj.sem, 1)
        mm.then_inc(chip.gemm_done, 2)
        pe.wait_ge(x_rest.sem, x_rest.of(KD - 1))
        chip.pe_features(pe, b_g, u_g, 4, KD, lambda k: (x_high[:, k, :], x_low[:, k, :]), split=split)

    def scalar(act):
        act.dma_start(p_in[:, :, :], chip.io["p"][layer].rearrange("(k p) t -> p k t", p=P))\
           .then_inc(loaded.sem, 16)
        for k in range(KD):
            act.activation(x_high[:, k, :], chip.x[:, k, :], ACT.Copy).then_inc(x_rounded.sem, 1)
        split.high(act, b_g)
        split.high(act, b_g + 1)
        for n in range(KD):
            if n < KD - 1:
                act.wait_ge(proj.sem, proj.of(n))
            else:
                act.wait_ge(chip.gemm_done, 2 * b_p + 2)
            u = u_p + n // 2
            act.activation(pp[:, n, :], chip.pair(u)[n % 2][:, :], ACT.Copy).then_inc(copied.sem, 1)
            act.wait_ge(copied.sem, copied.of(n))
            act.sem_inc(chip.pair_free[u % 2], 1)
        for n in range(KD):
            chip.wait_tile(act, b_g + n // 2, n % 2)
            if n >= 2:
                act.wait_ge(prod.sem, prod.of(n - 2))
            u = u_g + n // 2
            act.activation(sig[:, n % 2, :], chip.pair(u)[n % 2][:, :], ACT.Sigmoid).then_inc(gate.sem, 1)
            act.wait_ge(gate.sem, gate.of(n))
            act.sem_inc(chip.pair_free[u % 2], 1)
            if n in (1, 3):
                split.high(act, b_g + n // 2 + 2)

    def gpsimd(pool):
        for n in range(4):
            split.low(pool, b_g + n)

    def vector(dve):
        for k in range(KD):
            dve.wait_ge(x_rounded.sem, x_rounded.of(k))
            dve.tensor_tensor(x_low[:, k, :], chip.x[:, k, :], x_high[:, k, :].bitcast(F32), ALU.subtract)\
               .then_inc(x_rest.sem, 1)
        for n in range(KD):
            dve.wait_ge(gate.sem, gate.of(n))
            dve.tensor_tensor(pp[:, n, :], pp[:, n, :], sig[:, n % 2, :], ALU.mult).then_inc(prod.sem, 1)
        dve.wait_ge(prod.sem, prod.of(KD - 1))
        for n in range(KD):
            dve.tensor_tensor(chip.x[:, n, :], chip.x[:, n, :], pp[:, n, :], ALU.add).then_inc(added.sem, 1)

    return tensor, scalar, vector, gpsimd


def mla(chip):
    ST, H = T // P, MLA_HEADS
    SCALE = float(NOPE + ROPE) ** -0.5
    QT, CT = Q_LORA // P, KV_LORA // P
    h_offset = chip.top
    qn, kn = chip.keep("q_nope", [P, 4, T]), chip.keep("k_nope", [P, 4, T])
    h, h_low, y = (chip.over(n, [P, KD, T], dt, h_offset) for n, dt in (("h", F32), ("h_low", F32R), ("y", F32)))
    c_offset = chip.top
    c, c_high = chip.keep("latents", [P, QT + CT, T]), chip.keep("latents_high", [P, QT + CT, T], F32R)
    c_low = chip.over("latents_low", [P, QT + CT, T], F32R, c_offset)
    c_sq = chip.over("latents_squared", [P, QT + CT, T], F32, c_offset + 4 * (QT + CT) * T)
    z_high = chip.over("z_high", [P, H, T], F32R, c_offset)
    kz, qr = chip.keep("k_rope", [P, 2, T]), chip.keep("q_rope", [P, 2, T])
    v = chip.keep("v_tok", [P, ST, 4 * P])
    z_offset = chip.top
    z = chip.keep("z", [P, H, T])
    z_low = chip.over("z_low", [P, H, T], F32R, z_offset)
    rope = Rope(chip, 1)
    turn_offset = chip.top
    turn = chip.keep("turned", [P, 4, T])
    o = chip.over("o", [P, 4, T], F32, turn_offset)
    probs_offset = chip.top
    pr = chip.keep("probs", [P, ST, T])
    pt = chip.keep("probs_t", [P, ST, T])
    h_high, y_sq = (chip.over(n, [P, KD, T], dt, probs_offset) for n, dt in (("h_high", F32R), ("y_squared", F32)))
    small = chip.keep("softmax_cols", [P, 2, 4 * ST])
    norm = Norm(chip, lambda n: chip.x[:, n, :], lambda n: h[:, n, :], KD,
                lambda n: chip.v("pre_g")[:, KD + n:KD + n + 1], high=lambda n: h_high[:, n, :],
                low=lambda n: h_low[:, n, :])
    q_norm = Norm(chip, lambda n: c[:, n, :], lambda n: c[:, n, :], QT,
                  lambda n: chip.v("q_g")[:, n:n + 1], squares=lambda n: c_sq[:, n, :], rstd=norm.rstd,
                  high=lambda n: c_high[:, n, :], low=lambda n: c_low[:, n, :])
    kv_norm = Norm(chip, lambda n: c[:, QT + n, :], lambda n: c[:, QT + n, :], CT,
                   lambda n: chip.v("kv_g")[:, n:n + 1], squares=lambda n: c_sq[:, QT + n, :], rstd=rope.ang,
                   bank=5, high=lambda n: c_high[:, QT + n, :], low=lambda n: c_low[:, QT + n, :])
    b_c, u_c = chip.take_blocks(4), chip.take_groups(4)
    b_r, u_r = chip.take_blocks(1), chip.take_groups(1)
    b_g, u_g = chip.take_blocks(8), chip.take_groups(8)
    quarters = [(chip.take_blocks(4), chip.take_groups(7)) for _ in range(4)]
    b_o, u_o = chip.take_blocks(8), chip.take_groups(4)
    split = Split(chip, b_c, b_o + 8 - b_c)
    lat = Step(chip, "mla_latent", QT + CT)
    zeroed, k_rope = Step(chip, "mla_zeroed", 1), Step(chip, "mla_k_rope", 4)
    turned = Step(chip, "mla_turned", 4 * 5)
    q_rope = Step(chip, "mla_q_rope", 8 * 4)
    raised = Step(chip, "mla_raised", 4 * 12)
    up_mm = Step(chip, "mla_up_mm", 4 * 7)
    s_mm = Step(chip, "mla_scores", H * ST)
    masked, top, negated = (Step(chip, "mla_" + n, H * ST) for n in ("masked", "max", "neg_max"))
    ex, inv, soft = (Step(chip, "mla_" + n, H * ST) for n in ("exp", "inverse", "softmax"))
    t_mm, t_copy = Step(chip, "mla_t_mm", H * ST), Step(chip, "mla_t_copy", H * ST)
    o_mm, o_copy = Step(chip, "mla_o_mm", H), Step(chip, "mla_o_copy", H)
    silu, z_ready = Step(chip, "mla_silu", H), Step(chip, "mla_z", H)
    z_rounded, z_rest = Step(chip, "mla_z_rounded", H), Step(chip, "mla_z_rest", H)
    post = PostNorm(chip, y, y_sq, 1, b_o, u_o, rstd=norm.rstd)

    def latent_parts(n):
        return c_high[:, n, :], c_low[:, n, :]

    def tensor(pe):
        norm.tensor(pe)

        def h_parts(n):
            return h_high[:, n, :], h_low[:, n, :]

        chip.pe_features(pe, b_c, u_c, 4, KD, h_parts, before=lambda n: norm.wait(pe, n), split=split)
        chip.pe_features(pe, b_r, u_r, 1, KD, h_parts, split=split)
        chip.pe_features(pe, b_g, u_g, 4, KD, h_parts, split=split)
        q_norm.tensor(pe)
        kv_norm.tensor(pe)
        chip.pe_features(pe, b_g + 4, u_g + 4, 4, KD, h_parts, split=split)
        q_norm.wait(pe, QT - 1)
        kv_norm.wait(pe, CT - 1)
        for qt in range(4):
            b, u = quarters[qt]
            chip.pe_features(pe, b, u, 3, QT, latent_parts, split=split)
            split.wait(pe, b + 3)
            w_high, w_low = split.parts(b + 3, CT, 8 * P)
            for n in range(8):
                g = u + 3 + n // 2
                if n % 2 == 0:
                    chip.wait_pair(pe, g)
                out = chip.pair(g)[n % 2]
                for k in range(CT):
                    if n < 4:
                        mm = three(pe, out[:, :], (w_high, w_low), k, slice(n * P, (n + 1) * P),
                                   latent_parts(QT + k), k == 0, k == CT - 1)
                    else:
                        w_v = [a[:, k, 4 * P:8 * P] for a in (w_high, w_low)]
                        mm = three(pe, out[:, :], (c_high, c_low), QT + k, slice((n - 4) * P, (n - 3) * P),
                                   w_v, k == 0, k == CT - 1)
                if n < 7:
                    mm.then_inc(up_mm.sem, 1)
            mm.then_inc(chip.gemm_done, 2)
            pe.wait_ge(raised.sem, raised.of(12 * qt + 11))
            pe.wait_ge(q_rope.sem, q_rope.of(8 * qt + 7))
            pe.wait_ge(k_rope.sem, k_rope.of(3))

            def scores(hd):
                a = hd % 4
                for j in range(ST):
                    n = hd * ST + j
                    if hd:
                        pe.wait_ge(ex.sem, ex.of(n - ST))
                    out = chip.bank[4 + j][:, 0:(j + 1) * P]
                    pe.matmul(out, qn[:, a, j * P:(j + 1) * P], kn[:, a, 0:(j + 1) * P], start=True, stop=False)
                    pe.matmul(out, qr[:, a // 2, j * P:(j + 1) * P], kz[:, a % 2, 0:(j + 1) * P],
                              start=False, stop=True).then_inc(s_mm.sem, 1)

            def values(hd):
                for i in range(ST):
                    n = hd * ST + i
                    if n >= 2:
                        pe.wait_ge(t_copy.sem, t_copy.of(n - 2))
                    for j in range(i, ST):
                        if i == 0:
                            pe.wait_ge(soft.sem, soft.of(hd * ST + j))
                        mm = pe.matmul(chip.bank[i % 2][:, j * P:(j + 1) * P], pr[:, j, i * P:(i + 1) * P],
                                       chip.ident[:, :], start=True, stop=True)
                    mm.then_inc(t_mm.sem, 1)
                if hd >= 2:
                    pe.wait_ge(o_copy.sem, o_copy.of(hd - 2))
                for i in range(ST):
                    pe.wait_ge(t_copy.sem, t_copy.of(hd * ST + i))
                    mm = pe.matmul(chip.bank[2 + hd % 2][:, i * P:T], v[:, i, (hd % 4) * P:(hd % 4 + 1) * P],
                                   pt[:, i, i * P:T], start=(i == 0), stop=(i == ST - 1))
                mm.then_inc(o_mm.sem, 1)

            scores(4 * qt)
            for a in range(4):
                if a < 3:
                    scores(4 * qt + a + 1)
                values(4 * qt + a)
            pe.wait_ge(o_copy.sem, o_copy.of(4 * qt + 3))
        for r in range(4):
            for tile in range(2):
                split.wait(pe, b_o + 2 * r + tile)
                if tile == 0:
                    chip.wait_pair(pe, u_o + r)
                parts = split.parts(b_o + 2 * r + tile, H, P)
                for n in range(H):
                    if r == 0 and tile == 0:
                        pe.wait_ge(z_rest.sem, z_rest.of(n))
                    mm = three(pe, chip.pair(u_o + r)[tile][:, :], parts, n, slice(0, P),
                               (z_high[:, n, :], z_low[:, n, :]), n == 0, n == H - 1)
                mm.then_inc(chip.gemm_done, 2)
        post.norm.tensor(pe)

    def scalar(act):
        rope.load(act)
        split.high(act, b_c)
        split.high(act, b_c + 1)
        norm.scalar(act)
        for n in range(QT + CT):
            if n == 4:
                rope.scalar(act)
            chip.wait_tile(act, b_c + n // 2, n % 2)
            u = u_c + n // 2
            act.activation(c[:, n, :], chip.pair(u)[n % 2][:, :], ACT.Copy).then_inc(lat.sem, 1)
            act.wait_ge(lat.sem, lat.of(n))
            act.sem_inc(chip.pair_free[u % 2], 1)
            if n % 2:
                split.high(act, b_c + n // 2 + 2)
        q_norm.square(act)
        kv_norm.square(act)
        split.high(act, b_g + 1)
        for n in range(H):
            if n == 8:
                q_norm.root_and_round(act)
                kv_norm.root_and_round(act)
            chip.wait_tile(act, b_g + n // 2, n % 2)
            u = u_g + n // 2
            act.activation(z[:, n, :], chip.pair(u)[n % 2][:, :], ACT.Silu).then_inc(silu.sem, 1)
            act.wait_ge(silu.sem, silu.of(n))
            act.sem_inc(chip.pair_free[u % 2], 1)
            if n % 2:
                split.high(act, b_g + n // 2 + 2, cols=SLOT if n < H - 4 else QT * 2 * P)
        for qt in range(4):
            b, u = quarters[qt]
            if qt:
                act.wait_ge(o_mm.sem, o_mm.of(4 * qt - 1))
            for n in range(4):
                g = u + n // 2
                chip.wait_tile(act, b + n // 2, n % 2)
                act.activation(qn[:, n, :], chip.pair(g)[n % 2][:, :], ACT.Copy).then_inc(raised.sem, 1)
                act.wait_ge(raised.sem, raised.of(12 * qt + n))
                act.sem_inc(chip.pair_free[g % 2], 1)
                if n % 2:
                    split.high(act, b + n // 2 + 2, cols=QT * 2 * P if n == 1 else SLOT)
            for n in range(8):
                g = u + 3 + n // 2
                if n < 7:
                    act.wait_ge(up_mm.sem, up_mm.of(7 * qt + n))
                else:
                    act.wait_ge(chip.gemm_done, 2 * (b + 3) + 2)
                dst = kn[:, n, :] if n < 4 else v[:, n - 4, :]
                act.activation(dst, chip.pair(g)[n % 2][:, :], ACT.Copy).then_inc(raised.sem, 1)
                act.wait_ge(raised.sem, raised.of(12 * qt + 4 + n))
                act.sem_inc(chip.pair_free[g % 2], 1)
            for n in range(2):
                split.high(act, b + 4 + n, cols=QT * 2 * P if qt < 3 else SLOT)
            for a in range(5):
                if a < 4:
                    hd = 4 * qt + a
                    for j in range(ST):
                        n = hd * ST + j
                        act.wait_ge(negated.sem, negated.of(n))
                        if hd:
                            act.wait_ge(t_mm.sem, t_mm.of(hd * ST - 1))
                        w = (j + 1) * P
                        act.activation(pr[:, j, 0:w], chip.bank[4 + j][:, 0:w], ACT.Exp,
                                       bias=small[:, 0, 4 * (hd % 4) + j:4 * (hd % 4) + j + 1], scale=SCALE,
                                       accum_out=small[:, 1, 4 * (hd % 4) + j:4 * (hd % 4) + j + 1])\
                           .then_inc(ex.sem, 1)
                    for i in range(ST):
                        n = hd * ST + i
                        act.wait_ge(t_mm.sem, t_mm.of(n))
                        if hd:
                            act.wait_ge(o_mm.sem, o_mm.of(hd - 1))
                        act.activation(pt[:, i, i * P:T], chip.bank[i % 2][:, i * P:T], ACT.Copy)\
                           .then_inc(t_copy.sem, 1)
                if a:
                    hd = 4 * qt + a - 1
                    act.wait_ge(o_mm.sem, o_mm.of(hd))
                    act.activation(o[:, hd % 4, :], chip.bank[2 + hd % 2][:, :], ACT.Copy).then_inc(o_copy.sem, 1)
        for n in range(H):
            act.wait_ge(z_ready.sem, z_ready.of(n))
            act.activation(z_high[:, n, :], z[:, n, :], ACT.Copy).then_inc(z_rounded.sem, 1)
        post.scalar(act, split=split)

    def vector(dve):
        norm.vector(dve)
        rope.vector(dve)
        rope.wait(dve)
        dve.memset(kz[:, :, :], 0.0).then_inc(zeroed.sem, 1)

        def turn_pair(n, x1, x2):
            for m, (a, b) in enumerate(((x1, rope.cos), (x2, rope.sin), (x2, rope.cos), (x1, rope.sin))):
                dve.tensor_tensor(turn[:, m, :], a[:, :], b[:, :], ALU.mult).then_inc(turned.sem, 1)
            dve.wait_ge(turned.sem, turned.of(4 * n + 3))

        chip.wait_tile(dve, b_r, 1)
        turn_pair(0, *chip.pair(u_r))
        dve.sem_inc(chip.pair_free[u_r % 2], 2)
        dve.wait_ge(zeroed.sem, zeroed.of(0))
        for g in range(4):
            rows = slice(32 * g, 32 * g + 32)
            a = 2 * (g % 2)
            dve.tensor_tensor(kz[rows, g // 2, :], turn[rows, a, :], turn[rows, a + 1, :],
                              ALU.add if g % 2 else ALU.subtract).then_inc(k_rope.sem, 1)
        q_norm.vector(dve)
        kv_norm.vector(dve)
        for qt in range(4):
            b, u = quarters[qt]
            chip.wait_tile(dve, b + 2, 1)
            dve.wait_ge(k_rope.sem, k_rope.of(3)) if qt == 0 else dve.wait_ge(q_rope.sem, q_rope.of(8 * qt - 1))
            if qt:
                dve.wait_ge(z_ready.sem, z_ready.of(4 * qt - 1))
            turn_pair(qt + 1, *chip.pair(u + 2))
            dve.sem_inc(chip.pair_free[(u + 2) % 2], 2)
            for g in range(4):
                rows = slice(32 * g, 32 * g + 32)
                for half in range(2):
                    at_ = 64 * (g % 2) + 32 * half
                    dve.tensor_tensor(qr[at_:at_ + 32, g // 2, :], turn[rows, 2 * half, :],
                                      turn[rows, 2 * half + 1, :], ALU.add if half else ALU.subtract)\
                       .then_inc(q_rope.sem, 1)
            def maxima(hd):
                for j in range(ST):
                    n = hd * ST + j
                    col = 4 * (hd % 4) + j
                    w = (j + 1) * P
                    s = chip.bank[4 + j]
                    dve.wait_ge(s_mm.sem, s_mm.of(n))
                    dve.tensor_tensor(s[:, j * P:w], s[:, j * P:w], chip.k("later"), ALU.add)\
                       .then_inc(masked.sem, 1)
                    dve.wait_ge(masked.sem, masked.of(n))
                    dve.reduce_max(small[:, 0, col:col + 1], s[:, 0:w], AX_X).then_inc(top.sem, 1)
                    dve.wait_ge(top.sem, top.of(n))
                    dve.tensor_scalar(small[:, 0, col:col + 1], small[:, 0, col:col + 1], -SCALE, None, ALU.mult)\
                       .then_inc(negated.sem, 1)

            def normalise(hd):
                for j in range(ST):
                    n = hd * ST + j
                    col = 4 * (hd % 4) + j
                    w = (j + 1) * P
                    s1 = small[:, 1, col:col + 1]
                    dve.wait_ge(ex.sem, ex.of(n))
                    dve.reciprocal(s1, s1).then_inc(inv.sem, 1)
                    dve.wait_ge(inv.sem, inv.of(n))
                    dve.tensor_scalar(pr[:, j, 0:w], pr[:, j, 0:w], s1, None, ALU.mult).then_inc(soft.sem, 1)

            for a in range(4):
                maxima(4 * qt + a)
                normalise(4 * qt + a)
        for n in range(H):
            dve.wait_ge(z_rounded.sem, z_rounded.of(n))
            dve.tensor_tensor(z_low[:, n, :], z[:, n, :], z_high[:, n, :].bitcast(F32), ALU.subtract)\
               .then_inc(z_rest.sem, 1)
        post.vector(dve)

    def gpsimd(pool):
        for b in range(b_c, quarters[0][0]):
            split.low(pool, b)
        for n in range(2):
            split.low(pool, quarters[0][0] + n, cols=QT * 2 * P)
        for qt in range(4):
            b = quarters[qt][0]
            split.low(pool, b + 2, cols=QT * 2 * P)
            split.low(pool, b + 3)
            for n in range(2):
                split.low(pool, b + 4 + n, cols=QT * 2 * P if qt < 3 else SLOT)
            for hd in range(4 * qt, 4 * qt + 4):
                pool.wait_ge(o_copy.sem, o_copy.of(hd))
                pool.tensor_tensor(z[:, hd, :], z[:, hd, :], o[:, hd % 4, :], ALU.mult).then_inc(z_ready.sem, 1)
        for b in range(b_o + 2, b_o + 8):
            split.low(pool, b)

    return tensor, scalar, vector, gpsimd


def block_trunk(nc, io, phases):
    with ExitStack() as ctx:
        chip = Chip(nc, ctx, io)
        const_ready, vec_ready = chip.sem("const_ready"), chip.sem("vec_ready")
        phase_done, out_done = chip.sem("phase_done"), chip.sem("out_done")
        programs = []
        for phase in phases:
            chip.begin_phase()
            programs.append(phase(chip))
        n_blocks = chip.blocks
        assert n_blocks == io["stream"].shape[0], (n_blocks, io["stream"].shape)

        def between(eng, n):
            if n:
                eng.wait_ge(phase_done, 4 * n)
            else:
                eng.wait_ge(const_ready, CONSTS)
                eng.wait_ge(vec_ready, 16 * 3)

        block = ctx.enter_context(nc.Block())

        @block.sync
        def _(sp):
            sp.dma_start(chip.vec[:, :], io["vec"]).then_inc(vec_ready, 16)
            sp.dma_start(chip.const[:, :], io["const"]).then_inc(vec_ready, 16)
            sp.dma_start(chip.x[:, :, :], io["x"].rearrange("(k p) t -> p k t", p=P)).then_inc(vec_ready, 16)

            def load(i, s):
                if isinstance(i, int):
                    if i:
                        sp.wait_ge(chip.gemm_done, 8 * i + 2 * s - 6)
                    src = io["stream"][4 * i + s:4 * i + s + 1, :, :]
                else:
                    sp.wait_ge(chip.gemm_done, 8 * i + 2 * s - 6)
                    src = io["stream"][bass.ds(4 * i + s, 1), :, :]
                sp.dma_start(chip.ring[:, s, :], src.rearrange("a p n -> p (a n)")).then_inc(chip.w_full[s], 16)

            for s in range(min(SLOTS, n_blocks)):
                load(0, s)
            if n_blocks // 4 > 2:
                with sp.Fori(1, n_blocks // 4) as i:
                    for s in range(4):
                        load(i, s)
            elif n_blocks // 4 == 2:
                for s in range(4):
                    load(1, s)
            for s in range(n_blocks % 4 if n_blocks > 4 else 0):
                load(n_blocks // 4, s)
            sp.wait_ge(phase_done, 4 * len(programs))
            sp.dma_start(io["y"].rearrange("(k p) t -> p k t", p=P), chip.x[:, :, :]).then_inc(out_done, 16)
            sp.wait_ge(out_done, 16)

        @block.tensor
        def _(pe):
            for n, (tensor, _, _, _) in enumerate(programs):
                between(pe, n)
                tensor(pe)
                pe.drain().then_inc(phase_done, 1)

        @block.scalar
        def _(act):
            for n, (_, scalar, _, _) in enumerate(programs):
                between(act, n)
                scalar(act)
                act.drain().then_inc(phase_done, 1)

        @block.vector
        def _(dve):
            for pair in chip.pair_free:
                dve.sem_inc(pair, 2)
            dve.memset(chip.ones[:, :], 1.0).then_inc(const_ready, 1)
            dve.memset(chip.eps[:, :], EPS).then_inc(const_ready, 1)
            dve.memset(chip.gn_eps[:, :], GN_EPS).then_inc(const_ready, 1)
            for n, (_, _, vector, _) in enumerate(programs):
                between(dve, n)
                vector(dve)
                dve.drain().then_inc(phase_done, 1)

        @block.gpsimd
        def _(pool):
            pool.memset(chip.ident[:, :], 0.0).then_inc(const_ready, 1)
            pool.wait_ge(const_ready, CONSTS - 1)
            pool.affine_select(out=chip.ident[:, :], in_=chip.ident[:, :], compare_op=ALU.not_equal, fill=1.0,
                               base=0, pattern=[[-1, P]], channel_multiplier=1).then_inc(const_ready, 1)
            for n, (_, _, _, gpsimd) in enumerate(programs):
                between(pool, n)
                if gpsimd:
                    gpsimd(pool)
                pool.drain().then_inc(phase_done, 1)


CONSTS = 5


def tiles(a):
    return np.ascontiguousarray(np.asarray(a).reshape(-1, P).T)


def weight_blocks(w, kt, cols):
    n = w.shape[1] // cols
    b = w.reshape(kt, P, n, cols).transpose(2, 1, 0, 3).reshape(n, P, kt * cols)
    return slotted(b)


def slotted(b):
    return np.pad(b, ((0, 0), (0, 0), (0, SLOT - b.shape[2])))


def stream_rwkv(i):
    w = i["rw_w_in"][0]
    o = {"r": 0, "w": D, "k": D + 64, "v": 2 * D + 64, "a": 3 * D + 64, "g": 3 * D + 128}
    out = [weight_blocks(w[:, o[s]:o[s] + D], KD, 2 * P) for s in "rkv"]
    z = np.zeros((D, 2 * P), w.dtype)
    wa, g = z.copy(), z.copy()
    wa[:, :64], wa[:, 64:128] = w[:, o["w"]:o["w"] + 64], w[:, o["a"]:o["a"] + 64]
    g[:, :LORA_G] = w[:, o["g"]:]
    out += [weight_blocks(wa, KD, 2 * P), weight_blocks(g, KD, 2 * P)]
    low = np.zeros((1, P, SLOT), w.dtype)
    low[0, :64, :D], low[0, :64, D:] = i["rw_w2"][0], i["rw_a2"][0]
    return out + [low]


def stream_rwkv_output(i):
    g2 = np.zeros((1, P, SLOT), i["rw_g2"].dtype)
    g2[0, :, :D], g2[0, :LORA_G - P, D:] = i["rw_g2"][0][:P], i["rw_g2"][0][P:]
    return [g2, weight_blocks(i["rw_w_out"][0], KD, 2 * P)]


def stream_ffn(i, layer):
    gu = i["ffn_w_gu"][layer].reshape(D, 2, KF, P).transpose(0, 2, 1, 3).reshape(D, 2 * FF)
    down = i["ffn_w_down"][layer].reshape(2, KF // 2, P, KD, P).transpose(3, 0, 2, 1, 4)
    return [weight_blocks(gu, KD, 2 * P), slotted(down.reshape(2 * KD, P, KF // 2 * P))]


def stream_mlstm(i):
    w = i["ml_w_in"][0]
    gates = np.zeros((D, 2 * P), w.dtype)
    gates[:, :2 * ML_HEADS] = w[:, 3 * D:]
    return [weight_blocks(w[:, :D], KD, 2 * P), weight_blocks(gates, KD, 2 * P),
            weight_blocks(w[:, D:3 * D], KD, 2 * P), weight_blocks(i["ml_w_out"][0], KD, 2 * P)]


def stream_retention(i):
    w = i["ret_w_in_2"][0]
    out = i["ret_w_out_2"][0]
    b = weight_blocks(w, KD, 2 * P)
    q, k, v, g = b[0:4], b[4:8], b[8:16], b[16:24]
    return [g, q[0:2], k[0:2], v[0:4], q[2:4], k[2:4], v[4:8], weight_blocks(out, 2 * KD, P)]


def stream_ple(i, layer):
    proj = i["ple_w_proj_2"][layer].reshape(2, P, D).transpose(1, 0, 2).reshape(1, P, SLOT)
    return [proj, weight_blocks(i["ple_w_gate_2"][layer], KD, 2 * P)]


def stream_mla(i):
    w = i["mla_w_in_2"][0]
    c = Q_LORA + KV_LORA
    r1, r2 = w[:, c:c + 32], w[:, c + 32:c + 64]
    rope_w = np.concatenate([r1] * 4 + [r2] * 4, 1)
    out = [weight_blocks(w[:, :c], KD, 2 * P), weight_blocks(rope_w, KD, 2 * P),
           weight_blocks(w[:, c + ROPE:], KD, 2 * P)]
    uq = i["mla_w_uq_2"][0].reshape(Q_LORA, MLA_HEADS, NOPE + ROPE)
    uk, uv = i["mla_w_uk_2"][0], i["mla_w_uv_2"][0]
    for n in range(0, MLA_HEADS, 4):
        out.append(weight_blocks(uq[:, n:n + 4, :NOPE].reshape(Q_LORA, 4 * P), 6, 2 * P))
        halves = [uq[:, n:n + 4, NOPE + 32 * a:NOPE + 32 * a + 32].reshape(Q_LORA, P) for a in range(2)]
        out.append(weight_blocks(np.concatenate(halves, 1), 6, 2 * P))
        kv = [u[:, n:n + 4].reshape(KV_LORA, 4 * P) for u in (uk, uv)]
        out.append(weight_blocks(np.concatenate(kv, 1), 2, 8 * P))
    return out + [weight_blocks(i["mla_w_out_2"][0], 2 * KD, P)]


def retention_decay():
    log_g = np.log(np.float32(1) - np.float32(2) ** (np.float32(-5) - np.arange(RET_HEADS, dtype=np.float32)))
    rel = np.arange(T, dtype=np.float32)[None, None, :] - np.arange(P, dtype=np.float32)[:, None, None]
    g = np.where(rel >= 0, np.exp(np.maximum(rel, np.float32(0)) * log_g[None, :, None]), np.float32(0))
    return g.astype(np.float32).reshape(P, RET_HEADS * T)


def vectors(i):
    conv = tiles(i["ml_conv_w"][0])
    gate = np.zeros((P, 2), np.float32)
    gate[:ML_HEADS, 0], gate[:ML_HEADS, 1] = i["ml_b_i"][0], i["ml_b_f"][0]
    parts = {
        "c": tiles(i["c"]), "ada_b": tiles(i["ada_b"]), "mix": tiles(i["rw_mix"]), "w0": tiles(i["rw_w0"]),
        "a0": tiles(i["rw_a0"]), "k_k": tiles(i["rw_k_k"]), "k_a": tiles(i["rw_k_a"]), "r_k": tiles(i["rw_r_k"]),
        "gn_w": tiles(i["rw_gn_w"]), "gn_b": tiles(i["rw_gn_b"]), "conv_w": conv, "conv_b": tiles(i["ml_conv_b"]),
        "hn_w": tiles(i["ml_hn_w"]), "gate_b": gate, "final_w": tiles(i["final_w"]),
        "pre_g": tiles(i["pre_norm_g_2"]), "post_g": tiles(i["post_norm_g_2"]), "ret_gn": tiles(i["ret_gn_g_2"]),
        "q_g": tiles(i["mla_q_norm_g_2"]), "kv_g": tiles(i["mla_kv_norm_g_2"])}
    out = np.zeros((P, VEC_COLS), np.float32)
    for name, (a, b) in VEC.items():
        out[:, a:b] = parts[name]
    return out


def constants():
    out = np.zeros((P, CONST_COLS), np.float32)
    p, q = np.arange(P)[:, None], np.arange(P)[None, :]
    s, t, same = p % 64, q % 64, p // 64 == q // 64
    made = {
        "block_ones": same,
        "head_rows": np.concatenate([np.arange(16)[None, :] == 2 * n + p // 64 for n in range(KD)], 1),
        "chunk_keep": np.broadcast_to(np.arange(T) % CHUNK != 0, (P, T)),
        "fold": p % 64 == np.arange(64)[None, :],
        "before": same & (s < t), "upto": same & (s <= t),
        "levels": np.concatenate([same & (s // (2 * m) == t // (2 * m)) & (s // m % 2 == 0) & (t // m % 2 == 1)
                                  for m in (1, 2, 4, 8, 16, 32)], 1),
        "later": np.where(q > p, np.float32(-1e30), np.float32(0)), "inv_freq": INV_FREQ}
    for name, (a, b) in CONST.items():
        out[:, a:b] = made[name]
    return out


def head_columns():
    return (np.arange(D)[None, :] // HEAD == np.arange(16)[:, None]).astype(np.float32)


_E = np.float32(10000.0)
INV_FREQ = np.stack([_E ** (-np.arange(128, dtype=np.float32) / np.float32(128)),
                     np.tile(_E ** (-np.arange(32, dtype=np.float32) / np.float32(32)), 4)], 1).astype(np.float32)


def ada_blocks(i, first, last):
    return [np.concatenate([weight_blocks(i["ada_w"][n], KD, 2 * P) for n in range(2)])[first:last]]


def stages():
    return [
        (ada, lambda i: ada_blocks(i, 0, ADA_FIRST)),
        (rwkv_project, stream_rwkv), (rwkv_chunks, lambda i: ada_blocks(i, ADA_FIRST, ADA_BLOCKS)), (rwkv_output, stream_rwkv_output),
        (lambda chip: ffn(chip, 0), lambda i: stream_ffn(i, 0)),
        (mlstm, stream_mlstm),
        (lambda chip: ffn(chip, 1), lambda i: stream_ffn(i, 1)),
        (final_norm, lambda i: []),
        (retention, stream_retention),
        (lambda chip: ple(chip, 0), lambda i: stream_ple(i, 0)),
        (mla, stream_mla),
        (lambda chip: ple(chip, 1), lambda i: stream_ple(i, 1)),
    ]


def kernel(**inputs):
    import concourse.bacc as bacc
    from concourse.bass_utils import run_bass_kernel_spmd

    i = {name: np.asarray(a) for name, a in inputs.items()}
    arrays = {
        "x": np.ascontiguousarray(i["x"][0].T),
        "vec": vectors(i),
        "const": constants(),
        "head_cols": head_columns(),
        "ret_decay": retention_decay(),
        "stream": np.concatenate([b for _, weights in stages() for b in weights(i)]),
        "p": np.ascontiguousarray(i["p_2"][:, 0].transpose(0, 2, 1)),
        "pos": np.ascontiguousarray(i["positions_2"]),
    }
    nc = bacc.Bacc("TRN2", target_bir_lowering=False, num_devices=1)
    io = {name: nc.dram_tensor(f"in_{name}", a.shape, mybir.dt.from_np(a.dtype), kind="ExternalInput").ap()
          for name, a in arrays.items()}
    io["y"] = nc.dram_tensor("out_y", (D, T), F32, kind="ExternalOutput").ap()
    block_trunk(nc, io, [phase for phase, _ in stages()])
    r = run_bass_kernel_spmd(nc, [{f"in_{name}": a for name, a in arrays.items()}], core_ids=[0])
    return np.ascontiguousarray(r.results[0]["out_y"].T)[None]
```
